# Optimizing a Trainium2 kernel written in Bass

```python
import math
import jax, jax.numpy as jnp
from jax import lax
import numpy as np

D_MODEL = 1024
BATCH = 1
SEQ = 512
DEPTH = 1

CHUNK = 64
EPS = 1e-6
NEG_INF = -1e30
SSM_WIDTH = D_MODEL // 2
SSM_GROUP = 16
SSM_GROUPS = SSM_WIDTH // SSM_GROUP
SSM_STATE = 64
HEAD_DIM = 64
N_Q_HEADS = (D_MODEL // 2) // HEAD_DIM
N_KV_HEADS = 2
Q_PER_KV = N_Q_HEADS // N_KV_HEADS
ATTN_WIDTH = N_Q_HEADS * HEAD_DIM
KV_WIDTH = N_KV_HEADS * HEAD_DIM
WINDOW = 128
WINDOW_CHUNKS = WINDOW // CHUNK
ATTN_BLOCK = 128
ROPE_THETA = 500000.0
ROPE_DIM = HEAD_DIM // 4
N_BRANCHES = 2
IN_WIDTH = SSM_WIDTH + ATTN_WIDTH + 2 * KV_WIDTH + N_BRANCHES * D_MODEL
N_GROUPS = 4
EXPERTS_PER_GROUP = 8
TOP_K = 2
D_EXPERT = D_MODEL // 4

kernel_name = "hybrid_s5_swa_sink_hmoe_block"

def rms_norm(x, g):
    xf = x.astype(jnp.float32)
    xf = xf * lax.rsqrt(jnp.mean(xf * xf, axis=-1, keepdims=True) + EPS)
    return (xf * g.astype(jnp.float32)).astype(x.dtype)

def partial_rope(t, pos):
    half = ROPE_DIM // 2
    inv_freq = ROPE_THETA ** (-jnp.arange(0, ROPE_DIM, 2, dtype=jnp.float32) / ROPE_DIM)
    ang = pos[:, None] * inv_freq[None, :]
    cos = jnp.cos(ang)[None, :, None, :]
    sin = jnp.sin(ang)[None, :, None, :]
    tr = t[..., :ROPE_DIM].astype(jnp.float32)
    t1, t2 = tr[..., :half], tr[..., half:]
    rot = jnp.concatenate([t1 * cos - t2 * sin, t2 * cos + t1 * sin], axis=-1)
    return jnp.concatenate([rot.astype(t.dtype), t[..., ROPE_DIM:]], axis=-1)

def _complex_scan_combine(e1, e2):
    a1r, a1i, b1r, b1i = e1
    a2r, a2i, b2r, b2i = e2
    return (a2r * a1r - a2i * a1i,
            a2r * a1i + a2i * a1r,
            a2r * b1r - a2i * b1i + b2r,
            a2r * b1i + a2i * b1r + b2i)

def s5_branch(u, lam_re, lam_im, log_step, b_re, b_im, c_re, c_im, d_skip, w_glu, b_glu):
    bsz, s, _ = u.shape
    dt = u.dtype
    f32 = jnp.float32
    uf = u.astype(f32).reshape(bsz, s, SSM_GROUPS, SSM_GROUP)
    step = jnp.exp(log_step.astype(f32))[:, None]
    lr, li = lam_re.astype(f32), lam_im.astype(f32)
    mag = jnp.exp(lr * step)
    ar, ai = mag * jnp.cos(li * step), mag * jnp.sin(li * step)
    den = lr * lr + li * li
    nr, ni = ar - 1.0, ai
    fr = (nr * lr + ni * li) / den
    fi = (ni * lr - nr * li) / den
    bu_r = jnp.einsum('bsgh,gph->bsgp', uf, b_re.astype(f32))
    bu_i = jnp.einsum('bsgh,gph->bsgp', uf, b_im.astype(f32))
    in_r = fr * bu_r - fi * bu_i
    in_i = fr * bu_i + fi * bu_r
    a_r = jnp.broadcast_to(ar, (1, s, SSM_GROUPS, SSM_STATE))
    a_i = jnp.broadcast_to(ai, (1, s, SSM_GROUPS, SSM_STATE))
    _, _, st_r, st_i = lax.associative_scan(_complex_scan_combine, (a_r, a_i, in_r, in_i), axis=1)
    y = (jnp.einsum('bsgp,ghp->bsgh', st_r, c_re.astype(f32))
         - jnp.einsum('bsgp,ghp->bsgh', st_i, c_im.astype(f32))
         + d_skip.astype(f32) * uf)
    y = jax.nn.gelu(y.reshape(bsz, s, SSM_WIDTH)).astype(dt)
    return y * jax.nn.sigmoid(y @ w_glu + b_glu)

def sliding_window_sink_attention(q, k, v, sinks):
    bsz, s, _, _ = q.shape
    nb = s // ATTN_BLOCK
    qb = q.reshape(bsz, nb, ATTN_BLOCK, N_KV_HEADS, Q_PER_KV, HEAD_DIM)
    kb = k.reshape(bsz, nb, ATTN_BLOCK, N_KV_HEADS, HEAD_DIM)
    vb = v.reshape(bsz, nb, ATTN_BLOCK, N_KV_HEADS, HEAD_DIM)
    pad = ((0, 0), (1, 0), (0, 0), (0, 0), (0, 0))
    k_band = jnp.concatenate([jnp.pad(kb, pad)[:, :-1], kb], axis=2)
    v_band = jnp.concatenate([jnp.pad(vb, pad)[:, :-1], vb], axis=2)
    scores = jnp.einsum('bnqhgd,bnkhd->bnhgqk', qb, k_band,
                        preferred_element_type=jnp.float32) * (HEAD_DIM ** -0.5)
    blk = jnp.arange(nb)[:, None]
    q_pos = blk * ATTN_BLOCK + jnp.arange(ATTN_BLOCK)[None, :]
    k_pos = (blk - 1) * ATTN_BLOCK + jnp.arange(2 * ATTN_BLOCK)[None, :]
    cq = (q_pos // CHUNK)[:, :, None]
    ck = (k_pos // CHUNK)[:, None, :]
    allowed = (k_pos[:, None, :] >= 0) & (ck <= cq) & (ck > cq - WINDOW_CHUNKS)
    scores = jnp.where(allowed[None, :, None, None], scores, NEG_INF)
    sink = sinks.astype(jnp.float32).reshape(N_KV_HEADS, Q_PER_KV)[None, None, :, :, None, None]
    m = jnp.maximum(jnp.max(scores, axis=-1, keepdims=True), sink)
    p = jnp.exp(scores - m)
    denom = jnp.sum(p, axis=-1, keepdims=True) + jnp.exp(sink - m)
    probs = (p / denom).astype(v.dtype)
    out = jnp.einsum('bnhgqk,bnkhd->bnqhgd', probs, v_band)
    return out.reshape(bsz, s, N_Q_HEADS * HEAD_DIM)

def hierarchical_moe(x, w_group_router, b_group_router, w_expert_router, b_expert_router,
                     w_gate, w_up, w_down):
    bsz, s, d = x.shape
    dt = x.dtype
    t = x.reshape(-1, d)
    g_logits = (t @ w_group_router).astype(jnp.float32) + b_group_router.astype(jnp.float32)
    g_prob = jax.nn.softmax(g_logits, axis=-1)
    g_sel = jnp.argmax(g_logits, axis=-1)
    g_w = jnp.take_along_axis(g_prob, g_sel[:, None], axis=-1)
    e_logits = (jnp.einsum('td,gde->tge', t, w_expert_router).astype(jnp.float32)
                + b_expert_router.astype(jnp.float32))
    e_sel_logits = jnp.take_along_axis(e_logits, g_sel[:, None, None], axis=1)[:, 0]
    top_v, top_i = lax.top_k(e_sel_logits, TOP_K)
    top_w = jax.nn.softmax(top_v, axis=-1) * g_w
    within = jnp.einsum('tk,tke->te', top_w,
                        jax.nn.one_hot(top_i, EXPERTS_PER_GROUP, dtype=jnp.float32))
    combine = (jax.nn.one_hot(g_sel, N_GROUPS, dtype=jnp.float32)[:, :, None]
               * within[:, None, :]).astype(dt)
    y = jnp.zeros_like(t)
    for grp in range(N_GROUPS):
        hid = (jax.nn.silu(jnp.einsum('td,edf->tef', t, w_gate[grp]))
               * jnp.einsum('td,edf->tef', t, w_up[grp]))
        y = y + jnp.einsum('tef,efd->td', hid * combine[:, grp, :, None], w_down[grp])
    return y.reshape(bsz, s, d)

def setup_inputs(seed: int = 0) -> dict:
    key = jax.random.key(seed)
    ks = jax.random.split(key, 32)
    f32 = jnp.float32
    L = DEPTH

    def nrm(k, shape, scale):
        return jax.random.normal(k, shape, f32) * scale

    n_idx = jnp.arange(SSM_STATE, dtype=f32)
    return {
        "x": nrm(ks[0], (BATCH, SEQ, D_MODEL), 1.0),
        "g_mix": 1.0 + nrm(ks[1], (L, D_MODEL), 0.02),
        "w_in": nrm(ks[2], (L, D_MODEL, IN_WIDTH), D_MODEL ** -0.5),
        "q_norm": 1.0 + nrm(ks[3], (L, HEAD_DIM), 0.02),
        "k_norm": 1.0 + nrm(ks[4], (L, HEAD_DIM), 0.02),
        "ssm_lambda_re": -0.5 + nrm(ks[5], (L, SSM_GROUPS, SSM_STATE), 0.01),
        "ssm_lambda_im": math.pi * n_idx + nrm(ks[6], (L, SSM_GROUPS, SSM_STATE), 0.01),
        "ssm_log_step": jax.random.uniform(ks[7], (L, SSM_GROUPS), f32,
                                           math.log(1e-3), math.log(1e-1)),
        "ssm_b_re": nrm(ks[8], (L, SSM_GROUPS, SSM_STATE, SSM_GROUP), SSM_GROUP ** -0.5),
        "ssm_b_im": nrm(ks[9], (L, SSM_GROUPS, SSM_STATE, SSM_GROUP), SSM_GROUP ** -0.5),
        "ssm_c_re": nrm(ks[10], (L, SSM_GROUPS, SSM_GROUP, SSM_STATE), SSM_STATE ** -0.5),
        "ssm_c_im": nrm(ks[11], (L, SSM_GROUPS, SSM_GROUP, SSM_STATE), SSM_STATE ** -0.5),
        "ssm_d": nrm(ks[12], (L, SSM_GROUPS, SSM_GROUP), 1.0),
        "ssm_w_glu": nrm(ks[13], (L, SSM_WIDTH, SSM_WIDTH), SSM_WIDTH ** -0.5),
        "ssm_b_glu": nrm(ks[14], (L, SSM_WIDTH), 0.02),
        "attn_sinks": nrm(ks[15], (L, N_Q_HEADS), 0.5),
        "w_ssm_proj": nrm(ks[16], (L, SSM_WIDTH, D_MODEL), SSM_WIDTH ** -0.5),
        "w_attn_proj": nrm(ks[17], (L, ATTN_WIDTH, D_MODEL), ATTN_WIDTH ** -0.5),
        "w_out": nrm(ks[18], (L, D_MODEL, D_MODEL), D_MODEL ** -0.5),
        "g_ffn": 1.0 + nrm(ks[19], (L, D_MODEL), 0.02),
        "w_group_router": nrm(ks[20], (L, D_MODEL, N_GROUPS), D_MODEL ** -0.5),
        "b_group_router": nrm(ks[21], (L, N_GROUPS), 0.01),
        "w_expert_router": nrm(ks[22], (L, N_GROUPS, D_MODEL, EXPERTS_PER_GROUP), D_MODEL ** -0.5),
        "b_expert_router": nrm(ks[23], (L, N_GROUPS, EXPERTS_PER_GROUP), 0.01),
        "w_expert_gate": nrm(ks[24], (L, N_GROUPS, EXPERTS_PER_GROUP, D_MODEL, D_EXPERT), D_MODEL ** -0.5),
        "w_expert_up": nrm(ks[25], (L, N_GROUPS, EXPERTS_PER_GROUP, D_MODEL, D_EXPERT), D_MODEL ** -0.5),
        "w_expert_down": nrm(ks[26], (L, N_GROUPS, EXPERTS_PER_GROUP, D_EXPERT, D_MODEL), D_EXPERT ** -0.5),
    }

def reference(x, g_mix, w_in, q_norm, k_norm, ssm_lambda_re, ssm_lambda_im, ssm_log_step,
              ssm_b_re, ssm_b_im, ssm_c_re, ssm_c_im, ssm_d, ssm_w_glu, ssm_b_glu, attn_sinks,
              w_ssm_proj, w_attn_proj, w_out, g_ffn, w_group_router, b_group_router,
              w_expert_router, b_expert_router, w_expert_gate, w_expert_up, w_expert_down):
    bsz, s, _ = x.shape
    pos = jnp.arange(s, dtype=jnp.float32)
    splits = [SSM_WIDTH, SSM_WIDTH + ATTN_WIDTH, SSM_WIDTH + ATTN_WIDTH + KV_WIDTH,
              SSM_WIDTH + ATTN_WIDTH + 2 * KV_WIDTH]
    for layer in range(DEPTH):
        h = rms_norm(x, g_mix[layer])
        proj = h @ w_in[layer]
        u_ssm, q, k, v, gate_logits = jnp.split(proj, splits, axis=-1)
        q = q.reshape(bsz, s, N_Q_HEADS, HEAD_DIM)
        k = k.reshape(bsz, s, N_KV_HEADS, HEAD_DIM)
        v = v.reshape(bsz, s, N_KV_HEADS, HEAD_DIM)
        q = partial_rope(rms_norm(q, q_norm[layer]), pos)
        k = partial_rope(rms_norm(k, k_norm[layer]), pos)
        ssm_y = s5_branch(u_ssm, ssm_lambda_re[layer], ssm_lambda_im[layer], ssm_log_step[layer],
                          ssm_b_re[layer], ssm_b_im[layer], ssm_c_re[layer], ssm_c_im[layer],
                          ssm_d[layer], ssm_w_glu[layer], ssm_b_glu[layer])
        attn_y = sliding_window_sink_attention(q, k, v, attn_sinks[layer])
        ssm_out = ssm_y @ w_ssm_proj[layer]
        attn_out = attn_y @ w_attn_proj[layer]
        gates = jax.nn.sigmoid(gate_logits).reshape(bsz, s, N_BRANCHES, D_MODEL)
        merged = gates[:, :, 0, :] * ssm_out + gates[:, :, 1, :] * attn_out
        x = x + merged @ w_out[layer]
        x = x + hierarchical_moe(rms_norm(x, g_ffn[layer]), w_group_router[layer],
                                 b_group_router[layer], w_expert_router[layer],
                                 b_expert_router[layer], w_expert_gate[layer],
                                 w_expert_up[layer], w_expert_down[layer])
    return x


_drawn_inputs = setup_inputs


def setup_inputs(seed=0):
    import zlib

    import numpy as np

    out = dict(_drawn_inputs(seed))
    spreads = {}
    factors = {'g_mix': 3.382,
     'q_norm': 5.844,
     'k_norm': 8.0,
     'ssm_lambda_re': 64.0,
     'ssm_b_glu': 26.256,
     'attn_sinks': 8.0,
     'b_group_router': 48.386,
     'b_expert_router': 18.044,
     'ssm_log_step': 2.694,
     'ssm_b_re': 3.242,
     'ssm_b_im': 3.307,
     'ssm_c_re': 3.049,
     'ssm_c_im': 3.356,
     'g_ffn': 4.36}
    for name, (base, spread) in spreads.items():
        noise = np.random.default_rng([zlib.crc32(name.encode()), seed]).standard_normal(out[name].shape)
        drawn = base * np.exp(spread * noise) if base else spread * noise
        out[name] = __import__('jax').numpy.asarray(drawn.astype(out[name].dtype))
    for name, factor in factors.items():
        out[name] = (out[name] * factor).astype(out[name].dtype)
    return out
```

```python
from contextlib import ExitStack

import numpy as np

import concourse.bass as bass
from concourse import mybir

F32 = mybir.dt.float32
I32 = mybir.dt.int32
ALU = mybir.AluOpType
ACT = mybir.ActivationFunctionType
AX = mybir.AxisListType

P = 128
D = 1024
KD = D // P
T = 512
TT = T // P
CH = 512
NG, SG, NS = 32, 16, 64
ST = NG * NS // P
NH, HD = 8, 64
NKV = 2
PAIRS = NH // 2
QKV = NH * HD + 2 * NKV * HD
CHUNK = 64
NC = T // CHUNK
W_IN = CH + QKV + 2 * D
COLS = 256
BLOCK = KD * COLS
RING = 4
NGRP, EPG = 4, 8
NE = NGRP * EPG
DE = 256
SLOTS = 4
NR = NGRP + NE
EPS = 1e-6
MAGIC = 12582912.0
TWO_PI = 6.283185
NONE = 4096
LN2_HI, LN2_LO = 0.693359375, -2.12194440e-4

C_ID, C_TRI, C_ONE = 0, 128, 256
C_T = 384
C_ROPE = C_T + T
C_GL = C_ROPE + TT * 32
C_I4 = C_GL + 4
C_I8 = C_I4 + NGRP
C_E = C_I8 + EPG
C_REC = C_E + NE
C_Q = C_REC + TT * 8
C_N = C_Q + 1


def constants():
    c = np.zeros((P, C_N), np.float32)
    c[:, C_ID:C_ID + P] = np.eye(P)
    c[:, C_TRI:C_TRI + P] = np.triu(np.ones((P, P)), 1)
    c[:, C_ONE:C_ONE + P] = 1.0
    c[:, C_T:C_T + T] = np.arange(T)
    inv = np.float32(500000.0) ** (-np.arange(0, 16, 2, dtype=np.float32) / np.float32(16))
    ang = (np.arange(T, dtype=np.float32)[:, None] * inv[None]).astype(np.float64)
    rope = np.concatenate([np.cos(ang), np.cos(ang), -np.sin(ang), np.sin(ang)], 1)
    c[:, C_ROPE:C_GL] = rope.reshape(TT, P, 32).transpose(1, 0, 2).reshape(P, TT * 32)
    odd = (np.arange(P) // SG) % 2
    for n, m in enumerate((1 - odd, odd, odd - 1, -odd)):
        c[:, C_GL + n] = m
    c[:, C_I4:C_I4 + NGRP] = np.arange(NGRP)
    c[:, C_I8:C_I8 + EPG] = np.arange(EPG)
    c[:, C_E:C_E + NE] = np.arange(NE)
    rec = np.zeros((P, TT, 2, 4), np.int32)
    tok = np.arange(TT)[None, :] * P + np.arange(P)[:, None]
    for choice in range(2):
        rec[:, :, choice, 0] = tok
        rec[:, :, choice, 1] = tok + T * choice
    c[:, C_Q] = np.pi / 2
    c[:, C_REC:C_Q] = rec.reshape(P, TT * 8).view(np.float32)
    return c


class Order:

    def __init__(self, eng, sem):
        self.eng, self.sem, self.n = eng, sem, 0

    def mark(self, ins):
        self.n += 1
        ins.then_inc(self.sem, 1)
        return self.n

    def wait(self, n=None):
        self.eng.wait_ge(self.sem, self.n if n is None else n)

    def link(self, ins):
        self.mark(ins)
        self.wait()


class Banks:

    def __init__(self):
        self.used = [0] * 8
        self.of = {}
        self.turn = 0

    def take(self, key, bank=None):
        if bank is None:
            bank = 5 + self.turn % 3
            self.turn += 1
        self.of[key] = (bank, self.used[bank])
        self.used[bank] += 1


def slot_work(t):
    if t < 4:
        return [("qkv", 3 * t + i) for i in range(3)]
    return [("gate", t - 4)]


def plan_banks():
    b = Banks()
    for tt in range(TT):
        for half in range(2):
            b.take(("xT", tt, half), (2 * tt + half) % 4)
    for c in range(TT):
        b.take(("u", c))
    for ri in range(2):
        b.take(("bT", ri), ri)
        b.take(("cT", ri), 2 + ri)
    for t in range(2):
        for ri in range(2):
            b.take(("bu", t, ri), (t % 2) * 2 + ri)
    for t in range(ST):
        for w in slot_work(t):
            b.take(w)
        if t + 2 < ST:
            for ri in range(2):
                b.take(("bu", t + 2, ri), (t % 2) * 2 + ri)
        if t % 4 == 0:
            b.take(("y", t // 4), 4)
    for tt in range(TT):
        b.take(("qT", tt))
        b.take(("kT", tt))
    for c in range(NC):
        b.take(("score", c), c % 2)
        if c % 2 == 0:
            b.take(("gate", 12 + c // 2))
        b.take(("pT", c), 2 + c % 2)
        b.take(("pv", c), 4)
    for j in range(4):
        b.take(("glu", j))
    for j in range(KD):
        b.take(("ssm", j))
        b.take(("att", j))
    for tt in range(TT):
        for half in range(2):
            b.take(("o", tt, half))
    for tt in range(TT):
        for half in range(2):
            b.take(("hT", tt, half), (2 * tt + half) % 4)
        b.take(("logit", tt), 4)
    b.take(("rank",), 5)
    b.take(("count",), 6)
    return b


def weight_blocks():
    blocks = [("in", c) for c in range(W_IN // COLS)]
    blocks += [("glu", 0), ("ssm", 0), ("att", 0), ("ssm", 1), ("att", 1)]
    return blocks + [("out", c) for c in range(D // COLS)]


def last_use(kind, c):
    if kind == "in":
        return ("u", 2 * c + 1) if c < 2 else ("qkv", 4 * c - 5) if c < 5 else ("gate", 2 * c - 9)
    return ("o", TT - 1, 1) if kind == "out" else ("glu", 3) if kind == "glu" else (kind, 4 * c + 3)


def build(nc, x, g_mix, w_in, q_norm, k_norm, lam_re, lam_im, log_step, b_re, b_im, c_re, c_im,
          ssm_d, w_glu, b_glu, sinks, w_ssm, w_att, w_out, g_ffn, w_rg, b_rg, w_re, b_er,
          w_eg, w_eu, w_ed, consts, out):
    banks = plan_banks()
    of = banks.of
    blocks = weight_blocks()
    block_at = {b: n for n, b in enumerate(blocks)}

    with ExitStack() as ctx:
        def sb(name, shape, dt=F32):
            return ctx.enter_context(nc.sbuf_tensor(name, [P, *shape], dt))

        def sem(name):
            return ctx.enter_context(nc.semaphore(name))

        pb = [ctx.enter_context(nc.psum_tensor(f"bank{i}", [P, 512], F32)) for i in range(8)]

        cst = sb("cst", [C_N])
        xr = sb("xr", [TT, D])
        hT = sb("hT", [KD, T])
        xs = sb("xs", [2, D])
        cw = xs[:, 0, :].rearrange("p (q r m) -> p q r m", q=4, r=2)
        ring = sb("ring", [RING, BLOCK])
        gates = sb("gates", [2 * KD, T])
        slot0 = sb("slot0", [3 * BLOCK])
        slot1 = sb("slot1", [3 * BLOCK])
        slot2 = sb("slot2", [3 * BLOCK])
        odd = sb("odd", [4, T])
        qT = sb("qT", [PAIRS, T])
        kT = sb("kT", [NKV, CHUNK + T])
        v_mid = sb("v_mid", [NC // 2 - 1, NKV * HD])
        par = sb("par", [16, ST])
        g1 = sb("g1", [KD])
        g2 = sb("g2", [KD])
        dsk = sb("dsk", [4])
        bgl = sb("bgl", [4])
        qkn = sb("qkn", [2, HD])
        snk = sb("snk", [PAIRS])
        wr = sb("wr", [KD, NR])
        brt = sb("brt", [NR])
        small = sb("small", [64])
        soft = sb("soft", [2, 8, PAIRS])
        nrm = sb("nrm", [4, TT, NH + NKV])
        bgh = sb("bgh", [4])
        rc = sb("rc", [SLOTS, 4], I32)
        to = sb("to", [SLOTS], I32)
        idx = sb("idx", [TT, 2], I32)
        most = sb("most", [1], I32)

        ident = cst[:, C_ID:C_ID + P]
        tri = cst[:, C_TRI:C_TRI + P]
        ones = cst[:, C_ONE:C_ONE + P]
        tpos = cst[:, C_T:C_T + T]

        none = odd[:, 3, :].bitcast(I32)
        s5 = slot0[:, :].rearrange("p (n t) -> p n t", t=T)
        turn, rot = s5[:, 0], s5[:, 1]
        sin_t = [s5[:, 2], s5[:, 3]]
        cos_t = [s5[:, 4], s5[:, 5]]
        prs = [[s5[:, 6 + n] for n in range(4)], [odd[:, n] for n in range(4)]]
        st_re, st_im = s5[:, 10], s5[:, 11]
        raw_b = [slot0[:, 256 * n:256 * n + 256].rearrange("p (t h) -> p t h", h=SG) for n in range(2)]
        raw_c = [slot0[:, 512 + 256 * n:768 + 256 * n].rearrange("p (q s) -> p q s", s=NS) for n in range(2)]
        blk_b = [slot0[:, 1024 + 512 * n:1536 + 512 * n].rearrange("p (t g h) -> p t g h", g=2, h=SG)
                 for n in range(2)]
        blk_c = [slot0[:, 2048 + 512 * n:2560 + 512 * n].rearrange("p (q g s) -> p q g s", g=2, s=NS)
                 for n in range(2)]
        tmp_b = [slot0[:, 3072 + 256 * n:3328 + 256 * n].rearrange("p (t h) -> p t h", h=SG) for n in range(4)]
        qkv = slot1[:, 0:TT * QKV].rearrange("p (t c) -> p t c", c=QKV)
        kdup = slot1[:, 3072:4096].rearrange("p (t v r d) -> p t v r d", v=NKV, r=2, d=HD)
        prob = [slot1[:, 3072 + 512 * n:3584 + 512 * n].rearrange("p (h k) -> p h k", k=P) for n in range(2)]
        prT = [slot1[:, 4096 + 512 * n:4608 + 512 * n].rearrange("p (h k) -> p h k", k=P) for n in range(2)]
        sqk = slot1[:, 4096:4096 + 640]
        ropet = [slot1[:, 4736:4864], slot1[:, 4864:4928]]
        ropes = [slot1[:, 4928:5056], slot1[:, 5056:5120]]
        bw = slot1[:, 5120:6144].rearrange("p (q r s) -> p q r s", r=2, s=P)
        uT = slot2[:, 0:2048].rearrange("p (c t) -> p c t", t=T)
        yT = slot2[:, 2048:4096].rearrange("p (c t) -> p c t", t=T)
        y2 = slot2[:, 4096:6144].rearrange("p (c t) -> p c t", t=T)
        mg = gates
        sgl = xs[:, 0, :].rearrange("p (n t) -> p n t", t=T)
        mtmp = xs[:, 1, :].rearrange("p (n t) -> p n t", t=T)
        junk = qT[:, 0:2, :].rearrange("p a b -> p (a b)")
        quarter = cst[:, C_Q:C_Q + 1]
        rt = kT[:, :, :].rearrange("p a b -> p (a b)")
        lg = rt[:, 0:144].rearrange("p (t n) -> p t n", n=NR)
        goh = rt[:, 144:160].rearrange("p (t n) -> p t n", n=NGRP)
        gtm = rt[:, 160:176].rearrange("p (t n) -> p t n", n=NGRP)
        oh = [rt[:, 176 + 32 * n:208 + 32 * n].rearrange("p (t n) -> p t n", n=EPG) for n in range(2)]
        esel = rt[:, 240:272].rearrange("p (t n) -> p t n", n=EPG)
        etm = rt[:, 272:304].rearrange("p (t n) -> p t n", n=EPG)
        st4 = [rt[:, 304 + 4 * n:308 + 4 * n] for n in range(10)]
        gsel = rt[:, 352:480].rearrange("p (t g e) -> p t g e", g=NGRP, e=EPG)
        ohe = [rt[:, 480 + 128 * n:608 + 128 * n].rearrange("p (t n) -> p t n", n=NE) for n in range(2)]
        both = rt[:, 736:864].rearrange("p (t n) -> p t n", n=NE)
        place = rt[:, 864:992].rearrange("p (t n) -> p t n", n=NE)
        rec = rt[:, 992:1024].rearrange("p (t c f) -> p t c f", c=2, f=4)
        gf = gates[:, :, :].rearrange("p a b -> p (a b)")
        xe = hT[:, :, :].rearrange("p a b -> p (a b)").rearrange("p (n d) -> p n d", d=D)
        xeT = gf[:, 0:2048].rearrange("p (n k c) -> p n k c", n=2, c=P)
        oe = gf[:, 2048:6144].rearrange("p (n d) -> p n d", d=D)
        hid = gf[:, 6144:6656].rearrange("p (n f) -> p n f", f=DE)
        sg = gf[:, 6656:7168].rearrange("p (n f) -> p n f", f=DE)
        hidT = gf[:, 7168:7680].rearrange("p (n j c) -> p n j c", n=2, c=P)
        lst = gf[:, 7680:8192].bitcast(I32).rearrange("p (i f) -> p i f", f=4)
        eslot = [slot0[:, :], slot1[:, :], slot2[:, :],
                 ring[:, 0:3, :].rearrange("p a b -> p (a b)")]

        hrow = nc.dram_tensor("normed_rows", (T, D), F32, kind="Internal").ap()
        lists = nc.dram_tensor("expert_lists", (T * NE, 4), I32, kind="Internal").ap()
        yrow = nc.dram_tensor("expert_rows", (2 * T, D), F32, kind="Internal").ap()

        full = [sem(f"bank{i}_full") for i in range(8)]
        free = [sem(f"bank{i}_free") for i in range(8)]
        x_in = [sem(f"x_in{t}") for t in range(TT)]
        cst_in, par_in, bc_in = sem("cst_in"), sem("par_in"), sem("bc_in")
        gain_in, late_in = sem("gain_in"), sem("late_in")
        ring_in = [sem(f"ring{s}_loaded") for s in range(RING)]
        act_order, dve_order, pool_order = sem("act_order"), sem("dve_order"), sem("pool_order")
        ssq_done, rstd_done, xs_done = sem("ssq_done"), sem("rstd_done"), sem("xs_done")
        par_turn, par_trig = sem("par_turn"), sem("par_trig")
        blk_done = sem("blk_done")
        turns, whole, rot_done, cs_done = sem("turns"), sem("whole_turns"), sem("rot_done"), sem("cs_done")
        prod_done, in_done = sem("rotated_products"), sem("rotated_inputs")
        out_prod, st_done, st_used = sem("state_products"), sem("states_done"), sem("states_used")
        sq_done, sum_done, qk_rstd = sem("qk_squares"), sem("qk_sums"), sem("qk_rstd")
        qk_scaled, qk_done = sem("qk_scaled"), sem("qk_normed")
        v_moved = sem("v_moved")
        y_act = sem("y_activated")
        m_done, p_exp, p_done = sem("max_done"), sem("probs_exp"), sem("probs_done")
        y2_done, mg_done = sem("glu_done"), sem("merged_done")
        ssq2_done, rstd2_done, xs2_done = sem("ssq2"), sem("rstd2"), sem("xs2_done")
        row_out = [sem(f"row{n}_stored") for n in range(2)]
        kt_zero, none_set, lists_set = sem("kt_zero"), sem("none_set"), sem("lists_set")
        dexp_in, dexp_out = sem("router_exp_in"), sem("router_exp_out")
        both_done, rec_done, most_done = sem("both_done"), sem("rec_done"), sem("most_done")
        listed, lst_in = sem("listed"), sem("lst_in")
        gu_in = [sem(f"gate_up{s}_loaded") for s in range(SLOTS)]
        dn_in = [sem(f"down{s}_loaded") for s in range(SLOTS)]
        rc_ready, to_ready, dma_begun = sem("record_ready"), sem("result_row_ready"), sem("indirect_dma_begun")
        xe_in = [sem(f"xe{n}_gathered") for n in range(SLOTS)]
        xt_full, xt_out = sem("xt_full"), sem("xt_out")
        gu_done, silu_done, hid_done = sem("gate_up_done"), sem("silu_done"), sem("hid_done")
        ht_full, ht_out, dn_done = sem("hidT_full"), sem("hidT_out"), sem("down_done")
        oe_act, oe_dve = sem("oe_act"), sem("oe_dve")
        sc_done = [sem(f"rows{n}_scattered") for n in range(SLOTS)]
        moe_done, y_in, out_ready, stored = sem("moe_done"), [sem(f"y_in{t}") for t in range(TT)], \
            sem("out_ready"), sem("stored")

        bc = [(raw_b[n], src.rearrange("(t g) s h -> (g s) t h", g=2)) for n, src in enumerate((b_re, b_im))]
        bc += [(raw_c[n], src.rearrange("(q g) h s -> (g h) q s", q=4)) for n, src in enumerate((c_re, c_im))]
        late = [(dsk[:, :], ssm_d.rearrange("(q g) h -> (g h) q", q=4)),
                (bgl[:, :], b_glu.rearrange("(q p) -> p q", p=P)),
                (g2[:, :], g_ffn.rearrange("(p k) -> p k", k=KD)),
                (qkn[:, 0, :], q_norm.unsqueeze(0).broadcast_to([P, HD])),
                (qkn[:, 1, :], k_norm.unsqueeze(0).broadcast_to([P, HD])),
                (snk[0:HD, :], sinks.rearrange("(a b) -> b a", b=2)[0:1, :].broadcast_to([HD, PAIRS])),
                (snk[HD:P, :], sinks.rearrange("(a b) -> b a", b=2)[1:2, :].broadcast_to([HD, PAIRS])),
                (wr[:, :, 0:NGRP], w_rg.rearrange("(p k) g -> p k g", k=KD)),
                (brt[:, 0:NGRP], b_rg.unsqueeze(0).broadcast_to([P, NGRP])),
                (brt[:, NGRP:NR], b_er.rearrange("(a g) e -> a (g e)", a=1).broadcast_to([P, NE]))]
        late += [(wr[:, :, NGRP + EPG * g:NGRP + EPG * (g + 1)],
                  w_re[g].rearrange("(p k) e -> p k e", k=KD)) for g in range(NGRP)]
        tb, gu, hb, ob = pb[0:2], pb[2:4], pb[4], pb[6:8]

        block = ctx.enter_context(nc.Block())

        def read_out(eng, key):
            b, n = of[key]
            eng.wait_ge(free[b], n + 1)

        def filled(eng, key):
            b, n = of[key]
            eng.wait_ge(full[b], n + 1)
            return pb[b]

        def states_read(eng, t):
            if t % 4 == 3:
                filled(eng, ("y", t // 4))
            else:
                eng.wait_ge(st_used, t + 1 - (t + 1) // 4)

        def wait(eng, s, value):
            if not isinstance(value, int) or value > 0:
                eng.wait_ge(s, value)

        def expert_steps(eng, step):
            for j in range(1, 5):
                step(j // 4, j % 4)
            with eng.Fori(0, 6) as r:
                for j in range(5, 9):
                    step(r + j // 4, j % 4)
            for j in range(29, 32):
                step(j // 4, j % 4)

        def overflow(eng, step):
            eng.wait_ge(most_done, 1)
            count = eng.value_load(most[0:1, 0:1], min_val=0, max_val=T)
            with eng.If(count > P):
                with eng.Fori(1, T // P) as q:
                    with eng.Fori(0, NE // 4) as r:
                        for u in range(4):
                            step(q * 8 + r, u, r * 4 + u)

        @block.sync
        def _(sp):
            for tt in range(TT):
                sp.dma_start(xr[:, tt, :], x[0, tt * P:(tt + 1) * P, :]).then_inc(x_in[tt], 16)
            w_rows = w_in.rearrange("(p k) n -> p k n", k=KD)
            o_rows = w_out.rearrange("(k p) n -> p k n", p=P)
            eg = w_eg.rearrange("g e (p k) f -> (g e) p (k f)", k=KD)
            eu = w_eu.rearrange("g e (p k) f -> (g e) p (k f)", k=KD)
            ed = w_ed.rearrange("g e (p j) d -> (g e) p (j d)", j=2)

            def weights(n, u, e):
                i = n * 4 + u
                wait(sp, gu_done, i - 3)
                sp.dma_start(eslot[u][:, 0:BLOCK], eg[e]).then_inc(gu_in[u], 16)
                sp.dma_start(eslot[u][:, BLOCK:2 * BLOCK], eu[e]).then_inc(gu_in[u], 16)
                wait(sp, dn_done, i - 3)
                sp.dma_start(eslot[u][:, 2 * BLOCK:], ed[e]).then_inc(dn_in[u], 16)

            for n, (kind, c) in enumerate(blocks):
                if n in (2, RING):
                    with nc.allow_non_contiguous_dma("small parameters"):
                        for dst, src in bc if n == 2 else late:
                            sp.dma_start(dst, src).then_inc(bc_in if n == 2 else late_in, 16)
                s = n % RING
                if n >= RING:
                    filled(sp, last_use(*blocks[n - RING]))
                if kind == "in":
                    src = w_rows[:, :, c * COLS:(c + 1) * COLS]
                elif kind == "out":
                    src = o_rows[:, :, c * COLS:(c + 1) * COLS]
                else:
                    w = {"glu": w_glu, "ssm": w_ssm, "att": w_att}[kind]
                    src = w.rearrange("(k p) n -> p k n", p=P)[:, :, c * 512:(c + 1) * 512]
                dst = ring[:, s, :].rearrange("p (k n) -> p k n", k=src.shape[1])
                sp.dma_start(dst, src).then_inc(ring_in[s], 16)
            sp.wait_ge(mg_done, KD)
            weights(0, 0, 0)
            weights(0, 1, 1)
            weights(0, 2, 2)
            filled(sp, ("o", TT - 1, 1))
            weights(0, 3, 3)
            with sp.Fori(1, NE // 4) as r:
                for u in range(4):
                    weights(r, u, r * 4 + u)
            overflow(sp, weights)
            sp.wait_ge(moe_done, 1)
            ys = [slot0[:, 2048 * t:2048 * (t + 1)] for t in range(3)] + [slot1[:, 0:2048]]
            for tt in range(TT):
                sp.dma_start(ys[tt].rearrange("p (c d) -> p c d", c=2),
                             yrow.rearrange("(c t p) d -> t p c d", c=2, p=P)[tt]).then_inc(y_in[tt], 16)
            for tt in range(TT):
                sp.wait_ge(out_ready, tt + 1)
                sp.dma_start(out[0, tt * P:(tt + 1) * P, :], xr[:, tt, :]).then_inc(stored, 16)
            sp.wait_ge(stored, 16 * TT)

        @block.gpsimd
        def _(pool):
            order = Order(pool, pool_order)
            pool.memset(kT[:, :, 0:CHUNK], 0.0).then_inc(kt_zero, 1)
            pool.memset(none, NONE).then_inc(none_set, 1)
            pool.wait_ge(none_set, 1)
            pool.dma_start(lists.rearrange("(p n) f -> p (n f)", p=P), none).then_inc(lists_set, 16)
            for t in range(ST):
                pr = prs[t % 2]
                pool.wait_ge(prod_done, t + 1)
                pool.tensor_tensor(pr[0], pr[0], pr[1], ALU.add).then_inc(in_done, 1)
                read_out(pool, ("bu", t, 1))
                pool.tensor_tensor(pr[2], pr[2], pr[3], ALU.subtract).then_inc(in_done, 1)
                pool.wait_ge(out_prod, 2 * t + 1)
                if t:
                    states_read(pool, t - 1)
                pool.tensor_tensor(st_re, pr[0], pr[2], ALU.subtract).then_inc(st_done, 1)
                pool.wait_ge(out_prod, 2 * t + 2)
                pool.tensor_tensor(st_im, pr[1], pr[3], ALU.add).then_inc(st_done, 1)

            pool.wait_ge(lists_set, 16)
            pool.wait_ge(rec_done, 1)
            for tt in range(TT):
                for c in range(2):
                    pool.indirect_dma_start(lists, bass.IndirectOffsetOnAxis(idx[:, tt, c:c + 1], 0),
                                            rec[:, tt, c, :].bitcast(I32), None,
                                            bounds_check=T * NE - 1, oob_is_err=False).then_inc(listed, 16)
            pool.wait_ge(listed, 16 * 2 * TT)
            pool.dma_start(lst.rearrange("p (q e) f -> p q (e f)", e=NE),
                           lists.rearrange("(q p e) f -> p q (e f)", q=T // P, e=NE)).then_inc(lst_in, 16)
            pool.wait_ge(lst_in, 16)
            for n in range(2):
                pool.wait_ge(row_out[n], 32)

            last_token, last_result = pool.to_reg(T - 1), pool.to_reg(2 * T - 1)

            def gather(n, u):
                i = n * 4 + u
                wait(pool, xe_in[u], n * 16)
                wait(pool, hid_done, i - 3)
                pool.tensor_copy(rc[:, u, :], lst[:, i, :] if isinstance(i, int) else
                                 lst[:, bass.ds(i, 1), :].rearrange("p a f -> p (a f)")).then_inc(rc_ready, 1)
                pool.wait_ge(rc_ready, i + 1)
                wait(pool, xt_full, i - 3)
                pool.sem_inc(dma_begun, 1)
                pool.indirect_dma_start(xe[:, u, :], None, hrow, bass.IndirectOffsetOnAxis(rc[:, u, 0:1], 0),
                                        bounds_check=last_token, oob_is_err=False).then_inc(xe_in[u], 16)

            def scatter(n, u):
                i = n * 4 + u
                wait(pool, sc_done[u], n * 16)
                pool.tensor_copy(to[:, u:u + 1], lst[:, i, 1:2] if isinstance(i, int) else
                                 lst[:, bass.ds(i, 1), 1:2].rearrange("p a f -> p (a f)")).then_inc(to_ready, 1)
                pool.wait_ge(to_ready, i + 1)
                pool.wait_ge(oe_act, i + 1)
                pool.wait_ge(oe_dve, i + 1)
                pool.sem_inc(dma_begun, 1)
                pool.indirect_dma_start(yrow, bass.IndirectOffsetOnAxis(to[:, u:u + 1], 0), oe[:, u, :], None,
                                        bounds_check=last_result, oob_is_err=False).then_inc(sc_done[u], 16)

            def step(n, u):
                if not (isinstance(n, int) and n * 4 + u + 3 >= NE):
                    gather(n + (u + 3) // 4, (u + 3) % 4)
                scatter(n if u else n - 1, (u - 1) % 4)

            gather(0, 0)
            gather(0, 1)
            gather(0, 2)
            gather(0, 3)
            expert_steps(pool, step)
            scatter(7, 3)
            for u in range(SLOTS):
                pool.wait_ge(sc_done[u], 16 * NE // 4)

            def more(n, u, e):
                gather(n, u)
                scatter(n, u)
                pool.wait_ge(sc_done[u], (n + 1) * 16)

            overflow(pool, more)
            pool.memset(none[0:1, 0:1], 0).then_inc(moe_done, 1)

        @block.scalar
        def _(act):
            order = Order(act, act_order)

            def evac(key, dst, src, func=ACT.Copy, **kw):
                b, n = of[key]
                act.wait_ge(full[b], n + 1)
                act.activation(dst, src, func, **kw).then_inc(free[b], 1)

            act.dma_start(cst[:, :], consts).then_inc(cst_in, 16)
            with nc.allow_non_contiguous_dma("small parameters"):
                for n, src in enumerate((lam_re, lam_im)):
                    act.dma_start(par[:, n, :], src.rearrange("(t g) s -> (g s) t", g=2)).then_inc(par_in, 16)
                for g in range(2):
                    act.dma_start(par[g * NS:(g + 1) * NS, 2, :],
                                  log_step.rearrange("(t g) -> g t", g=2)[g:g + 1, :].broadcast_to([NS, ST])
                                  ).then_inc(par_in, 16)
                act.dma_start(g1[:, :], g_mix.rearrange("(p k) -> p k", k=KD)).then_inc(gain_in, 16)

            for tt in range(TT):
                act.wait_ge(x_in[tt], 16)
                act.activation(hT[:, 2 * tt:2 * tt + 2, :].rearrange("p a b -> p (a b)"), xr[:, tt, :],
                               ACT.Square, accum_out=small[:, tt:tt + 1]).then_inc(ssq_done, 1)
            act.wait_ge(rstd_done, 1)
            for tt in range(TT):
                if tt >= 2:
                    for half in range(2):
                        filled(act, ("xT", tt - 2, half))
                act.activation(xs[:, tt % 2, :], xr[:, tt, :], ACT.Copy,
                               scale=small[:, 8 + tt:9 + tt]).then_inc(xs_done, 1)
            act.wait_ge(cst_in, 16)
            act.wait_ge(par_turn, 1)
            act.activation(par[:, 9, :], par[:, 7, :], ACT.Sin, scale=TWO_PI)
            order.link(act.activation(par[:, 7, :], par[:, 7, :], ACT.Abs))
            act.activation(par[:, 10, :], par[:, 7, :], ACT.Sin, scale=-TWO_PI, bias=quarter).then_inc(par_trig, 1)
            for c in range(4):
                evac(("u", c), uT[:, c, :], pb[of[("u", c)][0]][:, :])
            for ri in range(2):
                evac(("bT", ri), bw[:, :, ri, :], pb[of[("bT", ri)][0]][:, :].rearrange("p (q s) -> p q s", s=P))
            for tt in (2, 3):
                for half in range(2):
                    filled(act, ("xT", tt, half))
            for ri in range(2):
                evac(("cT", ri), cw[:, :, ri, :], pb[of[("cT", ri)][0]][:, :].rearrange("p (q s) -> p q s", s=P))

            def whole_turns(t):
                act.wait_ge(turns, t + 1)
                act.activation(turn, turn, ACT.Copy, bias=-MAGIC).then_inc(whole, 1)

            def table(t):
                act.wait_ge(rot_done, t + 1)
                if t >= 2:
                    act.wait_ge(out_prod, 2 * (t - 2) + 2)
                act.activation(sin_t[t % 2], rot, ACT.Sin, scale=TWO_PI)
                order.link(act.activation(rot, rot, ACT.Abs))
                act.activation(cos_t[t % 2], rot, ACT.Sin, scale=-TWO_PI, bias=quarter).then_inc(cs_done, 1)

            def dense(key):
                b = pb[of[key][0]]
                if key[0] == "qkv":
                    blk, tt = divmod(key[1], TT)
                    evac(key, qkv[:, tt, blk * COLS:(blk + 1) * COLS], b[:, 0:COLS])
                else:
                    evac(key, gates[:, key[1], :], b[:, :], ACT.Tanh, scale=0.5)

            whole_turns(0)
            table(0)
            whole_turns(1)
            for t in range(ST):
                if t + 1 < ST:
                    table(t + 1)
                if t + 2 < ST:
                    whole_turns(t + 2)
                for w in slot_work(t):
                    dense(w)
                if t == 4:
                    for n in range(4):
                        read_out(act, ("qkv", 8 + n))
                    for h in range(2):
                        act.dma_start(v_mid[h * CHUNK:(h + 1) * CHUNK, :, :],
                                      qkv[(1 - h) * CHUNK:(2 - h) * CHUNK, h:h + 3, 640:768]).then_inc(v_moved, 16)
                if 4 <= t < 8:
                    if t > 4:
                        act.wait_ge(sum_done, t - 4)
                    act.activation(sqk, qkv[:, t - 4, 0:640], ACT.Square).then_inc(sq_done, 1)
                if 10 <= t < 14:
                    if t == 10:
                        act.wait_ge(qk_rstd, 1)
                    for h in range(NH + NKV):
                        head = qkv[:, t - 10, h * HD:(h + 1) * HD]
                        ins = act.activation(head, head, ACT.Copy, scale=nrm[:, 2, t - 10, h:h + 1])
                    ins.then_inc(qk_scaled, 1)
            for tt in range(TT):
                evac(("qT", tt), qT[:, :, tt * P:(tt + 1) * P],
                     pb[of[("qT", tt)][0]][:, :].rearrange("p (h t) -> p h t", t=P))
                evac(("kT", tt), kT[:, :, CHUNK + tt * P:CHUNK + (tt + 1) * P],
                     pb[of[("kT", tt)][0]][:, 0:NKV * P].rearrange("p (h t) -> p h t", t=P))

            def exps(c):
                lo = CHUNK if c == 0 else 0
                b, n = of[("score", c)]
                z = soft[:, c % 2]
                act.wait_ge(m_done, c + 1)
                if c >= 2:
                    filled(act, ("pT", c - 2))
                s = pb[b][:, :].rearrange("p (h k) -> p h k", k=P)
                for h in range(PAIRS):
                    ins = act.activation(prob[c % 2][:, h, lo:P], s[:, h, lo:P], ACT.Exp, scale=HD ** -0.5,
                                         bias=z[:, 2, h:h + 1], accum_out=z[:, 3, h:h + 1])
                ins.then_inc(free[b], 1)
                act.activation(z[:, 4, :], z[:, 5, :], ACT.Exp).then_inc(p_exp, 1)

            exps(0)
            for c in range(NC):
                lo = CHUNK if c == 0 else 0
                if c + 1 < NC:
                    exps(c + 1)
                if c % 2 == 0:
                    dense(("gate", 12 + c // 2))
                if c >= 2:
                    filled(act, ("pv", c - 2))
                evac(("pT", c), prT[c % 2][0:P - lo, :, :],
                     pb[of[("pT", c)][0]][0:P - lo, :].rearrange("p (h k) -> p h k", k=P))
            for q in range(4):
                read_out(act, ("y", q))
                order.link(act.activation(yT[:, q, :], yT[:, q, :], ACT.Gelu_apprx_tanh))
                act.activation(y2[:, q, :], yT[:, q, :], ACT.Copy, scale=0.5).then_inc(y_act, 1)
            for j in range(4):
                if j >= 2:
                    act.wait_ge(y2_done, j - 1)
                evac(("glu", j), sgl[:, j % 2, :], pb[of[("glu", j)][0]][:, :], ACT.Tanh, scale=0.5,
                     bias=bgh[:, j:j + 1])
            act.wait_ge(mg_done, KD)
            for tt in range(TT):
                read_out(act, ("o", tt, 1))
                act.activation(junk, xr[:, tt, :], ACT.Square, accum_out=small[:, 24 + tt:25 + tt]).then_inc(ssq2_done, 1)
                act.wait_ge(rstd2_done, tt + 1)
                if tt >= 2:
                    for half in range(2):
                        filled(act, ("hT", tt - 2, half))
                    act.wait_ge(row_out[tt % 2], 16)
                act.activation(xs[:, tt % 2, :], xr[:, tt, :], ACT.Copy,
                               scale=small[:, 32 + tt:33 + tt]).then_inc(xs2_done, 1)
                act.wait_ge(xs2_done, tt + 1)
                act.dma_start(hrow[tt * P:(tt + 1) * P, :], xs[:, tt % 2, :]).then_inc(row_out[tt % 2], 16)
            act.wait_ge(dexp_in, 1)
            act.activation(gtm, gtm, ACT.Exp)
            act.activation(st4[6], st4[6], ACT.Exp).then_inc(dexp_out, 1)

            def silu(n, u):
                i = n * 4 + u
                act.wait_ge(gu_done, i + 1)
                wait(act, hid_done, i - 1)
                act.activation(sg[:, u % 2, :], gu[u % 2][:, 0:DE], ACT.Silu).then_inc(silu_done, 1)

            def hidT_out(n, u):
                i = n * 4 + u
                act.wait_ge(ht_full, i + 1)
                wait(act, dn_done, i - 1)
                act.activation(hidT[:, u % 2, :, :], hb[:, 0:DE].rearrange("p (j c) -> p j c", c=P),
                               ACT.Copy).then_inc(ht_out, 1)

            def half_out(n, u):
                i = n * 4 + u
                act.wait_ge(dn_done, i + 1)
                wait(act, sc_done[u], n * 16)
                act.activation(oe[:, u, 512:D], ob[1][:, :], ACT.Copy).then_inc(oe_act, 1)

            def step(n, u):
                p, v = (n, u - 1) if u else (n - 1, 3)
                hidT_out(p, v)
                silu(n, u)
                half_out(p, v)

            silu(0, 0)
            expert_steps(act, step)
            hidT_out(7, 3)
            half_out(7, 3)

            def more(n, u, e):
                silu(n, u)
                hidT_out(n, u)
                half_out(n, u)

            overflow(act, more)

        @block.vector
        def _(dve):
            order = Order(dve, dve_order)
            link, mark = order.link, order.mark

            def rsqrt(y, v, t, done=None):
                link(dve.tensor_scalar(y.bitcast(I32), v.bitcast(I32), -0.5, 1597463007.0, ALU.mult, ALU.add))
                for n in range(3):
                    link(dve.tensor_tensor(t, y, y, ALU.mult))
                    link(dve.scalar_tensor_tensor(t, t, -0.5, v, ALU.mult, ALU.mult))
                    ins = dve.scalar_tensor_tensor(y, t, 1.5, y, ALU.add, ALU.mult)
                    if n == 2 and done is not None:
                        ins.then_inc(done, 1)
                    else:
                        link(ins)

            def exp(y, v, n, r, w):
                link(dve.tensor_scalar(v, v, -87.0, 88.0, ALU.max, ALU.min))
                link(dve.tensor_scalar(n, v, 1.4426950408889634, MAGIC, ALU.mult, ALU.add))
                link(dve.tensor_scalar(n, n, -MAGIC, None, ALU.add))
                link(dve.scalar_tensor_tensor(r, n, -LN2_HI, v, ALU.mult, ALU.add))
                link(dve.scalar_tensor_tensor(r, n, -LN2_LO, r, ALU.mult, ALU.add))
                link(dve.tensor_scalar(y, r, 1 / 5040, None, ALU.mult))
                for k in (720, 120, 24, 6, 2, 1):
                    link(dve.scalar_tensor_tensor(y, y, 1 / k, r, ALU.add, ALU.mult))
                link(dve.tensor_scalar(w.bitcast(I32), n, 127.0, 8388608.0, ALU.add, ALU.mult))
                link(dve.scalar_tensor_tensor(y, y, 1.0, w, ALU.add, ALU.mult))

            dve.wait_ge(ssq_done, TT)
            link(dve.tensor_scalar(small[:, 16:20], small[:, 0:4], 1.0 / D, EPS, ALU.mult, ALU.add))
            rsqrt(small[:, 8:12], small[:, 16:20], small[:, 20:24], rstd_done)

            def rows_out(kind, tt, half, g):
                src = filled(dve, (kind, tt, half))[:, :].rearrange("p (k t) -> p k t", t=P)
                ks = slice(4 * half, 4 * half + 4)
                dve.tensor_tensor(hT[:, ks, tt * P:(tt + 1) * P], src,
                                  g[:, ks].unsqueeze(2).broadcast_to([P, 4, P]), ALU.mult
                                  ).then_inc(free[of[(kind, tt, half)][0]], 1)

            dve.wait_ge(gain_in, 16)
            for tt in range(TT):
                for half in range(2):
                    rows_out("xT", tt, half, g1)

            lr, li, step_, mag, cyc, t1, t2, t3, cs, sn = (par[:, n, :] for n in (0, 1, 3, 4, 5, 6, 7, 8, 10, 9))
            ar, ai, den, fr, fi = (par[:, n, :] for n in range(11, 16))
            dve.wait_ge(par_in, 64)
            exp(step_, par[:, 2, :], t1, t2, t3)
            link(dve.tensor_tensor(sn, lr, step_, ALU.mult))
            exp(mag, sn, t1, t2, t3)
            link(dve.tensor_tensor(cyc, li, step_, ALU.mult))
            link(dve.tensor_scalar(cyc, cyc, 0.15915494309189535, None, ALU.mult))
            link(dve.tensor_scalar(t1, cyc, MAGIC, None, ALU.add))
            link(dve.tensor_scalar(t1, t1, -MAGIC, None, ALU.add))
            dve.tensor_tensor(t2, cyc, t1, ALU.subtract).then_inc(par_turn, 1)

            dve.wait_ge(par_trig, 1)
            mark(dve.tensor_tensor(ar, mag, cs, ALU.mult))
            link(dve.tensor_tensor(ai, mag, sn, ALU.mult))
            mark(dve.tensor_tensor(t1, lr, lr, ALU.mult))
            mark(dve.tensor_tensor(t2, li, li, ALU.mult))
            link(dve.tensor_scalar(ar, ar, -1.0, None, ALU.add))
            link(dve.tensor_tensor(den, t1, t2, ALU.add))
            mark(dve.reciprocal(den, den))
            mark(dve.tensor_tensor(t1, ar, lr, ALU.mult))
            mark(dve.tensor_tensor(t2, ai, li, ALU.mult))
            mark(dve.tensor_tensor(t3, ai, lr, ALU.mult))
            link(dve.tensor_tensor(sn, ar, li, ALU.mult))
            mark(dve.tensor_tensor(fr, t1, t2, ALU.add))
            link(dve.tensor_tensor(fi, t3, sn, ALU.subtract))
            mark(dve.tensor_tensor(fr, fr, den, ALU.mult))
            mark(dve.tensor_tensor(fi, fi, den, ALU.mult))
            dve.memset(blk_b[0], 0.0)
            link(dve.memset(blk_b[1], 0.0))
            dve.wait_ge(bc_in, 64)
            fr3, fi3 = (f.unsqueeze(2).broadcast_to([P, ST, SG]) for f in (fr, fi))
            mark(dve.tensor_tensor(tmp_b[0], raw_b[0], fr3, ALU.mult))
            mark(dve.tensor_tensor(tmp_b[1], raw_b[1], fi3, ALU.mult))
            mark(dve.tensor_tensor(tmp_b[2], raw_b[1], fr3, ALU.mult))
            link(dve.tensor_tensor(tmp_b[3], raw_b[0], fi3, ALU.mult))
            for g in range(2):
                h = slice(g * NS, (g + 1) * NS)
                dve.tensor_tensor(blk_b[0][h, :, g, :], tmp_b[0][h], tmp_b[1][h], ALU.subtract)
                dve.tensor_tensor(blk_b[1][h, :, g, :], tmp_b[2][h], tmp_b[3][h], ALU.add)
            dve.wait_ge(cst_in, 16)
            for g in range(2):
                for n in range(2):
                    ins = dve.tensor_scalar(blk_c[n][:, :, g, :], raw_c[n],
                                            cst[:, C_GL + 2 * n + g:C_GL + 2 * n + g + 1], None, ALU.mult)
            ins.then_inc(blk_done, 1)

            def turns_of(t):
                if t == 0:
                    dve.wait_ge(blk_done, 1)
                else:
                    dve.wait_ge(rot_done, t)

                dve.tensor_scalar(turn, tpos, cyc[:, t:t + 1], MAGIC, ALU.mult, ALU.add).then_inc(turns, 1)

            def rot_of(t):
                dve.wait_ge(whole, t + 1)
                wait(dve, cs_done, t)
                dve.scalar_tensor_tensor(rot, tpos, cyc[:, t:t + 1], turn, ALU.mult, ALU.subtract).then_inc(rot_done, 1)

            def y_of(q):
                src = filled(dve, ("y", q))
                dve.scalar_tensor_tensor(yT[:, q, :], uT[:, q, :], dsk[:, q:q + 1], src[:, :], ALU.mult, ALU.add
                                         ).then_inc(free[4], 1)

            def qk_sums(tt):
                dve.wait_ge(sq_done, tt + 1)
                dve.tensor_reduce(nrm[:, 0, tt, :], sqk.rearrange("p (h d) -> p h d", d=HD), AX.X, ALU.add
                                  ).then_inc(sum_done, 1)

            def qk_rms():
                dve.wait_ge(sum_done, TT)
                link(dve.tensor_scalar(nrm[:, 1], nrm[:, 0], 1.0 / HD, EPS, ALU.mult, ALU.add))
                rsqrt(nrm[:, 2], nrm[:, 1], nrm[:, 3], qk_rstd)

            def qk_norm(tt):
                dve.wait_ge(qk_scaled, tt + 1)
                qk = qkv[:, tt, 0:640].rearrange("p (h d) -> p h d", d=HD)
                q = qk[:, 0:NH, :]
                mark(dve.tensor_tensor(q, q, qkn[:, 0:1, :].broadcast_to([P, NH, HD]), ALU.mult))
                kd = kdup[:, tt]
                for r in range(2):
                    ins = dve.tensor_tensor(kd[:, :, r, :], qk[:, NH:, :], qkn[:, 1:2, :].broadcast_to([P, NKV, HD]),
                                            ALU.mult)
                link(ins)
                cos, sin = (cst[:, C_ROPE + 32 * tt + 16 * n:C_ROPE + 32 * tt + 16 * n + 16] for n in range(2))
                kf = kd.rearrange("p v r d -> p (v r) d")
                for a, h, n in ((q, NH, 0), (kf, 2 * NKV, 1)):
                    ta = ropet[n].rearrange("p (h c) -> p h c", c=16)
                    tb = ropes[n].rearrange("p (h c) -> p h c", c=16)
                    dve.tensor_tensor(ta, a[:, :, 0:16], cos.unsqueeze(1).broadcast_to([P, h, 16]), ALU.mult)
                    dve.tensor_tensor(tb[:, :, 0:8], a[:, :, 8:16], sin[:, 0:8].unsqueeze(1).broadcast_to([P, h, 8]), ALU.mult)
                    link(dve.tensor_tensor(tb[:, :, 8:16], a[:, :, 0:8], sin[:, 8:16].unsqueeze(1).broadcast_to([P, h, 8]), ALU.mult))
                    ins = dve.tensor_tensor(a[:, :, 0:16], ta, tb, ALU.add)
                ins.then_inc(qk_done, 1)

            dve.wait_ge(late_in, 16 * len(late))
            dve.tensor_scalar(bgh[:, :], bgl[:, :], 0.5, None, ALU.mult)
            turns_of(0)
            rot_of(0)
            turns_of(1)
            for t in range(ST):
                si, co = sin_t[t % 2], cos_t[t % 2]
                pr = prs[t % 2]
                br = filled(dve, ("bu", t, 0))
                bi = filled(dve, ("bu", t, 1))
                dve.wait_ge(cs_done, t + 1)
                if t == 1:
                    dve.wait_ge(lists_set, 16)
                if t >= 2:
                    dve.wait_ge(st_done, 2 * t - 2)
                dve.tensor_tensor(pr[0], br[:, :], co, ALU.mult)
                dve.tensor_tensor(pr[1], bi[:, :], si, ALU.mult).then_inc(prod_done, 1)
                dve.tensor_tensor(pr[3], br[:, :], si, ALU.mult).then_inc(free[of[("bu", t, 0)][0]], 1)
                dve.tensor_tensor(pr[2], bi[:, :], co, ALU.mult).then_inc(free[of[("bu", t, 1)][0]], 1)
                if t + 1 < ST:
                    rot_of(t + 1)
                if 5 <= t < 9:
                    qk_sums(t - 5)
                decay = mag[:, t:t + 1].broadcast_to([P, T])
                dve.wait_ge(in_done, 2 * t + 1)
                z_re = mark(dve.tensor_tensor_scan(pr[1], decay, pr[0], 0.0, ALU.mult, ALU.add))
                if t + 2 < ST:
                    turns_of(t + 2)
                dve.wait_ge(in_done, 2 * t + 2)
                z_im = mark(dve.tensor_tensor_scan(pr[3], decay, pr[2], 0.0, ALU.mult, ALU.add))
                order.wait(z_re)
                dve.tensor_tensor(pr[0], pr[1], co, ALU.mult)
                order.wait(z_im)
                dve.tensor_tensor(pr[2], pr[3], si, ALU.mult).then_inc(out_prod, 1)
                dve.wait_ge(out_prod, 2 * t + 1)
                dve.tensor_tensor(pr[1], pr[1], si, ALU.mult)
                dve.tensor_tensor(pr[3], pr[3], co, ALU.mult).then_inc(out_prod, 1)
                if t == 9:
                    qk_rms()
                if 11 <= t < 15:
                    qk_norm(t - 11)
                if t % 4 == 1 and t > 4:
                    y_of((t - 5) // 4)
            y_of(3)

            def maxima(c):
                lo = CHUNK if c == 0 else 0
                z = soft[:, c % 2]
                s = filled(dve, ("score", c))[:, :].rearrange("p (h k) -> p h k", k=P)
                link(dve.tensor_reduce(z[:, 0, :], s[:, :, lo:P], AX.X, ALU.max))
                link(dve.scalar_tensor_tensor(z[:, 1, :], z[:, 0, :], HD ** -0.5, snk[:, :], ALU.mult, ALU.max))
                dve.tensor_scalar(z[:, 2, :], z[:, 1, :], -1.0, None, ALU.mult)
                dve.tensor_tensor(z[:, 5, :], snk[:, :], z[:, 1, :], ALU.subtract).then_inc(m_done, 1)

            def normalise(c):
                lo = CHUNK if c == 0 else 0
                z = soft[:, c % 2]
                dve.wait_ge(p_exp, c + 1)
                link(dve.tensor_tensor(z[:, 6, :], z[:, 3, :], z[:, 4, :], ALU.add))
                link(dve.reciprocal(z[:, 7, :], z[:, 6, :]))
                pc = prob[c % 2][:, :, lo:P]
                dve.tensor_tensor(pc, pc, z[:, 7, :].unsqueeze(2).broadcast_to([P, PAIRS, P - lo]), ALU.mult
                                  ).then_inc(p_done, 1)

            def attended(c):
                src = filled(dve, ("pv", c))
                dve.tensor_copy(qT[:, :, c * CHUNK:(c + 1) * CHUNK],
                                src[:, 0:PAIRS * CHUNK].rearrange("p (h t) -> p h t", t=CHUNK)).then_inc(free[4], 1)

            maxima(0)
            for c in range(NC):
                if c + 1 < NC:
                    maxima(c + 1)
                normalise(c)
                if c:
                    attended(c - 1)
            attended(NC - 1)

            for j in range(4):
                read_out(dve, ("glu", j))
                dve.scalar_tensor_tensor(y2[:, j, :], sgl[:, j % 2, :], 1.0, y2[:, j, :], ALU.add, ALU.mult
                                         ).then_inc(y2_done, 1)
            for j in range(KD):
                src = filled(dve, ("ssm", j))
                dve.scalar_tensor_tensor(mg[:, j, :], gates[:, j, :], 1.0, src[:, :], ALU.add, ALU.mult
                                         ).then_inc(free[of[("ssm", j)][0]], 1)
                src = filled(dve, ("att", j))
                dve.scalar_tensor_tensor(mtmp[:, j % 2, :], gates[:, KD + j, :], 1.0, src[:, :], ALU.add, ALU.mult
                                         ).then_inc(free[of[("att", j)][0]], 1)
                read_out(dve, ("att", j))
                dve.tensor_tensor(mg[:, j, :], mg[:, j, :], mtmp[:, j % 2, :], ALU.add).then_inc(mg_done, 1)

            def residual(tt):
                for half in range(2):
                    src = filled(dve, ("o", tt, half))
                    xh = xr[:, tt, half * 512:(half + 1) * 512]
                    dve.scalar_tensor_tensor(xh, src[:, :], 0.5, xh, ALU.mult, ALU.add
                                             ).then_inc(free[of[("o", tt, half)][0]], 1)
                dve.wait_ge(ssq2_done, tt + 1)
                v = small[:, 40 + tt:41 + tt]
                link(dve.tensor_scalar(v, small[:, 24 + tt:25 + tt], 1.0 / D, EPS, ALU.mult, ALU.add))
                rsqrt(small[:, 32 + tt:33 + tt], v, small[:, 44 + tt:45 + tt], rstd2_done)

            def logits(tt):
                for half in range(2):
                    rows_out("hT", tt, half, g2)
                src = filled(dve, ("logit", tt))
                dve.tensor_tensor(lg[:, tt, :], src[:, 0:NR], brt[:, :], ALU.add).then_inc(free[4], 1)

            residual(0)
            for tt in range(1, TT):
                residual(tt)
                logits(tt - 1)
            logits(TT - 1)
            read_out(dve, ("logit", TT - 1))

            def over(a, n):
                return a.unsqueeze(2).broadcast_to([P, TT, n])

            def first_best(v, one, tmp, iota, n, best, at):
                link(dve.tensor_reduce(best, v, AX.X, ALU.max))
                link(dve.tensor_tensor(one, v, over(best, n), ALU.is_equal))
                link(dve.scalar_tensor_tensor(tmp, one, -64.0, iota.unsqueeze(1).broadcast_to([P, TT, n]),
                                              ALU.mult, ALU.add))
                link(dve.tensor_reduce(at, tmp, AX.X, ALU.min))
                link(dve.tensor_tensor(one, tmp, over(at, n), ALU.is_equal))

            i4, i8, ie = cst[:, C_I4:C_I4 + NGRP], cst[:, C_I8:C_I8 + EPG], cst[:, C_E:C_E + NE]
            gl, el = lg[:, :, 0:NGRP], lg[:, :, NGRP:NR].rearrange("p t (g e) -> p t g e", e=EPG)
            first_best(gl, goh, gtm, i4, NGRP, st4[0], st4[1])
            link(dve.tensor_tensor(gtm, gl, over(st4[0], NGRP), ALU.subtract))
            link(dve.tensor_tensor(gsel, el, goh.unsqueeze(3).broadcast_to([P, TT, NGRP, EPG]), ALU.mult))
            link(dve.tensor_reduce(esel, gsel.rearrange("p t g e -> p t e g"), AX.X, ALU.add))
            first_best(esel, oh[0], etm, i8, EPG, st4[2], st4[3])
            link(dve.scalar_tensor_tensor(esel, oh[0], -3e38, esel, ALU.mult, ALU.add))
            first_best(esel, oh[1], etm, i8, EPG, st4[4], st4[5])
            dve.tensor_tensor(st4[6], st4[4], st4[2], ALU.subtract).then_inc(dexp_in, 1)
            for c in range(2):
                mark(dve.tensor_tensor(ohe[c].rearrange("p t (g e) -> p t g e", e=EPG),
                                       goh.unsqueeze(3).broadcast_to([P, TT, NGRP, EPG]),
                                       oh[c].unsqueeze(2).broadcast_to([P, TT, NGRP, EPG]), ALU.mult))
            order.wait()
            dve.tensor_tensor(both, ohe[0], ohe[1], ALU.add).then_inc(both_done, 1)
            mark(dve.tensor_copy(rec.bitcast(I32), cst[:, C_REC:C_Q].bitcast(I32).rearrange("p (t c f) -> p t c f", c=2, f=4)))
            dve.wait_ge(dexp_out, 1)
            mark(dve.tensor_reduce(st4[7], gtm, AX.X, ALU.add))
            link(dve.tensor_scalar(st4[8], st4[6], 1.0, None, ALU.add))
            link(dve.tensor_tensor(st4[7], st4[7], st4[8], ALU.mult))
            link(dve.reciprocal(st4[7], st4[7]))
            mark(dve.tensor_copy(rec[:, :, 0, 2], st4[7]))
            mark(dve.tensor_tensor(rec[:, :, 1, 2], st4[7], st4[6], ALU.mult))
            src = filled(dve, ("rank",))
            link(dve.scalar_tensor_tensor(place, src[:, 0:TT * NE].rearrange("p (t e) -> p t e", e=NE), float(NE),
                                          ie.unsqueeze(1).broadcast_to([P, TT, NE]), ALU.mult, ALU.add))
            for c in range(2):
                mark(dve.tensor_tensor(ohe[c], ohe[c], place, ALU.mult))
            order.wait()
            for c in range(2):
                mark(dve.tensor_reduce(st4[8 + c], ohe[c], AX.X, ALU.add))
            order.wait()
            for c in range(2):
                ins = dve.tensor_copy(idx[:, :, c], st4[8 + c])
            ins.then_inc(rec_done, 1)
            src = filled(dve, ("count",))
            link(dve.tensor_reduce(small[0:1, 48:49], src[0:1, 0:NE], AX.X, ALU.max))
            dve.tensor_copy(most[0:1, 0:1], small[0:1, 48:49]).then_inc(most_done, 1)

            def rows_turned(n, u):
                i = n * 4 + u
                dve.wait_ge(xt_full, i + 1)
                wait(dve, gu_done, i - 1)
                for half in range(2):
                    ks = slice(4 * half, 4 * half + 4)
                    ins = dve.tensor_tensor(xeT[:, u % 2, ks, :], tb[half][:, :].rearrange("p (k c) -> p k c", c=P),
                                            g2[:, ks].unsqueeze(2).broadcast_to([P, 4, P]), ALU.mult)
                ins.then_inc(xt_out, 1)

            def hidden(n, u):
                i = n * 4 + u
                dve.wait_ge(silu_done, i + 1)
                dve.wait_ge(rc_ready, i + 1)
                wait(dve, ht_full, i - 1)
                dve.scalar_tensor_tensor(hid[:, u % 2, :], gu[u % 2][:, DE:2 * DE], rc[:, u, 2:3].bitcast(F32),
                                         sg[:, u % 2, :], ALU.mult, ALU.mult).then_inc(hid_done, 1)

            def half_out(n, u):
                i = n * 4 + u
                dve.wait_ge(dn_done, i + 1)
                wait(dve, sc_done[u], n * 16)
                dve.tensor_copy(oe[:, u, 0:512], ob[0][:, :]).then_inc(oe_dve, 1)

            def step(n, u, last=False):
                if not (isinstance(n, int) and n * 4 + u + 1 >= NE):
                    rows_turned(n + (u + 1) // 4, (u + 1) % 4)
                hidden(n, u)
                half_out(n if u else n - 1, (u - 1) % 4)

            rows_turned(0, 0)
            rows_turned(0, 1)
            hidden(0, 0)
            expert_steps(dve, step)
            half_out(7, 3)

            def more(n, u, e):
                rows_turned(n, u)
                hidden(n, u)
                half_out(n, u)

            overflow(dve, more)
            ys = [slot0[:, 2048 * t:2048 * (t + 1)] for t in range(3)] + [slot1[:, 0:2048]]
            for tt in range(TT):
                y = ys[tt].rearrange("p (c d) -> p c d", c=2)
                dve.wait_ge(y_in[tt], 16)
                link(dve.tensor_tensor(y[:, 0, :], y[:, 0, :], y[:, 1, :], ALU.add))
                dve.tensor_tensor(xr[:, tt, :], xr[:, tt, :], y[:, 0, :], ALU.add).then_inc(out_ready, 1)

        @block.tensor
        def _(pe):
            def begin(key):
                b, n = of[key]
                if n:
                    pe.wait_ge(free[b], n)
                return pb[b]

            def end(key, ins):
                ins.then_inc(full[of[key][0]], 1)

            def weight(kind, c):
                n = block_at[(kind, c)]
                pe.wait_ge(ring_in[n % RING], 16 * (n // RING + 1))
                return ring[:, n % RING, :].rearrange("p (k n) -> p k n", k=KD if kind in ("in", "out") else 4)

            def product(dst, pairs):
                for n, (lhsT, rhs) in enumerate(pairs):
                    ins = pe.matmul(dst, lhsT, rhs, start=(n == 0), stop=(n == len(pairs) - 1))
                return ins

            def turn_rows(kind, tt, rows):
                for half in range(2):
                    b = begin((kind, tt, half))
                    for k in range(4):
                        ins = pe.transpose(b[:, k * P:(k + 1) * P], rows[:, 4 * half + k::KD], ident)
                    end((kind, tt, half), ins)

            pe.wait_ge(cst_in, 16)
            for tt in range(TT):
                pe.wait_ge(xs_done, tt + 1)
                turn_rows("xT", tt, xs[:, tt % 2, :])
            for tt in range(TT):
                for half in range(2):
                    read_out(pe, ("xT", tt, half))
            for c in range(4):
                w = weight("in", c // 2)
                b = begin(("u", c))
                cols = slice((c % 2) * P, (c % 2 + 1) * P)
                ins = product(b[:, :], [(w[:, k, cols], hT[:, k, :]) for k in range(KD)])
                end(("u", c), ins)
            pe.wait_ge(blk_done, 1)
            for ri in range(2):
                b = begin(("bT", ri))
                src = blk_b[ri].rearrange("p t g h -> p (t g h)")
                for q in range(4):
                    ins = pe.transpose(b[:, q * P:(q + 1) * P], src[:, q * P:(q + 1) * P], ident)
                end(("bT", ri), ins)
            for ri in range(2):
                b = begin(("cT", ri))
                src = blk_c[ri].rearrange("p q g s -> p (q g s)")
                for q in range(4):
                    ins = pe.transpose(b[:, q * P:(q + 1) * P], src[:, q * P:(q + 1) * P], ident)
                end(("cT", ri), ins)
            for ri in range(2):
                read_out(pe, ("bT", ri))
                read_out(pe, ("cT", ri))
            for c in range(4):
                read_out(pe, ("u", c))

            def inputs_of(t):
                rows = slice(32 * (t % 4), 32 * (t % 4) + 32)
                for ri in range(2):
                    key = ("bu", t, ri)
                    b = begin(key)
                    end(key, pe.matmul(b[:, :], bw[rows, t // 4, ri, :], uT[rows, t // 4, :], start=True, stop=True))

            def outputs_of(t):
                j = 32 * (t % 4)
                key = ("y", t // 4)
                b = begin(key) if t % 4 == 0 else pb[4]
                pe.wait_ge(st_done, 2 * t + 1)
                pe.matmul(b[j:j + 32, :], cw[:, t // 4, 0, j:j + 32], st_re, start=True, stop=False)
                pe.wait_ge(st_done, 2 * t + 2)
                ins = pe.matmul(b[j:j + 32, :], cw[:, t // 4, 1, j:j + 32], st_im, start=False, stop=True)
                if t % 4 == 3:
                    end(key, ins)
                else:
                    ins.then_inc(st_used, 1)

            def dense(key):
                b = begin(key)
                if key[0] == "qkv":
                    blk, tt = divmod(key[1], TT)
                    w = weight("in", 2 + blk)
                    ins = product(b[:, 0:COLS], [(hT[:, k, tt * P:(tt + 1) * P], w[:, k, :]) for k in range(KD)])
                else:
                    w = weight("in", 5 + key[1] // 2)
                    cols = slice((key[1] % 2) * P, (key[1] % 2 + 1) * P)
                    ins = product(b[:, :], [(w[:, k, cols], hT[:, k, :]) for k in range(KD)])
                end(key, ins)

            for t in range(2):
                inputs_of(t)
            for t in range(ST):
                for key in slot_work(t):
                    dense(key)
                if t:
                    outputs_of(t - 1)
                if t + 2 < ST:
                    inputs_of(t + 2)
            outputs_of(ST - 1)

            for tt in range(TT):
                pe.wait_ge(qk_done, tt + 1)
                b = begin(("qT", tt))
                for h in range(PAIRS):
                    ins = pe.transpose(b[:, h * P:(h + 1) * P], qkv[:, tt, h * P:(h + 1) * P], ident)
                end(("qT", tt), ins)
                b = begin(("kT", tt))
                for v in range(NKV):
                    ins = pe.transpose(b[:, v * P:(v + 1) * P], kdup[:, tt, v].rearrange("p r d -> p (r d)"), ident)
                end(("kT", tt), ins)
            pe.wait_ge(kt_zero, 1)
            for tt in range(TT):
                read_out(pe, ("qT", tt))
                read_out(pe, ("kT", tt))

            def scores(c):
                lo = CHUNK if c == 0 else 0
                b = begin(("score", c))
                for h in range(NH):
                    r = slice((h % 2) * HD, (h % 2 + 1) * HD)
                    ins = pe.matmul(b[r, (h // 2) * P + lo:(h // 2 + 1) * P], qT[r, h // 2, c * CHUNK:(c + 1) * CHUNK],
                                    kT[r, h // (NH // NKV), c * CHUNK + lo:c * CHUNK + P], start=True, stop=True)
                end(("score", c), ins)

            def turn_probs(c):
                lo = CHUNK if c == 0 else 0
                pe.wait_ge(p_done, c + 1)
                b = begin(("pT", c))
                for h in range(PAIRS):
                    ins = pe.transpose(b[0:P - lo, h * P:(h + 1) * P], prob[c % 2][:, h, lo:P], ident)
                end(("pT", c), ins)

            def attend(c):
                k = CHUNK if c == 0 else P
                read_out(pe, ("pT", c))
                b = begin(("pv", c))
                if c == 2:
                    pe.wait_ge(v_moved, 32)
                for v in range(NKV):
                    if c % 2 or c == 0:
                        val = qkv[0:k, c // 2, 640 + v * HD:640 + (v + 1) * HD]
                    else:
                        val = v_mid[:, c // 2 - 1, v * HD:(v + 1) * HD]
                    for r in range(2):
                        ins = pe.matmul(b[r * HD:(r + 1) * HD, v * 2 * CHUNK:(v + 1) * 2 * CHUNK], val,
                                        prT[c % 2][0:k, 2 * v:2 * v + 2, r * CHUNK:(r + 1) * CHUNK],
                                        start=True, stop=True)
                end(("pv", c), ins)

            scores(0)
            for c in range(NC):
                if c + 1 < NC:
                    scores(c + 1)
                if c % 2 == 0:
                    dense(("gate", 12 + c // 2))
                turn_probs(c)
                if c:
                    attend(c - 1)
            attend(NC - 1)

            w = weight("glu", 0)
            pe.wait_ge(y_act, 4)
            for j in range(4):
                b = begin(("glu", j))
                end(("glu", j), product(b[:, :], [(w[:, k, j * P:(j + 1) * P], yT[:, k, :]) for k in range(4)]))
            pe.wait_ge(y2_done, 4)
            read_out(pe, ("pv", NC - 1))
            for j in range(KD):
                cols = slice((j % 4) * P, (j % 4 + 1) * P)
                for kind, src in (("ssm", y2), ("att", qT)):
                    w = weight(kind, j // 4)
                    b = begin((kind, j))
                    end((kind, j), product(b[:, :], [(w[:, k, cols], src[:, k, :]) for k in range(4)]))

            def project(tt):
                for half in range(2):
                    for c in range(2):
                        weight("out", 2 * half + c)
                    s = block_at[("out", 2 * half)] % RING
                    w = ring[:, s:s + 2, :].rearrange("p c (k n) -> p c k n", k=KD)
                    b = begin(("o", tt, half))
                    end(("o", tt, half), product(b[:, :], [(hTm[:, k, tt * P:(tt + 1) * P], w[:, :, k, :])
                                                           for k in range(KD)]))

            def route(tt):
                pe.wait_ge(xs2_done, tt + 1)
                turn_rows("hT", tt, xs[:, tt % 2, :])
                for half in range(2):
                    read_out(pe, ("hT", tt, half))
                b = begin(("logit", tt))
                end(("logit", tt), product(b[:, 0:NR], [(hT[:, k, tt * P:(tt + 1) * P], wr[:, k, :]) for k in range(KD)]))

            hTm = mg
            pe.wait_ge(mg_done, KD)
            pe.wait_ge(late_in, 16 * len(late))
            project(0)
            for tt in range(1, TT):
                project(tt)
                route(tt - 1)
            route(TT - 1)
            pe.wait_ge(both_done, 1)
            b = begin(("rank",))
            for t in range(TT):
                ins = product(b[:, t * NE:(t + 1) * NE], [(ones, both[:, s, :]) for s in range(t)] + [(tri, both[:, t, :])])
            end(("rank",), ins)
            b = begin(("count",))
            end(("count",), product(b[0:1, 0:NE], [(ones[:, 0:1], both[:, s, :]) for s in range(TT)]))
            for n in range(8):
                if n not in (5, 6):
                    pe.wait_ge(free[n], banks.used[n])
            pe.wait_ge(rec_done, 1)
            pe.wait_ge(most_done, 1)

            def turn_tile(n, u):
                i = n * 4 + u
                pe.wait_ge(xe_in[u], (n + 1) * 16)
                wait(pe, xt_out, i)
                for k in range(KD):
                    ins = pe.transpose(tb[k // 4][:, (k % 4) * P:(k % 4 + 1) * P], xe[:, u, k::KD], ident)
                ins.then_inc(xt_full, 1)

            def gate_up(n, u):
                i = n * 4 + u
                pe.wait_ge(xt_out, i + 1)
                pe.wait_ge(gu_in[u], (n + 1) * 32)
                wait(pe, hid_done, i - 1)
                w = eslot[u][:, 0:2 * BLOCK].rearrange("p (m k f) -> p m k f", m=2, k=KD)
                product(gu[u % 2][:, :], [(xeT[:, u % 2, k, :], w[:, :, k, :]) for k in range(KD)]).then_inc(gu_done, 1)

            def turn_hidden(n, u):
                i = n * 4 + u
                pe.wait_ge(hid_done, i + 1)
                wait(pe, ht_out, i)
                for j in range(2):
                    ins = pe.transpose(hb[:, j * P:(j + 1) * P], hid[:, u % 2, j::2], ident)
                ins.then_inc(ht_full, 1)

            def down(n, u):
                i = n * 4 + u
                pe.wait_ge(ht_out, i + 1)
                pe.wait_ge(dn_in[u], (n + 1) * 16)
                wait(pe, oe_act, i)
                wait(pe, oe_dve, i)
                w = eslot[u][:, 2 * BLOCK:3 * BLOCK].rearrange("p (j d) -> p j d", j=2)
                for half in range(2):
                    ins = product(ob[half][:, :], [(hidT[:, u % 2, j, :], w[:, j, half * 512:(half + 1) * 512])
                                                   for j in range(2)])
                ins.then_inc(dn_done, 1)

            def step(n, u):
                p, v = (n, u - 1) if u else (n - 1, 3)
                turn_hidden(p, v)
                if not (isinstance(n, int) and n * 4 + u + 1 >= NE):
                    turn_tile(n + (u + 1) // 4, (u + 1) % 4)
                gate_up(n, u)
                down(p, v)

            turn_tile(0, 0)
            turn_tile(0, 1)
            gate_up(0, 0)
            expert_steps(pe, step)
            turn_hidden(7, 3)
            down(7, 3)

            def more(n, u, e):
                turn_tile(n, u)
                gate_up(n, u)
                turn_hidden(n, u)
                down(n, u)

            overflow(pe, more)


_INS = ["x", "g_mix", "w_in", "q_norm", "k_norm", "ssm_lambda_re", "ssm_lambda_im", "ssm_log_step",
        "ssm_b_re", "ssm_b_im", "ssm_c_re", "ssm_c_im", "ssm_d", "ssm_w_glu", "ssm_b_glu", "attn_sinks",
        "w_ssm_proj", "w_attn_proj", "w_out", "g_ffn", "w_group_router", "b_group_router",
        "w_expert_router", "b_expert_router", "w_expert_gate", "w_expert_up", "w_expert_down"]


def kernel(**inputs):
    import concourse.bacc as bacc
    from concourse.bass_utils import run_bass_kernel_spmd

    nc = bacc.Bacc("TRN2", target_bir_lowering=False, num_devices=1)
    arrays, args = {}, []
    for name in _INS:
        a = np.ascontiguousarray(inputs[name])
        if name != "x":
            a = a[0]
        arrays[f"in_{name}"] = a
    arrays["in_constants"] = constants()
    for name, a in arrays.items():
        args.append(nc.dram_tensor(name, a.shape, mybir.dt.from_np(a.dtype), kind="ExternalInput").ap())
    out = nc.dram_tensor("out_x", (1, T, D), F32, kind="ExternalOutput").ap()
    build(nc, *args, out)
    r = run_bass_kernel_spmd(nc, [arrays], core_ids=[0])
    return r.results[0]["out_x"]
```

```python
from contextlib import ExitStack

import numpy as np

import concourse.bass as bass
from concourse import mybir

F32 = mybir.dt.float32
I32 = mybir.dt.int32
ALU = mybir.AluOpType
ACT = mybir.ActivationFunctionType
AX = mybir.AxisListType

P = 128
D = 1024
KD = D // P
T = 512
TT = T // P
CH = 512
NG, SG, NS = 32, 16, 64
ST = NG * NS // P
NH, HD = 8, 64
NKV = 2
PAIRS = NH // 2
QKV = NH * HD + 2 * NKV * HD
CHUNK = 64
NC = T // CHUNK
W_IN = CH + QKV + 2 * D
COLS = 256
BLOCK = KD * COLS
RING = 4
NGRP, EPG = 4, 8
NE = NGRP * EPG
DE = 256
SLOTS = 4
ROWS = P // 2
TILES = NE // 2
NR = NGRP + NE
LIST = 5
EPS = 1e-6
MAGIC = 12582912.0
TWO_PI = 6.283185
NONE = 4096
LN2_HI, LN2_LO = 0.693359375, -2.12194440e-4

C_ID, C_TRI, C_ONE = 0, 128, 256
C_T = 384
C_ROPE = C_T + T
C_GL = C_ROPE + TT * 32
C_I4 = C_GL + 4
C_I8 = C_I4 + NGRP
C_REC = C_I8 + EPG
C_Q = C_REC + TT * 6
C_N = C_Q + 1


def constants():
    c = np.zeros((P, C_N), np.float32)
    c[:, C_ID:C_ID + P] = np.eye(P)
    c[:, C_TRI:C_TRI + P] = np.triu(np.ones((P, P)), 1)
    c[:, C_ONE:C_ONE + P] = 1.0
    c[:, C_T:C_T + T] = np.arange(T)
    inv = np.float32(500000.0) ** (-np.arange(0, 16, 2, dtype=np.float32) / np.float32(16))
    ang = (np.arange(T, dtype=np.float32)[:, None] * inv[None]).astype(np.float64)
    rope = np.concatenate([np.cos(ang), np.cos(ang), -np.sin(ang), np.sin(ang)], 1)
    c[:, C_ROPE:C_GL] = rope.reshape(TT, P, 32).transpose(1, 0, 2).reshape(P, TT * 32)
    odd = (np.arange(P) // SG) % 2
    for n, m in enumerate((1 - odd, odd, odd - 1, -odd)):
        c[:, C_GL + n] = m
    c[:, C_I4:C_I4 + NGRP] = np.arange(NGRP)
    c[:, C_I8:C_I8 + EPG] = np.arange(EPG)
    rec = np.zeros((P, TT, 2, 3), np.float32)
    tok = np.arange(TT)[None, :] * P + np.arange(P)[:, None]
    for choice in range(2):
        rec[:, :, choice, 0] = tok - NONE
        rec[:, :, choice, 1] = tok + T * choice - NONE
    c[:, C_Q] = np.pi / 2
    c[:, C_REC:C_Q] = rec.reshape(P, TT * 6)
    return c


class Order:

    def __init__(self, eng, sem):
        self.eng, self.sem, self.n = eng, sem, 0

    def mark(self, ins):
        self.n += 1
        ins.then_inc(self.sem, 1)
        return self.n

    def wait(self, n=None):
        self.eng.wait_ge(self.sem, self.n if n is None else n)

    def link(self, ins):
        self.mark(ins)
        self.wait()


class Banks:

    def __init__(self):
        self.used = [0] * 8
        self.of = {}
        self.turn = 0

    def take(self, key, bank=None):
        if bank is None:
            bank = 5 + self.turn % 3
            self.turn += 1
        self.of[key] = (bank, self.used[bank])
        self.used[bank] += 1


def slot_work(t):
    if t < 4:
        return [("qkv", 3 * t + i) for i in range(3)]
    return [("gate", t - 4)]


def plan_banks():
    b = Banks()
    for tt in range(TT):
        for half in range(2):
            b.take(("xT", tt, half), (2 * tt + half) % 4)
    for c in range(TT):
        b.take(("u", c))
    for ri in range(2):
        b.take(("bT", ri), ri)
        b.take(("cT", ri), 2 + ri)
    for t in range(2):
        for ri in range(2):
            b.take(("bu", t, ri), (t % 2) * 2 + ri)
    for t in range(ST):
        for w in slot_work(t):
            b.take(w)
        if t + 2 < ST:
            for ri in range(2):
                b.take(("bu", t + 2, ri), (t % 2) * 2 + ri)
        if t % 4 == 0:
            b.take(("y", t // 4), 4)
    for tt in range(TT):
        b.take(("qT", tt))
        b.take(("kT", tt))
    for c in range(NC):
        b.take(("score", c), c % 2)
        if c % 2 == 0:
            b.take(("gate", 12 + c // 2))
        b.take(("pT", c), 2 + c % 2)
        b.take(("pv", c), 4)
    for j in range(4):
        b.take(("glu", j))
    for j in range(KD):
        b.take(("ssm", j))
        b.take(("att", j))
    for tt in range(TT):
        for half in range(2):
            b.take(("o", tt, half))
    for tt in range(TT):
        for half in range(2):
            b.take(("hT", tt, half), (2 * tt + half) % 4)
        b.take(("logit", tt), 4)
    b.take(("rank",), LIST)
    b.take(("count",), LIST + 1)
    return b


def weight_blocks():
    blocks = [("in", c) for c in range(W_IN // COLS)]
    blocks += [("glu", 0), ("ssm", 0), ("att", 0), ("ssm", 1), ("att", 1)]
    return blocks + [("out", c) for c in range(D // COLS)]


def last_use(kind, c):
    if kind == "in":
        return ("u", 2 * c + 1) if c < 2 else ("qkv", 4 * c - 5) if c < 5 else ("gate", 2 * c - 9)
    return ("o", TT - 1, 1) if kind == "out" else ("glu", 3) if kind == "glu" else (kind, 4 * c + 3)


def build(nc, x, g_mix, w_in, q_norm, k_norm, lam_re, lam_im, log_step, b_re, b_im, c_re, c_im,
          ssm_d, w_glu, b_glu, sinks, w_ssm, w_att, w_out, g_ffn, w_rg, b_rg, w_re, b_er,
          w_eg, w_eu, w_ed, consts, out):
    banks = plan_banks()
    of = banks.of
    blocks = weight_blocks()
    block_at = {b: n for n, b in enumerate(blocks)}

    with ExitStack() as ctx:
        def sb(name, shape, dt=F32):
            return ctx.enter_context(nc.sbuf_tensor(name, [P, *shape], dt))

        def sem(name):
            return ctx.enter_context(nc.semaphore(name))

        pb = [ctx.enter_context(nc.psum_tensor(f"bank{i}", [P, 512], F32)) for i in range(8)]

        cst = sb("cst", [C_N])
        xr = sb("xr", [TT, D])
        hT = sb("hT", [KD, T])
        xs = sb("xs", [2, D])
        cw = xs[:, 0, :].rearrange("p (q r m) -> p q r m", q=4, r=2)
        ring = sb("ring", [RING, BLOCK])
        gates = sb("gates", [2 * KD, T])
        slot0 = sb("slot0", [3 * BLOCK])
        slot1 = sb("slot1", [3 * BLOCK])
        slot2 = sb("slot2", [3 * BLOCK])
        odd = sb("odd", [4, T])
        qT = sb("qT", [PAIRS, T])
        kT = sb("kT", [NKV, CHUNK + T])
        v_mid = sb("v_mid", [NC // 2 - 1, NKV * HD])
        par = sb("par", [16, ST])
        g1 = sb("g1", [KD])
        g2 = sb("g2", [KD])
        dsk = sb("dsk", [4])
        bgl = sb("bgl", [4])
        qkn = sb("qkn", [2, HD])
        snk = sb("snk", [PAIRS])
        wr = sb("wr", [KD, NR])
        brt = sb("brt", [NR])
        small = sb("small", [64])
        soft = sb("soft", [2, 8, PAIRS])
        nrm = sb("nrm", [4, TT, NH + NKV])
        bgh = sb("bgh", [4])
        rc = sb("rc", [SLOTS, 3], I32)
        to = sb("to", [SLOTS], I32)
        most = sb("most", [1], I32)

        ident = cst[:, C_ID:C_ID + P]
        tri = cst[:, C_TRI:C_TRI + P]
        ones = cst[:, C_ONE:C_ONE + P]
        tpos = cst[:, C_T:C_T + T]

        s5 = slot0[:, :].rearrange("p (n t) -> p n t", t=T)
        turn, rot = s5[:, 0], s5[:, 1]
        sin_t = [s5[:, 2], s5[:, 3]]
        cos_t = [s5[:, 4], s5[:, 5]]
        prs = [[s5[:, 6 + n] for n in range(4)], [odd[:, n] for n in range(4)]]
        st_re, st_im = s5[:, 10], s5[:, 11]
        raw_b = [slot0[:, 256 * n:256 * n + 256].rearrange("p (t h) -> p t h", h=SG) for n in range(2)]
        raw_c = [slot0[:, 512 + 256 * n:768 + 256 * n].rearrange("p (q s) -> p q s", s=NS) for n in range(2)]
        blk_b = [slot0[:, 1024 + 512 * n:1536 + 512 * n].rearrange("p (t g h) -> p t g h", g=2, h=SG)
                 for n in range(2)]
        blk_c = [slot0[:, 2048 + 512 * n:2560 + 512 * n].rearrange("p (q g s) -> p q g s", g=2, s=NS)
                 for n in range(2)]
        tmp_b = [slot0[:, 3072 + 256 * n:3328 + 256 * n].rearrange("p (t h) -> p t h", h=SG) for n in range(4)]
        qkv = slot1[:, 0:TT * QKV].rearrange("p (t c) -> p t c", c=QKV)
        kdup = slot1[:, 3072:4096].rearrange("p (t v r d) -> p t v r d", v=NKV, r=2, d=HD)
        prob = [slot1[:, 3072 + 512 * n:3584 + 512 * n].rearrange("p (h k) -> p h k", k=P) for n in range(2)]
        prT = [slot1[:, 4096 + 512 * n:4608 + 512 * n].rearrange("p (h k) -> p h k", k=P) for n in range(2)]
        sqk = slot1[:, 4096:4096 + 640]
        ropet = [slot1[:, 4736:4864], slot1[:, 4864:4928]]
        ropes = [slot1[:, 4928:5056], slot1[:, 5056:5120]]
        bw = slot1[:, 5120:6144].rearrange("p (q r s) -> p q r s", r=2, s=P)
        uT = slot2[:, 0:2048].rearrange("p (c t) -> p c t", t=T)
        yT = slot2[:, 2048:4096].rearrange("p (c t) -> p c t", t=T)
        y2 = slot2[:, 4096:6144].rearrange("p (c t) -> p c t", t=T)
        mg = gates
        sgl = xs[:, 0, :].rearrange("p (n t) -> p n t", t=T)
        mtmp = xs[:, 1, :].rearrange("p (n t) -> p n t", t=T)
        junk = qT[:, 0:2, :].rearrange("p a b -> p (a b)")
        quarter = cst[:, C_Q:C_Q + 1]
        rt = kT[:, :, :].rearrange("p a b -> p (a b)")
        lg = rt[:, 0:144].rearrange("p (t n) -> p t n", n=NR)
        goh = rt[:, 144:160].rearrange("p (t n) -> p t n", n=NGRP)
        gtm = rt[:, 160:176].rearrange("p (t n) -> p t n", n=NGRP)
        oh = [rt[:, 176 + 32 * n:208 + 32 * n].rearrange("p (t n) -> p t n", n=EPG) for n in range(2)]
        esel = rt[:, 240:272].rearrange("p (t n) -> p t n", n=EPG)
        etm = rt[:, 272:304].rearrange("p (t n) -> p t n", n=EPG)
        st4 = [rt[:, 304 + 4 * n:308 + 4 * n] for n in range(10)]
        gsel = rt[:, 352:480].rearrange("p (t g e) -> p t g e", g=NGRP, e=EPG)
        ohe = [rt[:, 480 + 128 * n:608 + 128 * n].rearrange("p (t n) -> p t n", n=NE) for n in range(2)]
        both = rt[:, 736:864].rearrange("p (t n) -> p t n", n=NE)
        place = rt[:, 864:992].rearrange("p (t n) -> p t n", n=NE)
        rec = rt[:, 992:1016].rearrange("p (t c f) -> p t c f", c=2, f=3)
        fo = odd[:, :, :].rearrange("p a b -> p (a b)")
        spot = [fo[:, 512 * c:512 * (c + 1)].rearrange("p (t r) -> p t r", r=P) for c in range(2)]
        note = [fo[:, 1024 + 384 * c:1408 + 384 * c].rearrange("p (t f e) -> p t f e", f=3, e=NE) for c in range(2)]
        gf = gates[:, :, :].rearrange("p a b -> p (a b)")
        xe = hT[:, :, :].rearrange("p a b -> p (a b)").rearrange("p (n d) -> p n d", d=D)
        xeT = gf[:, 0:2048].rearrange("p (n k c) -> p n k c", n=2, c=P)
        oe = gf[:, 2048:6144].rearrange("p (n d) -> p n d", d=D)
        hid = gf[:, 6144:6656].rearrange("p (n f) -> p n f", f=DE)
        sg = gf[:, 6656:7168].rearrange("p (n f) -> p n f", f=DE)
        hidT = gf[:, 7168:7680].rearrange("p (n j c) -> p n j c", n=2, c=P)
        lst = gf[:, 7680:8064].bitcast(I32).rearrange("p (i f) -> p i f", f=3)
        eslot = [slot0[:, :], slot1[:, :], slot2[:, :],
                 ring[:, 0:3, :].rearrange("p a b -> p (a b)")]

        hrow = nc.dram_tensor("normed_rows", (T, D), F32, kind="Internal").ap()
        yrow = nc.dram_tensor("expert_rows", (2 * T, D), F32, kind="Internal").ap()

        full = [sem(f"bank{i}_full") for i in range(8)]
        free = [sem(f"bank{i}_free") for i in range(8)]
        x_in = [sem(f"x_in{t}") for t in range(TT)]
        cst_in, par_in, bc_in = sem("cst_in"), sem("par_in"), sem("bc_in")
        gain_in, late_in = sem("gain_in"), sem("late_in")
        ring_in = [sem(f"ring{s}_loaded") for s in range(RING)]
        act_order, dve_order, pool_order = sem("act_order"), sem("dve_order"), sem("pool_order")
        ssq_done, rstd_done, xs_done = sem("ssq_done"), sem("rstd_done"), sem("xs_done")
        par_turn, par_trig = sem("par_turn"), sem("par_trig")
        blk_done = sem("blk_done")
        turns, whole, rot_done, cs_done = sem("turns"), sem("whole_turns"), sem("rot_done"), sem("cs_done")
        prod_done, in_done = sem("rotated_products"), sem("rotated_inputs")
        out_prod, st_done, st_used = sem("state_products"), sem("states_done"), sem("states_used")
        sq_done, sum_done, qk_rstd = sem("qk_squares"), sem("qk_sums"), sem("qk_rstd")
        qk_scaled, qk_done = sem("qk_scaled"), sem("qk_normed")
        v_moved = sem("v_moved")
        y_act = sem("y_activated")
        m_done, p_exp, p_done = sem("max_done"), sem("probs_exp"), sem("probs_done")
        y2_done, mg_done = sem("glu_done"), sem("merged_done")
        ssq2_done, rstd2_done, xs2_done = sem("ssq2"), sem("rstd2"), sem("xs2_done")
        row_out = [sem(f"row{n}_stored") for n in range(2)]
        kt_zero = sem("kt_zero")
        dexp_in, dexp_out = sem("router_exp_in"), sem("router_exp_out")
        both_done, spot_done, most_done = sem("both_done"), sem("spots_done"), sem("most_done")
        list_full, list_set = sem("list_full"), sem("list_set")
        gu_in = [sem(f"gate_up{s}_loaded") for s in range(SLOTS)]
        dn_in = [sem(f"down{s}_loaded") for s in range(SLOTS)]
        rc_ready, to_ready, dma_begun = sem("record_ready"), sem("result_row_ready"), sem("indirect_dma_begun")
        xe_in = [sem(f"xe{n}_gathered") for n in range(SLOTS)]
        xt_full, xt_out = sem("xt_full"), sem("xt_out")
        gu_done, silu_done, hid_done = sem("gate_up_done"), sem("silu_done"), sem("hid_done")
        ht_full, ht_out, dn_done = sem("hidT_full"), sem("hidT_out"), sem("down_done")
        oe_act, oe_dve = sem("oe_act"), sem("oe_dve")
        sc_done = [sem(f"rows{n}_scattered") for n in range(SLOTS)]
        moe_done, y_in, out_ready, stored = sem("moe_done"), [sem(f"y_in{t}") for t in range(TT)], \
            sem("out_ready"), sem("stored")

        bc = [(raw_b[n], src.rearrange("(t g) s h -> (g s) t h", g=2)) for n, src in enumerate((b_re, b_im))]
        bc += [(raw_c[n], src.rearrange("(q g) h s -> (g h) q s", q=4)) for n, src in enumerate((c_re, c_im))]
        late = [(dsk[:, :], ssm_d.rearrange("(q g) h -> (g h) q", q=4)),
                (bgl[:, :], b_glu.rearrange("(q p) -> p q", p=P)),
                (g2[:, :], g_ffn.rearrange("(p k) -> p k", k=KD)),
                (qkn[:, 0, :], q_norm.unsqueeze(0).broadcast_to([P, HD])),
                (qkn[:, 1, :], k_norm.unsqueeze(0).broadcast_to([P, HD])),
                (snk[0:HD, :], sinks.rearrange("(a b) -> b a", b=2)[0:1, :].broadcast_to([HD, PAIRS])),
                (snk[HD:P, :], sinks.rearrange("(a b) -> b a", b=2)[1:2, :].broadcast_to([HD, PAIRS])),
                (wr[:, :, 0:NGRP], w_rg.rearrange("(p k) g -> p k g", k=KD)),
                (brt[:, 0:NGRP], b_rg.unsqueeze(0).broadcast_to([P, NGRP])),
                (brt[:, NGRP:NR], b_er.rearrange("(a g) e -> a (g e)", a=1).broadcast_to([P, NE]))]
        late += [(wr[:, :, NGRP + EPG * g:NGRP + EPG * (g + 1)],
                  w_re[g].rearrange("(p k) e -> p k e", k=KD)) for g in range(NGRP)]
        tb, gu, hb, ob = pb[0:2], pb[2:4], pb[4], pb[6:8]

        block = ctx.enter_context(nc.Block())

        def read_out(eng, key):
            b, n = of[key]
            eng.wait_ge(free[b], n + 1)

        def filled(eng, key):
            b, n = of[key]
            eng.wait_ge(full[b], n + 1)
            return pb[b]

        def states_read(eng, t):
            if t % 4 == 3:
                filled(eng, ("y", t // 4))
            else:
                eng.wait_ge(st_used, t + 1 - (t + 1) // 4)

        def wait(eng, s, value):
            if not isinstance(value, int) or value > 0:
                eng.wait_ge(s, value)

        def expert_steps(eng, step):
            for j in range(1, 5):
                step(j // 4, j % 4)
            with eng.Fori(0, TILES // 4 - 2) as r:
                for j in range(5, 9):
                    step(r + j // 4, j % 4)
            for j in range(TILES - 3, TILES):
                step(j // 4, j % 4)

        def overflow(eng, step, lists=None):
            eng.wait_ge(most_done, 1)
            count = eng.value_load(most[0:1, 0:1], min_val=0, max_val=T)
            for first, end in ((1, 2), (2, T // ROWS)):
                with eng.If(count > first * ROWS):
                    for q in range(first, end) if lists else ():
                        lists(q)
                    with eng.Fori(first, end) as q:
                        with eng.Fori(0, TILES // 4) as r:
                            for u in range(4):
                                step(q * (TILES // 4) + r, u, r * 4 + u)

        def slots_of(u):
            return u % 2 * 2, u % 2 * 2 + 1

        @block.sync
        def _(sp):
            for tt in range(TT):
                sp.dma_start(xr[:, tt, :], x[0, tt * P:(tt + 1) * P, :]).then_inc(x_in[tt], 16)
            w_rows = w_in.rearrange("(p k) n -> p k n", k=KD)
            o_rows = w_out.rearrange("(k p) n -> p k n", p=P)
            eg = w_eg.rearrange("g e (p k) f -> (g e) p (k f)", k=KD)
            eu = w_eu.rearrange("g e (p k) f -> (g e) p (k f)", k=KD)
            ed = w_ed.rearrange("g e (p j) d -> (g e) p (j d)", j=2)

            def gate_and_up(n, u, s, e):
                wait(sp, gu_done, n * 4 + u - 1)
                sp.dma_start(eslot[s][:, 0:BLOCK], eg[e]).then_inc(gu_in[s], 16)
                sp.dma_start(eslot[s][:, BLOCK:2 * BLOCK], eu[e]).then_inc(gu_in[s], 16)

            def down_weights(n, u, s, e):
                wait(sp, dn_done, n * 4 + u - 1)
                sp.dma_start(eslot[s][:, 2 * BLOCK:], ed[e]).then_inc(dn_in[s], 16)

            def weights(n, u, j):
                for load in (gate_and_up, down_weights):
                    for h, s in enumerate(slots_of(u)):
                        load(n, u, s, j * 2 + h)

            for n, (kind, c) in enumerate(blocks):
                if n in (2, RING):
                    with nc.allow_non_contiguous_dma("small parameters"):
                        for dst, src in bc if n == 2 else late:
                            sp.dma_start(dst, src).then_inc(bc_in if n == 2 else late_in, 16)
                s = n % RING
                if n >= RING:
                    filled(sp, last_use(*blocks[n - RING]))
                if kind == "in":
                    src = w_rows[:, :, c * COLS:(c + 1) * COLS]
                elif kind == "out":
                    src = o_rows[:, :, c * COLS:(c + 1) * COLS]
                else:
                    w = {"glu": w_glu, "ssm": w_ssm, "att": w_att}[kind]
                    src = w.rearrange("(k p) n -> p k n", p=P)[:, :, c * 512:(c + 1) * 512]
                dst = ring[:, s, :].rearrange("p (k n) -> p k n", k=src.shape[1])
                sp.dma_start(dst, src).then_inc(ring_in[s], 16)
            sp.wait_ge(mg_done, KD)
            weights(0, 0, 0)
            gate_and_up(0, 1, 2, 2)
            down_weights(0, 1, 2, 2)
            filled(sp, ("o", TT - 1, 1))
            gate_and_up(0, 1, 3, 3)
            down_weights(0, 1, 3, 3)
            for u in (2, 3):
                weights(0, u, u)
            with sp.Fori(1, TILES // 4) as r:
                for u in range(4):
                    weights(r, u, r * 4 + u)
            overflow(sp, weights)
            sp.wait_ge(moe_done, 1)
            ys = [slot0[:, 2048 * t:2048 * (t + 1)] for t in range(3)] + [slot1[:, 0:2048]]
            for tt in range(TT):
                sp.dma_start(ys[tt].rearrange("p (c d) -> p c d", c=2),
                             yrow.rearrange("(c t p) d -> t p c d", c=2, p=P)[tt]).then_inc(y_in[tt], 16)
            for tt in range(TT):
                sp.wait_ge(out_ready, tt + 1)
                sp.dma_start(out[0, tt * P:(tt + 1) * P, :], xr[:, tt, :]).then_inc(stored, 16)
            sp.wait_ge(stored, 16 * TT)

        @block.gpsimd
        def _(pool):
            order = Order(pool, pool_order)
            pool.memset(kT[:, :, 0:CHUNK], 0.0).then_inc(kt_zero, 1)
            for t in range(ST):
                pr = prs[t % 2]
                pool.wait_ge(prod_done, t + 1)
                pool.tensor_tensor(pr[0], pr[0], pr[1], ALU.add).then_inc(in_done, 1)
                read_out(pool, ("bu", t, 1))
                pool.tensor_tensor(pr[2], pr[2], pr[3], ALU.subtract).then_inc(in_done, 1)
                pool.wait_ge(out_prod, 2 * t + 1)
                if t:
                    states_read(pool, t - 1)
                pool.tensor_tensor(st_re, pr[0], pr[2], ALU.subtract).then_inc(st_done, 1)
                pool.wait_ge(out_prod, 2 * t + 2)
                pool.tensor_tensor(st_im, pr[1], pr[3], ALU.add).then_inc(st_done, 1)

            pool.wait_ge(list_set, 1)
            for n in range(2):
                pool.wait_ge(row_out[n], 32)

            last_token, last_result = pool.to_reg(T - 1), pool.to_reg(2 * T - 1)

            def gather(n, u):
                i = n * 4 + u
                wait(pool, xe_in[u], n * 16)
                wait(pool, hid_done, i - 3)
                pool.tensor_copy(rc[:, u, :], lst[:, i, :] if isinstance(i, int) else
                                 lst[:, bass.ds(i, 1), :].rearrange("p a f -> p (a f)")).then_inc(rc_ready, 1)
                pool.wait_ge(rc_ready, i + 1)
                wait(pool, xt_full, i - 3)
                pool.sem_inc(dma_begun, 1)
                pool.indirect_dma_start(xe[:, u, :], None, hrow, bass.IndirectOffsetOnAxis(rc[:, u, 0:1], 0),
                                        bounds_check=last_token, oob_is_err=False).then_inc(xe_in[u], 16)

            def scatter(n, u):
                i = n * 4 + u
                wait(pool, sc_done[u], n * 16)
                pool.tensor_copy(to[:, u:u + 1], lst[:, i, 1:2] if isinstance(i, int) else
                                 lst[:, bass.ds(i, 1), 1:2].rearrange("p a f -> p (a f)")).then_inc(to_ready, 1)
                pool.wait_ge(to_ready, i + 1)
                pool.wait_ge(oe_act, i + 1)
                pool.wait_ge(oe_dve, i + 1)
                pool.sem_inc(dma_begun, 1)
                pool.indirect_dma_start(yrow, bass.IndirectOffsetOnAxis(to[:, u:u + 1], 0), oe[:, u, :], None,
                                        bounds_check=last_result, oob_is_err=False).then_inc(sc_done[u], 16)

            def step(n, u):
                if not (isinstance(n, int) and n * 4 + u + 3 >= TILES):
                    gather(n + (u + 3) // 4, (u + 3) % 4)
                scatter(n if u else n - 1, (u - 1) % 4)

            gather(0, 0)
            gather(0, 1)
            gather(0, 2)
            gather(0, 3)
            expert_steps(pool, step)
            scatter(TILES // 4 - 1, 3)
            for u in range(SLOTS):
                pool.wait_ge(sc_done[u], 16 * TILES // 4)

            def more(n, u, j):
                gather(n, u)
                scatter(n, u)
                pool.wait_ge(sc_done[u], (n + 1) * 16)

            def lists(q):
                pool.wait_ge(list_set, q + 1)

            overflow(pool, more, lists)
            pool.sem_inc(moe_done, 1)

        @block.scalar
        def _(act):
            order = Order(act, act_order)

            def evac(key, dst, src, func=ACT.Copy, **kw):
                b, n = of[key]
                act.wait_ge(full[b], n + 1)
                act.activation(dst, src, func, **kw).then_inc(free[b], 1)

            act.dma_start(cst[:, :], consts).then_inc(cst_in, 16)
            with nc.allow_non_contiguous_dma("small parameters"):
                for n, src in enumerate((lam_re, lam_im)):
                    act.dma_start(par[:, n, :], src.rearrange("(t g) s -> (g s) t", g=2)).then_inc(par_in, 16)
                for g in range(2):
                    act.dma_start(par[g * NS:(g + 1) * NS, 2, :],
                                  log_step.rearrange("(t g) -> g t", g=2)[g:g + 1, :].broadcast_to([NS, ST])
                                  ).then_inc(par_in, 16)
                act.dma_start(g1[:, :], g_mix.rearrange("(p k) -> p k", k=KD)).then_inc(gain_in, 16)

            for tt in range(TT):
                act.wait_ge(x_in[tt], 16)
                act.activation(hT[:, 2 * tt:2 * tt + 2, :].rearrange("p a b -> p (a b)"), xr[:, tt, :],
                               ACT.Square, accum_out=small[:, tt:tt + 1]).then_inc(ssq_done, 1)
            act.wait_ge(rstd_done, 1)
            for tt in range(TT):
                if tt >= 2:
                    for half in range(2):
                        filled(act, ("xT", tt - 2, half))
                act.activation(xs[:, tt % 2, :], xr[:, tt, :], ACT.Copy,
                               scale=small[:, 8 + tt:9 + tt]).then_inc(xs_done, 1)
            act.wait_ge(cst_in, 16)
            act.wait_ge(par_turn, 1)
            act.activation(par[:, 9, :], par[:, 7, :], ACT.Sin, scale=TWO_PI)
            order.link(act.activation(par[:, 7, :], par[:, 7, :], ACT.Abs))
            act.activation(par[:, 10, :], par[:, 7, :], ACT.Sin, scale=-TWO_PI, bias=quarter).then_inc(par_trig, 1)
            for c in range(4):
                evac(("u", c), uT[:, c, :], pb[of[("u", c)][0]][:, :])
            for ri in range(2):
                evac(("bT", ri), bw[:, :, ri, :], pb[of[("bT", ri)][0]][:, :].rearrange("p (q s) -> p q s", s=P))
            for tt in (2, 3):
                for half in range(2):
                    filled(act, ("xT", tt, half))
            for ri in range(2):
                evac(("cT", ri), cw[:, :, ri, :], pb[of[("cT", ri)][0]][:, :].rearrange("p (q s) -> p q s", s=P))

            def whole_turns(t):
                act.wait_ge(turns, t + 1)
                act.activation(turn, turn, ACT.Copy, bias=-MAGIC).then_inc(whole, 1)

            def table(t):
                act.wait_ge(rot_done, t + 1)
                if t >= 2:
                    act.wait_ge(out_prod, 2 * (t - 2) + 2)
                act.activation(sin_t[t % 2], rot, ACT.Sin, scale=TWO_PI)
                order.link(act.activation(rot, rot, ACT.Abs))
                act.activation(cos_t[t % 2], rot, ACT.Sin, scale=-TWO_PI, bias=quarter).then_inc(cs_done, 1)

            def dense(key):
                b = pb[of[key][0]]
                if key[0] == "qkv":
                    blk, tt = divmod(key[1], TT)
                    evac(key, qkv[:, tt, blk * COLS:(blk + 1) * COLS], b[:, 0:COLS])
                else:
                    evac(key, gates[:, key[1], :], b[:, :], ACT.Tanh, scale=0.5)

            whole_turns(0)
            table(0)
            whole_turns(1)
            for t in range(ST):
                if t + 1 < ST:
                    table(t + 1)
                if t + 2 < ST:
                    whole_turns(t + 2)
                for w in slot_work(t):
                    dense(w)
                if t == 4:
                    for n in range(4):
                        read_out(act, ("qkv", 8 + n))
                    for h in range(2):
                        act.dma_start(v_mid[h * CHUNK:(h + 1) * CHUNK, :, :],
                                      qkv[(1 - h) * CHUNK:(2 - h) * CHUNK, h:h + 3, 640:768]).then_inc(v_moved, 16)
                if 4 <= t < 8:
                    if t > 4:
                        act.wait_ge(sum_done, t - 4)
                    act.activation(sqk, qkv[:, t - 4, 0:640], ACT.Square).then_inc(sq_done, 1)
                if 10 <= t < 14:
                    if t == 10:
                        act.wait_ge(qk_rstd, 1)
                    for h in range(NH + NKV):
                        head = qkv[:, t - 10, h * HD:(h + 1) * HD]
                        ins = act.activation(head, head, ACT.Copy, scale=nrm[:, 2, t - 10, h:h + 1])
                    ins.then_inc(qk_scaled, 1)
            for tt in range(TT):
                evac(("qT", tt), qT[:, :, tt * P:(tt + 1) * P],
                     pb[of[("qT", tt)][0]][:, :].rearrange("p (h t) -> p h t", t=P))
                evac(("kT", tt), kT[:, :, CHUNK + tt * P:CHUNK + (tt + 1) * P],
                     pb[of[("kT", tt)][0]][:, 0:NKV * P].rearrange("p (h t) -> p h t", t=P))

            def exps(c):
                lo = CHUNK if c == 0 else 0
                b, n = of[("score", c)]
                z = soft[:, c % 2]
                act.wait_ge(m_done, c + 1)
                if c >= 2:
                    filled(act, ("pT", c - 2))
                s = pb[b][:, :].rearrange("p (h k) -> p h k", k=P)
                for h in range(PAIRS):
                    ins = act.activation(prob[c % 2][:, h, lo:P], s[:, h, lo:P], ACT.Exp, scale=HD ** -0.5,
                                         bias=z[:, 2, h:h + 1], accum_out=z[:, 3, h:h + 1])
                ins.then_inc(free[b], 1)
                act.activation(z[:, 4, :], z[:, 5, :], ACT.Exp).then_inc(p_exp, 1)

            exps(0)
            for c in range(NC):
                lo = CHUNK if c == 0 else 0
                if c + 1 < NC:
                    exps(c + 1)
                if c % 2 == 0:
                    dense(("gate", 12 + c // 2))
                if c >= 2:
                    filled(act, ("pv", c - 2))
                evac(("pT", c), prT[c % 2][0:P - lo, :, :],
                     pb[of[("pT", c)][0]][0:P - lo, :].rearrange("p (h k) -> p h k", k=P))
            for q in range(4):
                read_out(act, ("y", q))
                order.link(act.activation(yT[:, q, :], yT[:, q, :], ACT.Gelu_apprx_tanh))
                act.activation(y2[:, q, :], yT[:, q, :], ACT.Copy, scale=0.5).then_inc(y_act, 1)
            for j in range(4):
                if j >= 2:
                    act.wait_ge(y2_done, j - 1)
                evac(("glu", j), sgl[:, j % 2, :], pb[of[("glu", j)][0]][:, :], ACT.Tanh, scale=0.5,
                     bias=bgh[:, j:j + 1])
            act.wait_ge(mg_done, KD)
            for tt in range(TT):
                read_out(act, ("o", tt, 1))
                act.activation(junk, xr[:, tt, :], ACT.Square, accum_out=small[:, 24 + tt:25 + tt]).then_inc(ssq2_done, 1)
                act.wait_ge(rstd2_done, tt + 1)
                if tt >= 2:
                    act.wait_ge(row_out[tt % 2], 16)
                act.activation(xs[:, tt % 2, :], xr[:, tt, :], ACT.Copy,
                               scale=small[:, 32 + tt:33 + tt]).then_inc(xs2_done, 1)
                act.wait_ge(xs2_done, tt + 1)
                act.dma_start(hrow[tt * P:(tt + 1) * P, :], xs[:, tt % 2, :]).then_inc(row_out[tt % 2], 16)
            act.wait_ge(dexp_in, 1)
            act.activation(gtm, gtm, ACT.Exp)
            act.activation(st4[6], st4[6], ACT.Exp).then_inc(dexp_out, 1)

            def silu(n, u):
                i = n * 4 + u
                act.wait_ge(gu_done, i + 1)
                wait(act, hid_done, i - 1)
                act.activation(sg[:, u % 2, :], gu[u % 2][:, 0:DE], ACT.Silu).then_inc(silu_done, 1)

            def hidT_out(n, u):
                i = n * 4 + u
                act.wait_ge(ht_full, i + 1)
                wait(act, dn_done, i - 1)
                act.activation(hidT[:, u % 2, :, :], hb[:, 0:DE].rearrange("p (j c) -> p j c", c=P),
                               ACT.Copy).then_inc(ht_out, 1)

            def half_out(n, u):
                i = n * 4 + u
                act.wait_ge(dn_done, i + 1)
                wait(act, sc_done[u], n * 16)
                act.activation(oe[:, u, 512:D], ob[1][:, :], ACT.Copy).then_inc(oe_act, 1)

            def step(n, u):
                p, v = (n, u - 1) if u else (n - 1, 3)
                hidT_out(p, v)
                silu(n, u)
                half_out(p, v)

            silu(0, 0)
            expert_steps(act, step)
            hidT_out(TILES // 4 - 1, 3)
            half_out(TILES // 4 - 1, 3)

            def more(n, u, j):
                silu(n, u)
                hidT_out(n, u)
                half_out(n, u)

            overflow(act, more)

        @block.vector
        def _(dve):
            order = Order(dve, dve_order)
            link, mark = order.link, order.mark

            def rsqrt(y, v, t, done=None):
                link(dve.tensor_scalar(y.bitcast(I32), v.bitcast(I32), -0.5, 1597463007.0, ALU.mult, ALU.add))
                for n in range(3):
                    link(dve.tensor_tensor(t, y, y, ALU.mult))
                    link(dve.scalar_tensor_tensor(t, t, -0.5, v, ALU.mult, ALU.mult))
                    ins = dve.scalar_tensor_tensor(y, t, 1.5, y, ALU.add, ALU.mult)
                    if n == 2 and done is not None:
                        ins.then_inc(done, 1)
                    else:
                        link(ins)

            def exp(y, v, n, r, w):
                link(dve.tensor_scalar(v, v, -87.0, 88.0, ALU.max, ALU.min))
                link(dve.tensor_scalar(n, v, 1.4426950408889634, MAGIC, ALU.mult, ALU.add))
                link(dve.tensor_scalar(n, n, -MAGIC, None, ALU.add))
                link(dve.scalar_tensor_tensor(r, n, -LN2_HI, v, ALU.mult, ALU.add))
                link(dve.scalar_tensor_tensor(r, n, -LN2_LO, r, ALU.mult, ALU.add))
                link(dve.tensor_scalar(y, r, 1 / 5040, None, ALU.mult))
                for k in (720, 120, 24, 6, 2, 1):
                    link(dve.scalar_tensor_tensor(y, y, 1 / k, r, ALU.add, ALU.mult))
                link(dve.tensor_scalar(w.bitcast(I32), n, 127.0, 8388608.0, ALU.add, ALU.mult))
                link(dve.scalar_tensor_tensor(y, y, 1.0, w, ALU.add, ALU.mult))

            dve.wait_ge(ssq_done, TT)
            link(dve.tensor_scalar(small[:, 16:20], small[:, 0:4], 1.0 / D, EPS, ALU.mult, ALU.add))
            rsqrt(small[:, 8:12], small[:, 16:20], small[:, 20:24], rstd_done)

            def rows_out(kind, tt, half, g):
                src = filled(dve, (kind, tt, half))[:, :].rearrange("p (k t) -> p k t", t=P)
                ks = slice(4 * half, 4 * half + 4)
                dve.tensor_tensor(hT[:, ks, tt * P:(tt + 1) * P], src,
                                  g[:, ks].unsqueeze(2).broadcast_to([P, 4, P]), ALU.mult
                                  ).then_inc(free[of[(kind, tt, half)][0]], 1)

            dve.wait_ge(gain_in, 16)
            for tt in range(TT):
                for half in range(2):
                    rows_out("xT", tt, half, g1)

            lr, li, step_, mag, cyc, t1, t2, t3, cs, sn = (par[:, n, :] for n in (0, 1, 3, 4, 5, 6, 7, 8, 10, 9))
            ar, ai, den, fr, fi = (par[:, n, :] for n in range(11, 16))
            dve.wait_ge(par_in, 64)
            exp(step_, par[:, 2, :], t1, t2, t3)
            link(dve.tensor_tensor(sn, lr, step_, ALU.mult))
            exp(mag, sn, t1, t2, t3)
            link(dve.tensor_tensor(cyc, li, step_, ALU.mult))
            link(dve.tensor_scalar(cyc, cyc, 0.15915494309189535, None, ALU.mult))
            link(dve.tensor_scalar(t1, cyc, MAGIC, None, ALU.add))
            link(dve.tensor_scalar(t1, t1, -MAGIC, None, ALU.add))
            dve.tensor_tensor(t2, cyc, t1, ALU.subtract).then_inc(par_turn, 1)

            dve.wait_ge(par_trig, 1)
            mark(dve.tensor_tensor(ar, mag, cs, ALU.mult))
            link(dve.tensor_tensor(ai, mag, sn, ALU.mult))
            mark(dve.tensor_tensor(t1, lr, lr, ALU.mult))
            mark(dve.tensor_tensor(t2, li, li, ALU.mult))
            link(dve.tensor_scalar(ar, ar, -1.0, None, ALU.add))
            link(dve.tensor_tensor(den, t1, t2, ALU.add))
            mark(dve.reciprocal(den, den))
            mark(dve.tensor_tensor(t1, ar, lr, ALU.mult))
            mark(dve.tensor_tensor(t2, ai, li, ALU.mult))
            mark(dve.tensor_tensor(t3, ai, lr, ALU.mult))
            link(dve.tensor_tensor(sn, ar, li, ALU.mult))
            mark(dve.tensor_tensor(fr, t1, t2, ALU.add))
            link(dve.tensor_tensor(fi, t3, sn, ALU.subtract))
            mark(dve.tensor_tensor(fr, fr, den, ALU.mult))
            mark(dve.tensor_tensor(fi, fi, den, ALU.mult))
            dve.memset(blk_b[0], 0.0)
            link(dve.memset(blk_b[1], 0.0))
            dve.wait_ge(bc_in, 64)
            fr3, fi3 = (f.unsqueeze(2).broadcast_to([P, ST, SG]) for f in (fr, fi))
            mark(dve.tensor_tensor(tmp_b[0], raw_b[0], fr3, ALU.mult))
            mark(dve.tensor_tensor(tmp_b[1], raw_b[1], fi3, ALU.mult))
            mark(dve.tensor_tensor(tmp_b[2], raw_b[1], fr3, ALU.mult))
            link(dve.tensor_tensor(tmp_b[3], raw_b[0], fi3, ALU.mult))
            for g in range(2):
                h = slice(g * NS, (g + 1) * NS)
                dve.tensor_tensor(blk_b[0][h, :, g, :], tmp_b[0][h], tmp_b[1][h], ALU.subtract)
                dve.tensor_tensor(blk_b[1][h, :, g, :], tmp_b[2][h], tmp_b[3][h], ALU.add)
            dve.wait_ge(cst_in, 16)
            for g in range(2):
                for n in range(2):
                    ins = dve.tensor_scalar(blk_c[n][:, :, g, :], raw_c[n],
                                            cst[:, C_GL + 2 * n + g:C_GL + 2 * n + g + 1], None, ALU.mult)
            ins.then_inc(blk_done, 1)

            def turns_of(t):
                if t == 0:
                    dve.wait_ge(blk_done, 1)
                else:
                    dve.wait_ge(rot_done, t)

                dve.tensor_scalar(turn, tpos, cyc[:, t:t + 1], MAGIC, ALU.mult, ALU.add).then_inc(turns, 1)

            def rot_of(t):
                dve.wait_ge(whole, t + 1)
                wait(dve, cs_done, t)
                dve.scalar_tensor_tensor(rot, tpos, cyc[:, t:t + 1], turn, ALU.mult, ALU.subtract).then_inc(rot_done, 1)

            def y_of(q):
                src = filled(dve, ("y", q))
                dve.scalar_tensor_tensor(yT[:, q, :], uT[:, q, :], dsk[:, q:q + 1], src[:, :], ALU.mult, ALU.add
                                         ).then_inc(free[4], 1)

            def qk_sums(tt):
                dve.wait_ge(sq_done, tt + 1)
                dve.tensor_reduce(nrm[:, 0, tt, :], sqk.rearrange("p (h d) -> p h d", d=HD), AX.X, ALU.add
                                  ).then_inc(sum_done, 1)

            def qk_rms():
                dve.wait_ge(sum_done, TT)
                link(dve.tensor_scalar(nrm[:, 1], nrm[:, 0], 1.0 / HD, EPS, ALU.mult, ALU.add))
                rsqrt(nrm[:, 2], nrm[:, 1], nrm[:, 3], qk_rstd)

            def qk_norm(tt):
                dve.wait_ge(qk_scaled, tt + 1)
                qk = qkv[:, tt, 0:640].rearrange("p (h d) -> p h d", d=HD)
                q = qk[:, 0:NH, :]
                mark(dve.tensor_tensor(q, q, qkn[:, 0:1, :].broadcast_to([P, NH, HD]), ALU.mult))
                kd = kdup[:, tt]
                for r in range(2):
                    ins = dve.tensor_tensor(kd[:, :, r, :], qk[:, NH:, :], qkn[:, 1:2, :].broadcast_to([P, NKV, HD]),
                                            ALU.mult)
                link(ins)
                cos, sin = (cst[:, C_ROPE + 32 * tt + 16 * n:C_ROPE + 32 * tt + 16 * n + 16] for n in range(2))
                kf = kd.rearrange("p v r d -> p (v r) d")
                for a, h, n in ((q, NH, 0), (kf, 2 * NKV, 1)):
                    ta = ropet[n].rearrange("p (h c) -> p h c", c=16)
                    tb = ropes[n].rearrange("p (h c) -> p h c", c=16)
                    dve.tensor_tensor(ta, a[:, :, 0:16], cos.unsqueeze(1).broadcast_to([P, h, 16]), ALU.mult)
                    dve.tensor_tensor(tb[:, :, 0:8], a[:, :, 8:16], sin[:, 0:8].unsqueeze(1).broadcast_to([P, h, 8]), ALU.mult)
                    link(dve.tensor_tensor(tb[:, :, 8:16], a[:, :, 0:8], sin[:, 8:16].unsqueeze(1).broadcast_to([P, h, 8]), ALU.mult))
                    ins = dve.tensor_tensor(a[:, :, 0:16], ta, tb, ALU.add)
                ins.then_inc(qk_done, 1)

            dve.wait_ge(late_in, 16 * len(late))
            dve.tensor_scalar(bgh[:, :], bgl[:, :], 0.5, None, ALU.mult)
            turns_of(0)
            rot_of(0)
            turns_of(1)
            for t in range(ST):
                si, co = sin_t[t % 2], cos_t[t % 2]
                pr = prs[t % 2]
                br = filled(dve, ("bu", t, 0))
                bi = filled(dve, ("bu", t, 1))
                dve.wait_ge(cs_done, t + 1)
                if t >= 2:
                    dve.wait_ge(st_done, 2 * t - 2)
                dve.tensor_tensor(pr[0], br[:, :], co, ALU.mult)
                dve.tensor_tensor(pr[1], bi[:, :], si, ALU.mult).then_inc(prod_done, 1)
                dve.tensor_tensor(pr[3], br[:, :], si, ALU.mult).then_inc(free[of[("bu", t, 0)][0]], 1)
                dve.tensor_tensor(pr[2], bi[:, :], co, ALU.mult).then_inc(free[of[("bu", t, 1)][0]], 1)
                if t + 1 < ST:
                    rot_of(t + 1)
                if 5 <= t < 9:
                    qk_sums(t - 5)
                decay = mag[:, t:t + 1].broadcast_to([P, T])
                dve.wait_ge(in_done, 2 * t + 1)
                z_re = mark(dve.tensor_tensor_scan(pr[1], decay, pr[0], 0.0, ALU.mult, ALU.add))
                if t + 2 < ST:
                    turns_of(t + 2)
                dve.wait_ge(in_done, 2 * t + 2)
                z_im = mark(dve.tensor_tensor_scan(pr[3], decay, pr[2], 0.0, ALU.mult, ALU.add))
                order.wait(z_re)
                dve.tensor_tensor(pr[0], pr[1], co, ALU.mult)
                order.wait(z_im)
                dve.tensor_tensor(pr[2], pr[3], si, ALU.mult).then_inc(out_prod, 1)
                dve.wait_ge(out_prod, 2 * t + 1)
                dve.tensor_tensor(pr[1], pr[1], si, ALU.mult)
                dve.tensor_tensor(pr[3], pr[3], co, ALU.mult).then_inc(out_prod, 1)
                if t == 9:
                    qk_rms()
                if 11 <= t < 15:
                    qk_norm(t - 11)
                if t % 4 == 1 and t > 4:
                    y_of((t - 5) // 4)
            y_of(3)

            def maxima(c):
                lo = CHUNK if c == 0 else 0
                z = soft[:, c % 2]
                s = filled(dve, ("score", c))[:, :].rearrange("p (h k) -> p h k", k=P)
                link(dve.tensor_reduce(z[:, 0, :], s[:, :, lo:P], AX.X, ALU.max))
                link(dve.scalar_tensor_tensor(z[:, 1, :], z[:, 0, :], HD ** -0.5, snk[:, :], ALU.mult, ALU.max))
                dve.tensor_scalar(z[:, 2, :], z[:, 1, :], -1.0, None, ALU.mult)
                dve.tensor_tensor(z[:, 5, :], snk[:, :], z[:, 1, :], ALU.subtract).then_inc(m_done, 1)

            def normalise(c):
                lo = CHUNK if c == 0 else 0
                z = soft[:, c % 2]
                dve.wait_ge(p_exp, c + 1)
                link(dve.tensor_tensor(z[:, 6, :], z[:, 3, :], z[:, 4, :], ALU.add))
                link(dve.reciprocal(z[:, 7, :], z[:, 6, :]))
                pc = prob[c % 2][:, :, lo:P]
                dve.tensor_tensor(pc, pc, z[:, 7, :].unsqueeze(2).broadcast_to([P, PAIRS, P - lo]), ALU.mult
                                  ).then_inc(p_done, 1)

            def attended(c):
                src = filled(dve, ("pv", c))
                dve.tensor_copy(qT[:, :, c * CHUNK:(c + 1) * CHUNK],
                                src[:, 0:PAIRS * CHUNK].rearrange("p (h t) -> p h t", t=CHUNK)).then_inc(free[4], 1)

            maxima(0)
            for c in range(NC):
                if c + 1 < NC:
                    maxima(c + 1)
                normalise(c)
                if c:
                    attended(c - 1)
            attended(NC - 1)

            for j in range(4):
                read_out(dve, ("glu", j))
                dve.scalar_tensor_tensor(y2[:, j, :], sgl[:, j % 2, :], 1.0, y2[:, j, :], ALU.add, ALU.mult
                                         ).then_inc(y2_done, 1)
            for j in range(KD):
                src = filled(dve, ("ssm", j))
                dve.scalar_tensor_tensor(mg[:, j, :], gates[:, j, :], 1.0, src[:, :], ALU.add, ALU.mult
                                         ).then_inc(free[of[("ssm", j)][0]], 1)
                src = filled(dve, ("att", j))
                dve.scalar_tensor_tensor(mtmp[:, j % 2, :], gates[:, KD + j, :], 1.0, src[:, :], ALU.add, ALU.mult
                                         ).then_inc(free[of[("att", j)][0]], 1)
                read_out(dve, ("att", j))
                dve.tensor_tensor(mg[:, j, :], mg[:, j, :], mtmp[:, j % 2, :], ALU.add).then_inc(mg_done, 1)

            def residual(tt):
                for half in range(2):
                    src = filled(dve, ("o", tt, half))
                    xh = xr[:, tt, half * 512:(half + 1) * 512]
                    dve.scalar_tensor_tensor(xh, src[:, :], 0.5, xh, ALU.mult, ALU.add
                                             ).then_inc(free[of[("o", tt, half)][0]], 1)

            def rms(tt):
                dve.wait_ge(ssq2_done, tt + 1)
                v = small[:, 40 + tt:41 + tt]
                link(dve.tensor_scalar(v, small[:, 24 + tt:25 + tt], 1.0 / D, EPS, ALU.mult, ALU.add))
                rsqrt(small[:, 32 + tt:33 + tt], v, small[:, 44 + tt:45 + tt], rstd2_done)

            def logits(tt):
                src = filled(dve, ("logit", tt))
                dve.wait_ge(rstd2_done, tt + 1)
                dve.scalar_tensor_tensor(lg[:, tt, :], src[:, 0:NR], small[:, 32 + tt:33 + tt], brt[:, :],
                                         ALU.mult, ALU.add).then_inc(free[4], 1)

            residual(0)
            residual(1)
            for tt in range(TT):
                for half in range(2):
                    rows_out("hT", tt, half, g2)
                if tt + 2 < TT:
                    residual(tt + 2)
                    if tt == 0:
                        rms(0)
                        rms(1)
                    rms(tt + 2)
                logits(tt)
            read_out(dve, ("logit", TT - 1))

            def over(a, n):
                return a.unsqueeze(2).broadcast_to([P, TT, n])

            def first_best(v, one, tmp, iota, n, best, at):
                link(dve.tensor_reduce(best, v, AX.X, ALU.max))
                link(dve.tensor_tensor(one, v, over(best, n), ALU.is_equal))
                link(dve.scalar_tensor_tensor(tmp, one, -64.0, iota.unsqueeze(1).broadcast_to([P, TT, n]),
                                              ALU.mult, ALU.add))
                link(dve.tensor_reduce(at, tmp, AX.X, ALU.min))
                link(dve.tensor_tensor(one, tmp, over(at, n), ALU.is_equal))

            i4, i8 = cst[:, C_I4:C_I4 + NGRP], cst[:, C_I8:C_I8 + EPG]
            gl, el = lg[:, :, 0:NGRP], lg[:, :, NGRP:NR].rearrange("p t (g e) -> p t g e", e=EPG)
            first_best(gl, goh, gtm, i4, NGRP, st4[0], st4[1])
            link(dve.tensor_tensor(gtm, gl, over(st4[0], NGRP), ALU.subtract))
            link(dve.tensor_tensor(gsel, el, goh.unsqueeze(3).broadcast_to([P, TT, NGRP, EPG]), ALU.mult))
            link(dve.tensor_reduce(esel, gsel.rearrange("p t g e -> p t e g"), AX.X, ALU.add))
            first_best(esel, oh[0], etm, i8, EPG, st4[2], st4[3])
            link(dve.scalar_tensor_tensor(esel, oh[0], -3e38, esel, ALU.mult, ALU.add))
            first_best(esel, oh[1], etm, i8, EPG, st4[4], st4[5])
            dve.tensor_tensor(st4[6], st4[4], st4[2], ALU.subtract).then_inc(dexp_in, 1)
            for c in range(2):
                mark(dve.tensor_tensor(ohe[c].rearrange("p t (g e) -> p t g e", e=EPG),
                                       goh.unsqueeze(3).broadcast_to([P, TT, NGRP, EPG]),
                                       oh[c].unsqueeze(2).broadcast_to([P, TT, NGRP, EPG]), ALU.mult))
            order.wait()
            dve.tensor_tensor(both, ohe[0], ohe[1], ALU.add).then_inc(both_done, 1)
            mark(dve.tensor_copy(rec, cst[:, C_REC:C_Q].rearrange("p (t c f) -> p t c f", c=2, f=3)))
            dve.wait_ge(dexp_out, 1)
            mark(dve.tensor_reduce(st4[7], gtm, AX.X, ALU.add))
            link(dve.tensor_scalar(st4[8], st4[6], 1.0, None, ALU.add))
            link(dve.tensor_tensor(st4[7], st4[7], st4[8], ALU.mult))
            link(dve.reciprocal(st4[7], st4[7]))
            mark(dve.tensor_copy(rec[:, :, 0, 2], st4[7]))
            mark(dve.tensor_tensor(rec[:, :, 1, 2], st4[7], st4[6], ALU.mult))
            order.wait()
            for c in range(2):
                mark(dve.tensor_tensor(note[c], ohe[c].unsqueeze(2).broadcast_to([P, TT, 3, NE]),
                                       rec[:, :, c, :].unsqueeze(3).broadcast_to([P, TT, 3, NE]), ALU.mult))
            src = filled(dve, ("rank",))
            ranks = src[:, 0:TT * NE].rearrange("p (t e) -> p t e", e=NE)
            flat = gsel.rearrange("p t g e -> p t (g e)")
            mark(dve.tensor_tensor(place, ohe[0], ranks, ALU.mult))
            dve.tensor_tensor(flat, ohe[1], ranks, ALU.mult).then_inc(free[of[("rank",)][0]], 1)
            read_out(dve, ("rank",))
            order.wait()
            for c, tmp in enumerate((place, flat)):
                mark(dve.tensor_reduce(st4[8 + c], tmp, AX.X, ALU.add))
            order.wait()

            def spots(q):
                wait(dve, list_full, q)
                for c in range(2):
                    ins = dve.tensor_tensor(
                        spot[c].rearrange("p t (h r) -> p t h r", h=2),
                        tpos[:, q * ROWS:(q + 1) * ROWS].unsqueeze(1).unsqueeze(1).broadcast_to([P, TT, 2, ROWS]),
                        st4[8 + c].unsqueeze(2).unsqueeze(3).broadcast_to([P, TT, 2, ROWS]), ALU.is_equal)
                ins.then_inc(spot_done, 1)

            def entries(q):
                dve.wait_ge(list_full, q + 1)
                dst = lst[:, q * TILES:(q + 1) * TILES, :].rearrange("p j f -> p f j")
                src = pb[LIST][:, 0:3 * NE].rearrange("p (f j h) -> p f j h", f=3, h=2)
                for h in range(2):
                    r = slice(h * ROWS, (h + 1) * ROWS)
                    dve.tensor_scalar(dst[r, 0:2, :], src[r, 0:2, :, h], float(NONE), None, ALU.add)
                    ins = dve.tensor_copy(dst[r, 2, :].bitcast(F32), src[r, 2, :, h])
                ins.then_inc(list_set, 1)

            def lists(q):
                spots(q)
                entries(q)

            spots(0)
            src = filled(dve, ("count",))
            link(dve.tensor_reduce(small[0:1, 48:49], src[0:1, 0:NE], AX.X, ALU.max))
            dve.tensor_copy(most[0:1, 0:1], small[0:1, 48:49]).then_inc(most_done, 1)
            entries(0)

            def rows_turned(n, u):
                i = n * 4 + u
                dve.wait_ge(xt_full, i + 1)
                wait(dve, gu_done, i - 1)
                for half in range(2):
                    ks = slice(4 * half, 4 * half + 4)
                    ins = dve.tensor_tensor(xeT[:, u % 2, ks, :], tb[half][:, :].rearrange("p (k c) -> p k c", c=P),
                                            g2[:, ks].unsqueeze(2).broadcast_to([P, 4, P]), ALU.mult)
                ins.then_inc(xt_out, 1)

            def hidden(n, u):
                i = n * 4 + u
                dve.wait_ge(silu_done, i + 1)
                dve.wait_ge(rc_ready, i + 1)
                wait(dve, ht_full, i - 1)
                dve.scalar_tensor_tensor(hid[:, u % 2, :], gu[u % 2][:, DE:2 * DE], rc[:, u, 2:3].bitcast(F32),
                                         sg[:, u % 2, :], ALU.mult, ALU.mult).then_inc(hid_done, 1)

            def half_out(n, u):
                i = n * 4 + u
                dve.wait_ge(dn_done, i + 1)
                wait(dve, sc_done[u], n * 16)
                dve.tensor_copy(oe[:, u, 0:512], ob[0][:, :]).then_inc(oe_dve, 1)

            def step(n, u, last=False):
                if not (isinstance(n, int) and n * 4 + u + 1 >= TILES):
                    rows_turned(n + (u + 1) // 4, (u + 1) % 4)
                hidden(n, u)
                half_out(n if u else n - 1, (u - 1) % 4)

            rows_turned(0, 0)
            rows_turned(0, 1)
            hidden(0, 0)
            expert_steps(dve, step)
            half_out(TILES // 4 - 1, 3)

            def more(n, u, j):
                rows_turned(n, u)
                hidden(n, u)
                half_out(n, u)

            overflow(dve, more, lists)
            ys = [slot0[:, 2048 * t:2048 * (t + 1)] for t in range(3)] + [slot1[:, 0:2048]]
            for tt in range(TT):
                y = ys[tt].rearrange("p (c d) -> p c d", c=2)
                dve.wait_ge(y_in[tt], 16)
                link(dve.tensor_tensor(y[:, 0, :], y[:, 0, :], y[:, 1, :], ALU.add))
                dve.tensor_tensor(xr[:, tt, :], xr[:, tt, :], y[:, 0, :], ALU.add).then_inc(out_ready, 1)

        @block.tensor
        def _(pe):
            def begin(key):
                b, n = of[key]
                if n:
                    pe.wait_ge(free[b], n)
                return pb[b]

            def end(key, ins):
                ins.then_inc(full[of[key][0]], 1)

            def weight(kind, c):
                n = block_at[(kind, c)]
                pe.wait_ge(ring_in[n % RING], 16 * (n // RING + 1))
                return ring[:, n % RING, :].rearrange("p (k n) -> p k n", k=KD if kind in ("in", "out") else 4)

            def product(dst, pairs):
                for n, (lhsT, rhs) in enumerate(pairs):
                    ins = pe.matmul(dst, lhsT, rhs, start=(n == 0), stop=(n == len(pairs) - 1))
                return ins

            def turn_rows(kind, tt, rows):
                for half in range(2):
                    b = begin((kind, tt, half))
                    for k in range(4):
                        ins = pe.transpose(b[:, k * P:(k + 1) * P], rows[:, 4 * half + k::KD], ident)
                    end((kind, tt, half), ins)

            pe.wait_ge(cst_in, 16)
            for tt in range(TT):
                pe.wait_ge(xs_done, tt + 1)
                turn_rows("xT", tt, xs[:, tt % 2, :])
            for tt in range(TT):
                for half in range(2):
                    read_out(pe, ("xT", tt, half))
            for c in range(4):
                w = weight("in", c // 2)
                b = begin(("u", c))
                cols = slice((c % 2) * P, (c % 2 + 1) * P)
                ins = product(b[:, :], [(w[:, k, cols], hT[:, k, :]) for k in range(KD)])
                end(("u", c), ins)
            pe.wait_ge(blk_done, 1)
            for ri in range(2):
                b = begin(("bT", ri))
                src = blk_b[ri].rearrange("p t g h -> p (t g h)")
                for q in range(4):
                    ins = pe.transpose(b[:, q * P:(q + 1) * P], src[:, q * P:(q + 1) * P], ident)
                end(("bT", ri), ins)
            for ri in range(2):
                b = begin(("cT", ri))
                src = blk_c[ri].rearrange("p q g s -> p (q g s)")
                for q in range(4):
                    ins = pe.transpose(b[:, q * P:(q + 1) * P], src[:, q * P:(q + 1) * P], ident)
                end(("cT", ri), ins)
            for ri in range(2):
                read_out(pe, ("bT", ri))
                read_out(pe, ("cT", ri))
            for c in range(4):
                read_out(pe, ("u", c))

            def inputs_of(t):
                rows = slice(32 * (t % 4), 32 * (t % 4) + 32)
                for ri in range(2):
                    key = ("bu", t, ri)
                    b = begin(key)
                    end(key, pe.matmul(b[:, :], bw[rows, t // 4, ri, :], uT[rows, t // 4, :], start=True, stop=True))

            def outputs_of(t):
                j = 32 * (t % 4)
                key = ("y", t // 4)
                b = begin(key) if t % 4 == 0 else pb[4]
                pe.wait_ge(st_done, 2 * t + 1)
                pe.matmul(b[j:j + 32, :], cw[:, t // 4, 0, j:j + 32], st_re, start=True, stop=False)
                pe.wait_ge(st_done, 2 * t + 2)
                ins = pe.matmul(b[j:j + 32, :], cw[:, t // 4, 1, j:j + 32], st_im, start=False, stop=True)
                if t % 4 == 3:
                    end(key, ins)
                else:
                    ins.then_inc(st_used, 1)

            def dense(key):
                b = begin(key)
                if key[0] == "qkv":
                    blk, tt = divmod(key[1], TT)
                    w = weight("in", 2 + blk)
                    ins = product(b[:, 0:COLS], [(hT[:, k, tt * P:(tt + 1) * P], w[:, k, :]) for k in range(KD)])
                else:
                    w = weight("in", 5 + key[1] // 2)
                    cols = slice((key[1] % 2) * P, (key[1] % 2 + 1) * P)
                    ins = product(b[:, :], [(w[:, k, cols], hT[:, k, :]) for k in range(KD)])
                end(key, ins)

            for t in range(2):
                inputs_of(t)
            for t in range(ST):
                for key in slot_work(t):
                    dense(key)
                if t:
                    outputs_of(t - 1)
                if t + 2 < ST:
                    inputs_of(t + 2)
            outputs_of(ST - 1)

            for tt in range(TT):
                pe.wait_ge(qk_done, tt + 1)
                b = begin(("qT", tt))
                for h in range(PAIRS):
                    ins = pe.transpose(b[:, h * P:(h + 1) * P], qkv[:, tt, h * P:(h + 1) * P], ident)
                end(("qT", tt), ins)
                b = begin(("kT", tt))
                for v in range(NKV):
                    ins = pe.transpose(b[:, v * P:(v + 1) * P], kdup[:, tt, v].rearrange("p r d -> p (r d)"), ident)
                end(("kT", tt), ins)
            pe.wait_ge(kt_zero, 1)
            for tt in range(TT):
                read_out(pe, ("qT", tt))
                read_out(pe, ("kT", tt))

            def scores(c):
                lo = CHUNK if c == 0 else 0
                b = begin(("score", c))
                for h in range(NH):
                    r = slice((h % 2) * HD, (h % 2 + 1) * HD)
                    ins = pe.matmul(b[r, (h // 2) * P + lo:(h // 2 + 1) * P], qT[r, h // 2, c * CHUNK:(c + 1) * CHUNK],
                                    kT[r, h // (NH // NKV), c * CHUNK + lo:c * CHUNK + P], start=True, stop=True)
                end(("score", c), ins)

            def turn_probs(c):
                lo = CHUNK if c == 0 else 0
                pe.wait_ge(p_done, c + 1)
                b = begin(("pT", c))
                for h in range(PAIRS):
                    ins = pe.transpose(b[0:P - lo, h * P:(h + 1) * P], prob[c % 2][:, h, lo:P], ident)
                end(("pT", c), ins)

            def attend(c):
                k = CHUNK if c == 0 else P
                read_out(pe, ("pT", c))
                b = begin(("pv", c))
                if c == 2:
                    pe.wait_ge(v_moved, 32)
                for v in range(NKV):
                    if c % 2 or c == 0:
                        val = qkv[0:k, c // 2, 640 + v * HD:640 + (v + 1) * HD]
                    else:
                        val = v_mid[:, c // 2 - 1, v * HD:(v + 1) * HD]
                    for r in range(2):
                        ins = pe.matmul(b[r * HD:(r + 1) * HD, v * 2 * CHUNK:(v + 1) * 2 * CHUNK], val,
                                        prT[c % 2][0:k, 2 * v:2 * v + 2, r * CHUNK:(r + 1) * CHUNK],
                                        start=True, stop=True)
                end(("pv", c), ins)

            scores(0)
            for c in range(NC):
                if c + 1 < NC:
                    scores(c + 1)
                if c % 2 == 0:
                    dense(("gate", 12 + c // 2))
                turn_probs(c)
                if c:
                    attend(c - 1)
            attend(NC - 1)

            w = weight("glu", 0)
            pe.wait_ge(y_act, 4)
            for j in range(4):
                b = begin(("glu", j))
                end(("glu", j), product(b[:, :], [(w[:, k, j * P:(j + 1) * P], yT[:, k, :]) for k in range(4)]))
            pe.wait_ge(y2_done, 4)
            read_out(pe, ("pv", NC - 1))
            for j in range(KD):
                cols = slice((j % 4) * P, (j % 4 + 1) * P)
                for kind, src in (("ssm", y2), ("att", qT)):
                    w = weight(kind, j // 4)
                    b = begin((kind, j))
                    end((kind, j), product(b[:, :], [(w[:, k, cols], src[:, k, :]) for k in range(4)]))

            def project(tt):
                for half in range(2):
                    for c in range(2):
                        weight("out", 2 * half + c)
                    s = block_at[("out", 2 * half)] % RING
                    w = ring[:, s:s + 2, :].rearrange("p c (k n) -> p c k n", k=KD)
                    b = begin(("o", tt, half))
                    end(("o", tt, half), product(b[:, :], [(hTm[:, k, tt * P:(tt + 1) * P], w[:, :, k, :])
                                                           for k in range(KD)]))

            def turn_stream(tt):
                for half in range(2):
                    read_out(pe, ("o", tt, half))
                turn_rows("hT", tt, xr[:, tt, :])

            def route(tt):
                for half in range(2):
                    read_out(pe, ("hT", tt, half))
                b = begin(("logit", tt))
                end(("logit", tt), product(b[:, 0:NR], [(hT[:, k, tt * P:(tt + 1) * P], wr[:, k, :]) for k in range(KD)]))

            hTm = mg
            pe.wait_ge(mg_done, KD)
            pe.wait_ge(late_in, 16 * len(late))
            project(0)
            project(1)
            for tt in range(TT):
                turn_stream(tt)
                if tt + 2 < TT:
                    project(tt + 2)
                route(tt)
            pe.wait_ge(both_done, 1)
            b = begin(("rank",))
            for t in range(TT):
                ins = product(b[:, t * NE:(t + 1) * NE], [(ones, both[:, s, :]) for s in range(t)] + [(tri, both[:, t, :])])
            end(("rank",), ins)
            b = begin(("count",))
            end(("count",), product(b[0:1, 0:NE], [(ones[:, 0:1], both[:, s, :]) for s in range(TT)]))

            def lists(q):
                pe.wait_ge(spot_done, q + 1)
                wait(pe, list_set, q)
                product(pb[LIST][:, 0:3 * NE], [(spot[c][:, t, :], note[c][:, t].rearrange("p f e -> p (f e)"))
                                                for c in range(2) for t in range(TT)]).then_inc(list_full, 1)

            lists(0)
            for n in range(8):
                if n != LIST + 1:
                    pe.wait_ge(free[n], banks.used[n])
            pe.wait_ge(most_done, 1)

            def turn_tile(n, u):
                i = n * 4 + u
                pe.wait_ge(xe_in[u], (n + 1) * 16)
                wait(pe, xt_out, i)
                for k in range(KD):
                    ins = pe.transpose(tb[k // 4][:, (k % 4) * P:(k % 4 + 1) * P], xe[:, u, k::KD], ident)
                ins.then_inc(xt_full, 1)

            def gate_up(n, u):
                i = n * 4 + u
                pe.wait_ge(xt_out, i + 1)
                wait(pe, hid_done, i - 1)
                w = []
                for s in slots_of(u):
                    pe.wait_ge(gu_in[s], (n * 2 + u // 2 + 1) * 32)
                    w.append(eslot[s][:, 0:2 * BLOCK].rearrange("p (m k f) -> p m k f", m=2, k=KD))
                for k in range(KD):
                    for h in range(2):
                        r = slice(h * ROWS, (h + 1) * ROWS)
                        ins = pe.matmul(gu[u % 2][r, :], xeT[:, u % 2, k, r], w[h][:, :, k, :],
                                        start=(k == 0), stop=(k == KD - 1))
                ins.then_inc(gu_done, 1)

            def turn_hidden(n, u):
                i = n * 4 + u
                pe.wait_ge(hid_done, i + 1)
                wait(pe, ht_out, i)
                for j in range(2):
                    ins = pe.transpose(hb[:, j * P:(j + 1) * P], hid[:, u % 2, j::2], ident)
                ins.then_inc(ht_full, 1)

            def down(n, u):
                i = n * 4 + u
                pe.wait_ge(ht_out, i + 1)
                wait(pe, oe_act, i)
                wait(pe, oe_dve, i)
                w = []
                for s in slots_of(u):
                    pe.wait_ge(dn_in[s], (n * 2 + u // 2 + 1) * 16)
                    w.append(eslot[s][:, 2 * BLOCK:3 * BLOCK].rearrange("p (j d) -> p j d", j=2))
                for half in range(2):
                    for j in range(2):
                        for h in range(2):
                            r = slice(h * ROWS, (h + 1) * ROWS)
                            ins = pe.matmul(ob[half][r, :], hidT[:, u % 2, j, r], w[h][:, j, half * 512:(half + 1) * 512],
                                            start=(j == 0), stop=(j == 1))
                ins.then_inc(dn_done, 1)

            def step(n, u):
                p, v = (n, u - 1) if u else (n - 1, 3)
                turn_hidden(p, v)
                if not (isinstance(n, int) and n * 4 + u + 1 >= TILES):
                    turn_tile(n + (u + 1) // 4, (u + 1) % 4)
                down(p, v)
                gate_up(n, u)

            turn_tile(0, 0)
            turn_tile(0, 1)
            gate_up(0, 0)
            expert_steps(pe, step)
            turn_hidden(TILES // 4 - 1, 3)
            down(TILES // 4 - 1, 3)

            def more(n, u, j):
                turn_tile(n, u)
                gate_up(n, u)
                turn_hidden(n, u)
                down(n, u)

            overflow(pe, more, lists)


_INS = ["x", "g_mix", "w_in", "q_norm", "k_norm", "ssm_lambda_re", "ssm_lambda_im", "ssm_log_step",
        "ssm_b_re", "ssm_b_im", "ssm_c_re", "ssm_c_im", "ssm_d", "ssm_w_glu", "ssm_b_glu", "attn_sinks",
        "w_ssm_proj", "w_attn_proj", "w_out", "g_ffn", "w_group_router", "b_group_router",
        "w_expert_router", "b_expert_router", "w_expert_gate", "w_expert_up", "w_expert_down"]


def kernel(**inputs):
    import concourse.bacc as bacc
    from concourse.bass_utils import run_bass_kernel_spmd

    nc = bacc.Bacc("TRN2", target_bir_lowering=False, num_devices=1)
    arrays, args = {}, []
    for name in _INS:
        a = np.ascontiguousarray(inputs[name])
        if name != "x":
            a = a[0]
        arrays[f"in_{name}"] = a
    arrays["in_constants"] = constants()
    for name, a in arrays.items():
        args.append(nc.dram_tensor(name, a.shape, mybir.dt.from_np(a.dtype), kind="ExternalInput").ap())
    out = nc.dram_tensor("out_x", (1, T, D), F32, kind="ExternalOutput").ap()
    build(nc, *args, out)
    r = run_bass_kernel_spmd(nc, [arrays], core_ids=[0])
    return r.results[0]["out_x"]
```

```python
from contextlib import ExitStack

import numpy as np

import concourse.bass as bass
from concourse import mybir

F32 = mybir.dt.float32
I32 = mybir.dt.int32
ALU = mybir.AluOpType
ACT = mybir.ActivationFunctionType
AX = mybir.AxisListType

P = 128
D = 1024
KD = D // P
T = 512
TT = T // P
CH = 512
NG, SG, NS = 32, 16, 64
ST = NG * NS // P
NH, HD = 8, 64
NKV = 2
PAIRS = NH // 2
QKV = NH * HD + 2 * NKV * HD
CHUNK = 64
NC = T // CHUNK
W_IN = CH + QKV + 2 * D
COLS = 256
BLOCK = KD * COLS
RING = 4
NGRP, EPG = 4, 8
NE = NGRP * EPG
DE = 256
SLOTS = 4
ROWS = P // 2
TILES = NE // 2
NR = NGRP + NE
LIST = 5
EPS = 1e-6
MAGIC = 12582912.0
TWO_PI = 6.283185
NONE = 4096
LN2_HI, LN2_LO = 0.693359375, -2.12194440e-4

C_ID, C_TRI, C_ONE = 0, 128, 256
C_T = 384
C_ROPE = C_T + T
C_GL = C_ROPE + TT * 32
C_I4 = C_GL + 4
C_I8 = C_I4 + NGRP
C_REC = C_I8 + EPG
C_Q = C_REC + TT * 6
C_N = C_Q + 1


def constants():
    c = np.zeros((P, C_N), np.float32)
    c[:, C_ID:C_ID + P] = np.eye(P)
    c[:, C_TRI:C_TRI + P] = np.triu(np.ones((P, P)), 1)
    c[:, C_ONE:C_ONE + P] = 1.0
    c[:, C_T:C_T + T] = np.arange(T)
    inv = np.float32(500000.0) ** (-np.arange(0, 16, 2, dtype=np.float32) / np.float32(16))
    ang = (np.arange(T, dtype=np.float32)[:, None] * inv[None]).astype(np.float64)
    rope = np.concatenate([np.cos(ang), np.cos(ang), -np.sin(ang), np.sin(ang)], 1)
    c[:, C_ROPE:C_GL] = rope.reshape(TT, P, 32).transpose(1, 0, 2).reshape(P, TT * 32)
    odd = (np.arange(P) // SG) % 2
    for n, m in enumerate((1 - odd, odd, odd - 1, -odd)):
        c[:, C_GL + n] = m
    c[:, C_I4:C_I4 + NGRP] = np.arange(NGRP)
    c[:, C_I8:C_I8 + EPG] = np.arange(EPG)
    rec = np.zeros((P, TT, 2, 3), np.float32)
    tok = np.arange(TT)[None, :] * P + np.arange(P)[:, None]
    for choice in range(2):
        rec[:, :, choice, 0] = tok - NONE
        rec[:, :, choice, 1] = tok + T * choice - NONE
    c[:, C_Q] = np.pi / 2
    c[:, C_REC:C_Q] = rec.reshape(P, TT * 6)
    return c


class Order:

    def __init__(self, eng, sem):
        self.eng, self.sem, self.n = eng, sem, 0

    def mark(self, ins):
        self.n += 1
        ins.then_inc(self.sem, 1)
        return self.n

    def wait(self, n=None):
        self.eng.wait_ge(self.sem, self.n if n is None else n)

    def link(self, ins):
        self.mark(ins)
        self.wait()


class Banks:

    def __init__(self):
        self.used = [0] * 8
        self.of = {}
        self.turn = 0

    def take(self, key, bank=None):
        if bank is None:
            bank = 5 + self.turn % 3
            self.turn += 1
        self.of[key] = (bank, self.used[bank])
        self.used[bank] += 1


UNITS = [("qkv", n) for n in range(12)] + [("gate", n, half) for n in range(12) for half in range(2)]
COUNTS = (3, 2, 2, 3, 2, 2, 2, 2, 2, 2, 3, 2, 3, 2, 2, 2)


def slot_work(t):
    return UNITS[sum(COUNTS[:t]):sum(COUNTS[:t + 1])]


def plan_banks():
    b = Banks()
    for tt in range(TT):
        for half in range(2):
            b.take(("xT", tt, half), (2 * tt + half) % 4)
    for c in range(TT):
        b.take(("u", c))
    for ri in range(2):
        b.take(("bT", ri), ri)
        b.take(("cT", ri), 2 + ri)
    for t in range(2):
        for ri in range(2):
            b.take(("bu", t, ri), (t % 2) * 2 + ri)
    for t in range(ST):
        for w in slot_work(t):
            if w[2:] != (1,):
                b.take(w[:2])
        if t + 2 < ST:
            for ri in range(2):
                b.take(("bu", t + 2, ri), (t % 2) * 2 + ri)
        if t % 4 == 0:
            b.take(("y", t // 4), 4)
    for tt in range(2):
        b.take(("qT", tt))
        b.take(("kT", tt))
    for c in range(NC):
        if c in (2, 4):
            b.take(("qT", 1 + c // 2))
            b.take(("kT", 1 + c // 2))
        b.take(("score", c), c % 2)
        if c % 2 == 0:
            b.take(("gate", 12 + c // 2))
        b.take(("pT", c), 2 + c % 2)
        b.take(("pv", c), 4)
    for j in range(4):
        b.take(("glu", j))
    for j in range(KD):
        b.take(("att", j))
        b.take(("ssm", j))
    for tt in range(TT):
        for half in range(2):
            b.take(("o", tt, half))
    for tt in range(TT):
        for half in range(2):
            b.take(("hT", tt, half), (2 * tt + half) % 4)
        b.take(("logit", tt), 4)
    b.take(("rank",), LIST)
    b.take(("count",), LIST + 1)
    return b


def weight_blocks():
    blocks = [("in", c) for c in range(W_IN // COLS)]
    blocks += [("glu", 0), ("att", 0), ("ssm", 0), ("att", 1), ("ssm", 1)]
    return blocks + [("out", c) for c in range(D // COLS)]


def last_use(kind, c):
    if kind == "in":
        return ("u", 2 * c + 1) if c < 2 else ("qkv", 4 * c - 5) if c < 5 else ("gate", 2 * c - 9)
    return ("o", TT - 1, 1) if kind == "out" else ("glu", 3) if kind == "glu" else (kind, 4 * c + 3)


def build(nc, x, g_mix, w_in, q_norm, k_norm, lam_re, lam_im, log_step, b_re, b_im, c_re, c_im,
          ssm_d, w_glu, b_glu, sinks, w_ssm, w_att, w_out, g_ffn, w_rg, b_rg, w_re, b_er,
          w_eg, w_eu, w_ed, consts, out):
    banks = plan_banks()
    of = banks.of
    blocks = weight_blocks()
    block_at = {b: n for n, b in enumerate(blocks)}

    with ExitStack() as ctx:
        def sb(name, shape, dt=F32):
            return ctx.enter_context(nc.sbuf_tensor(name, [P, *shape], dt))

        def sem(name):
            return ctx.enter_context(nc.semaphore(name))

        pb = [ctx.enter_context(nc.psum_tensor(f"bank{i}", [P, 512], F32)) for i in range(8)]

        cst = sb("cst", [C_N])
        xr = sb("xr", [TT, D])
        hT = sb("hT", [KD, T])
        xs = sb("xs", [2, D])
        cw = xs[:, 0, :].rearrange("p (q r m) -> p q r m", q=4, r=2)
        ring = sb("ring", [RING, BLOCK])
        gates = sb("gates", [2 * KD, T])
        slot0 = sb("slot0", [3 * BLOCK])
        slot1 = sb("slot1", [3 * BLOCK])
        slot2 = sb("slot2", [3 * BLOCK])
        free4 = sb("free4", [2, 4 * T])
        odd = free4[:, 0, :].rearrange("p (n t) -> p n t", t=T)
        qT = free4[:, 1, :].rearrange("p (h t) -> p h t", t=T)
        kT = sb("kT", [NKV, CHUNK + T])
        v_mid = sb("v_mid", [NC // 2 - 1, NKV * HD])
        early = sb("early", [26, ST])
        par = early[:, 0:16, :]
        nrm = early[:, 16:26, :].rearrange("p a b -> p (a b)").rearrange("p (n t h) -> p n t h", n=4, t=TT)
        g1 = sb("g1", [KD])
        g2 = sb("g2", [KD])
        dsk = sb("dsk", [4])
        bgl = sb("bgl", [4])
        qkn = sb("qkn", [2, HD])
        snk = sb("snk", [PAIRS])
        wr = sb("wr", [KD, NR])
        brt = sb("brt", [NR])
        small = sb("small", [64])
        soft = sb("soft", [2, 8, PAIRS])
        bgh = sb("bgh", [4])
        rc = sb("rc", [SLOTS, 3], I32)
        to = sb("to", [SLOTS], I32)
        most = sb("most", [1], I32)

        ident = cst[:, C_ID:C_ID + P]
        tri = cst[:, C_TRI:C_TRI + P]
        ones = cst[:, C_ONE:C_ONE + P]
        tpos = cst[:, C_T:C_T + T]

        s5 = slot0[:, :].rearrange("p (n t) -> p n t", t=T)
        turn, rot = s5[:, 0], s5[:, 1]
        sin_t = [s5[:, 2], s5[:, 3]]
        cos_t = [s5[:, 4], s5[:, 5]]
        prs = [[s5[:, 6 + n] for n in range(4)], [odd[:, n] for n in range(4)]]
        st_re, st_im = s5[:, 10], s5[:, 11]
        raw_b = [slot0[:, 256 * n:256 * n + 256].rearrange("p (t h) -> p t h", h=SG) for n in range(2)]
        raw_c = [slot0[:, 512 + 256 * n:768 + 256 * n].rearrange("p (q s) -> p q s", s=NS) for n in range(2)]
        blk_b = [slot0[:, 1024 + 512 * n:1536 + 512 * n].rearrange("p (t g h) -> p t g h", g=2, h=SG)
                 for n in range(2)]
        blk_c = [slot0[:, 2048 + 512 * n:2560 + 512 * n].rearrange("p (q g s) -> p q g s", g=2, s=NS)
                 for n in range(2)]
        tmp_b = [slot0[:, 3072 + 256 * n:3328 + 256 * n].rearrange("p (t h) -> p t h", h=SG) for n in range(4)]
        qkv = slot1[:, 0:TT * QKV].rearrange("p (t c) -> p t c", c=QKV)
        kdup = slot1[:, 3072:4096].rearrange("p (t v r d) -> p t v r d", v=NKV, r=2, d=HD)
        prob = [slot0[:, 1024 + 512 * n:1536 + 512 * n].rearrange("p (h k) -> p h k", k=P) for n in range(2)]
        prT = [slot0[:, 2048 + 512 * n:2560 + 512 * n].rearrange("p (h k) -> p h k", k=P) for n in range(2)]
        sqk = slot1[:, 4096:4096 + 640]
        ropet = [slot1[:, 4736:4864], slot1[:, 4864:4928]]
        ropes = [slot1[:, 4928:5056], slot1[:, 5056:5120]]
        bw = slot1[:, 5120:6144].rearrange("p (q r s) -> p q r s", r=2, s=P)
        uT = slot2[:, 0:2048].rearrange("p (c t) -> p c t", t=T)
        uT2 = slot2[:, 4096:6144].rearrange("p (c t) -> p c t", t=T)
        yT = slot2[:, 2048:4096].rearrange("p (c t) -> p c t", t=T)
        y2 = slot2[:, 4096:6144].rearrange("p (c t) -> p c t", t=T)
        mg = gates
        sgl = xs[:, 0, :].rearrange("p (n t) -> p n t", t=T)
        mtmp = xs[:, 1, :].rearrange("p (n t) -> p n t", t=T)
        quarter = cst[:, C_Q:C_Q + 1]
        rt = kT[:, :, :].rearrange("p a b -> p (a b)")
        lg = rt[:, 0:144].rearrange("p (t n) -> p t n", n=NR)
        goh = rt[:, 144:160].rearrange("p (t n) -> p t n", n=NGRP)
        gtm = rt[:, 160:176].rearrange("p (t n) -> p t n", n=NGRP)
        oh = [rt[:, 176 + 32 * n:208 + 32 * n].rearrange("p (t n) -> p t n", n=EPG) for n in range(2)]
        esel = rt[:, 240:272].rearrange("p (t n) -> p t n", n=EPG)
        etm = rt[:, 272:304].rearrange("p (t n) -> p t n", n=EPG)
        st4 = [rt[:, 304 + 4 * n:308 + 4 * n] for n in range(10)]
        gsel = rt[:, 352:480].rearrange("p (t g e) -> p t g e", g=NGRP, e=EPG)
        ohe = [rt[:, 480 + 128 * n:608 + 128 * n].rearrange("p (t n) -> p t n", n=NE) for n in range(2)]
        both = rt[:, 736:864].rearrange("p (t n) -> p t n", n=NE)
        place = rt[:, 864:992].rearrange("p (t n) -> p t n", n=NE)
        rec = rt[:, 992:1016].rearrange("p (t c f) -> p t c f", c=2, f=3)
        gf = gates[:, :, :].rearrange("p a b -> p (a b)")
        xeT = gf[:, 0:2048].rearrange("p (n k c) -> p n k c", n=2, c=P)
        oe = gf[:, 4096:6144].rearrange("p (n d) -> p n d", d=D)
        junk = oe[:, 0, :]
        spot = [gf[:, 6144 + 256 * c:6400 + 256 * c].rearrange("p (t r) -> p t r", r=ROWS) for c in range(2)]
        note = [gf[:, 6656 + 384 * c:7040 + 384 * c].rearrange("p (t f e) -> p t f e", f=3, e=NE) for c in range(2)]
        hid, sg = gf[:, 7424:7680], gf[:, 7680:7936]
        hidT = gf[:, 7936:8192].rearrange("p (j c) -> p j c", c=P)
        lst = early[:, 0:24, :].rearrange("p a b -> p (a b)").bitcast(I32).rearrange("p (i f) -> p i f", f=3)
        xe = xs
        whole = [slot0[:, :], slot1[:, :], slot2[:, :], ring[:, 0:3, :].rearrange("p a b -> p (a b)")]
        gu_w = [w[:, 0:2 * BLOCK] for w in whole] + [t[:, :, :].rearrange("p a b -> p (a b)") for t in (free4, hT)]
        dn_w = [w[:, 2 * BLOCK:] for w in whole] + [ring[:, 3, :], gf[:, 2048:4096]]

        pieces = [(tt, slice(half * 512, (half + 1) * 512)) for tt in range(TT) for half in range(2)]
        y = [(slot0, slot1)[n // 6][:, n % 6 * 1024:(n % 6 + 1) * 1024].rearrange("p (c d) -> p c d", c=2)
             for n in range(len(pieces))]

        hrow = nc.dram_tensor("normed_rows", (T, D), F32, kind="Internal").ap()
        yrow = nc.dram_tensor("expert_rows", (2 * T, D), F32, kind="Internal").ap()

        full = [sem(f"bank{i}_full") for i in range(8)]
        free = [sem(f"bank{i}_free") for i in range(8)]
        x_in = [sem(f"x_in{t}") for t in range(TT)]
        cst_in, par_in, bc_in = sem("cst_in"), sem("par_in"), sem("bc_in")
        gain_in, late_in = sem("gain_in"), sem("late_in")
        ring_in = [sem(f"ring{s}_loaded") for s in range(RING)]
        act_order, dve_order = sem("act_order"), sem("dve_order")
        ssq_done, rstd_done = sem("ssq_done"), sem("rstd_done")
        xs_done = [sem(f"xs{n}_done") for n in range(2)]
        par_turn, par_trig = sem("par_turn"), sem("par_trig")
        u2_in = sem("u_copied")
        blk_done = sem("blk_done")
        turns, whole, rot_done, cs_done = sem("turns"), sem("whole_turns"), sem("rot_done"), sem("cs_done")
        prod_done, in_done = sem("rotated_products"), sem("rotated_inputs")
        out_prod, st_done, st_used = sem("state_products"), sem("states_done"), sem("states_used")
        sq_done, sum_done, qk_rstd = sem("qk_squares"), sem("qk_sums"), sem("qk_rstd")
        qk_scaled, qk_done = sem("qk_scaled"), sem("qk_normed")
        v_moved = sem("v_moved")
        y_act = sem("y_activated")
        m_done, p_exp, p_done = sem("max_done"), sem("probs_exp"), sem("probs_done")
        gates_done = sem("gates_done")
        y2_done, mg_done = sem("glu_done"), sem("merged_done")
        ssq2_done, rstd2_done, xs2_done = sem("ssq2"), sem("rstd2"), sem("xs2_done")
        row_out = [sem(f"row{n}_stored") for n in range(2)]
        kt_zero = sem("kt_zero")
        dexp_in, dexp_out = sem("router_exp_in"), sem("router_exp_out")
        both_done, spot_done, most_done = sem("both_done"), sem("spots_done"), sem("most_done")
        list_full, list_set = sem("list_full"), sem("list_set")
        gu_in = [sem(f"gate_up{s}_loaded") for s in range(SLOTS + 2)]
        dn_in = [sem(f"down{s}_loaded") for s in range(SLOTS + 2)]
        rc_ready, to_ready, dma_begun = sem("record_ready"), sem("result_row_ready"), sem("indirect_dma_begun")
        xe_in = [sem(f"xe{n}_gathered") for n in range(SLOTS)]
        xt_full, xt_out = sem("xt_full"), sem("xt_out")
        gu_done, silu_done, hid_done = sem("gate_up_done"), sem("silu_done"), sem("hid_done")
        ht_full, ht_out, dn_done = sem("hidT_full"), sem("hidT_out"), sem("down_done")
        oe_act, oe_dve = sem("oe_act"), sem("oe_dve")
        sc_done = [sem(f"rows{n}_scattered") for n in range(SLOTS)]
        moe_done, y_in, out_ready, stored = sem("moe_done"), [sem(f"results{n}_in") for n in range(2 * TT)], \
            sem("out_ready"), sem("stored")

        first = [(par[:, n, :], src.rearrange("(t g) s -> (g s) t", g=2)) for n, src in enumerate((lam_re, lam_im))]
        first += [(par[g * NS:(g + 1) * NS, 2, :],
                   log_step.rearrange("(t g) -> g t", g=2)[g:g + 1, :].broadcast_to([NS, ST])) for g in range(2)]
        bc = [(raw_b[n], src.rearrange("(t g) s h -> (g s) t h", g=2)) for n, src in enumerate((b_re, b_im))]
        bc += [(raw_c[n], src.rearrange("(q g) h s -> (g h) q s", q=4)) for n, src in enumerate((c_re, c_im))]
        late = [(dsk[:, :], ssm_d.rearrange("(q g) h -> (g h) q", q=4)),
                (bgl[:, :], b_glu.rearrange("(q p) -> p q", p=P)),
                (g2[:, :], g_ffn.rearrange("(p k) -> p k", k=KD)),
                (qkn[:, 0, :], q_norm.unsqueeze(0).broadcast_to([P, HD])),
                (qkn[:, 1, :], k_norm.unsqueeze(0).broadcast_to([P, HD])),
                (snk[0:HD, :], sinks.rearrange("(a b) -> b a", b=2)[0:1, :].broadcast_to([HD, PAIRS])),
                (snk[HD:P, :], sinks.rearrange("(a b) -> b a", b=2)[1:2, :].broadcast_to([HD, PAIRS])),
                (wr[:, :, 0:NGRP], w_rg.rearrange("(p k) g -> p k g", k=KD)),
                (brt[:, 0:NGRP], b_rg.unsqueeze(0).broadcast_to([P, NGRP])),
                (brt[:, NGRP:NR], b_er.rearrange("(a g) e -> a (g e)", a=1).broadcast_to([P, NE]))]
        late += [(wr[:, :, NGRP + EPG * g:NGRP + EPG * (g + 1)],
                  w_re[g].rearrange("(p k) e -> p k e", k=KD)) for g in range(NGRP)]
        tb, gu, hb, ob = pb[0:2], pb[2:4], pb[4], pb[6:8]

        block = ctx.enter_context(nc.Block())

        def read_out(eng, key):
            b, n = of[key]
            eng.wait_ge(free[b], n + 1)

        def filled(eng, key):
            b, n = of[key]
            eng.wait_ge(full[b], n + 1)
            return pb[b]

        def states_read(eng, t):
            if t % 4 == 3:
                filled(eng, ("y", t // 4))
            else:
                eng.wait_ge(st_used, t + 1 - (t + 1) // 4)

        def wait(eng, s, value):
            if not isinstance(value, int) or value > 0:
                eng.wait_ge(s, value)

        def scattered(eng, n, u):
            wait(eng, sc_done[(u + 2) % 4], (n if u < 2 else n + 1) * 16)

        def expert_steps(eng, step):
            for j in range(1, 5):
                step(j // 4, j % 4)
            with eng.Fori(0, TILES // 4 - 2) as r:
                for j in range(5, 9):
                    step(r + j // 4, j % 4)
            for j in range(TILES - 3, TILES):
                step(j // 4, j % 4)

        def overflow(eng, step, lists=None):
            eng.wait_ge(most_done, 1)
            count = eng.value_load(most[0:1, 0:1], min_val=0, max_val=T)
            for first, end in ((1, 2), (2, T // ROWS)):
                with eng.If(count > first * ROWS):
                    for q in range(first, end) if lists else ():
                        lists(q)
                    with eng.Fori(first, end) as q:
                        with eng.Fori(0, TILES // 4) as r:
                            for u in range(4):
                                step(q * (TILES // 4) + r, u, r * 4 + u)

        def slots_of(n, u):
            if isinstance(n, int) and n == 0 and u < 3:
                return (2 * u, 2 * u + 1), 1
            m = n * 2 + u // 2
            return ((0, 1), m + 1) if u % 2 else ((2, 3), m)

        @block.sync
        def _(sp):
            for tt in range(TT):
                sp.dma_start(xr[:, tt, :], x[0, tt * P:(tt + 1) * P, :]).then_inc(x_in[tt], 16)
            with nc.allow_non_contiguous_dma("small parameters"):
                for dst, src in first:
                    sp.dma_start(dst, src).then_inc(par_in, 16)
                sp.dma_start(g1[:, :], g_mix.rearrange("(p k) -> p k", k=KD)).then_inc(gain_in, 16)
            w_rows = w_in.rearrange("(p k) n -> p k n", k=KD)
            o_rows = w_out.rearrange("(k p) n -> p k n", p=P)
            eg = w_eg.rearrange("g e (p k) f -> (g e) p (k f)", k=KD)
            eu = w_eu.rearrange("g e (p k) f -> (g e) p (k f)", k=KD)
            ed = w_ed.rearrange("g e (p j) d -> (g e) p (j d)", j=2)

            def gate_and_up(s, e, used):
                wait(sp, gu_done, used)
                sp.dma_start(gu_w[s][:, 0:BLOCK], eg[e]).then_inc(gu_in[s], 16)
                sp.dma_start(gu_w[s][:, BLOCK:], eu[e]).then_inc(gu_in[s], 16)

            def down_weights(s, e, used):
                wait(sp, dn_done, used)
                sp.dma_start(dn_w[s], ed[e]).then_inc(dn_in[s], 16)

            def weights(n, u, j):
                for load in (gate_and_up, down_weights):
                    for h, s in enumerate(slots_of(n, u)[0]):
                        load(s, j * 2 + h, n * 4 + u - 1)

            for n, (kind, c) in enumerate(blocks):
                if n in (2, RING):
                    with nc.allow_non_contiguous_dma("small parameters"):
                        for dst, src in bc if n == 2 else late:
                            sp.dma_start(dst, src).then_inc(bc_in if n == 2 else late_in, 16)
                s = n % RING
                if n >= RING:
                    filled(sp, last_use(*blocks[n - RING]))
                if kind == "in":
                    src = w_rows[:, :, c * COLS:(c + 1) * COLS]
                elif kind == "out":
                    src = o_rows[:, :, c * COLS:(c + 1) * COLS]
                else:
                    w = {"glu": w_glu, "ssm": w_ssm, "att": w_att}[kind]
                    src = w.rearrange("(k p) n -> p k n", p=P)[:, :, c * 512:(c + 1) * 512]
                dst = ring[:, s, :].rearrange("p (k n) -> p k n", k=src.shape[1])
                sp.dma_start(dst, src).then_inc(ring_in[s], 16)
            sp.wait_ge(mg_done, KD)
            for e in (0, 1, 2):
                gate_and_up(e, e, 0)
                down_weights(e, e, 0)
            gate_and_up(4, 4, 0)
            filled(sp, ("o", TT - 1, 1))
            gate_and_up(3, 3, 0)
            down_weights(3, 3, 0)
            down_weights(4, 4, 0)
            filled(sp, ("logit", TT - 1))
            gate_and_up(5, 5, 0)
            down_weights(5, 5, 0)
            for tile in (0, 1):
                for load in (gate_and_up, down_weights):
                    for h in range(2):
                        load(2 * tile + h, 2 * tile + 6 + h, tile + 1)
            for u in (1, 2, 3):
                weights(1, u, 4 + u)
            with sp.Fori(2, TILES // 4) as r:
                for u in range(4):
                    weights(r, u, r * 4 + u)
            overflow(sp, weights)
            sp.wait_ge(moe_done, 1)
            for n, (tt, half) in enumerate(pieces):
                sp.dma_start(y[n], yrow.rearrange("(c t p) d -> t p c d", c=2, p=P)[tt, :, :, half]).then_inc(y_in[n], 16)
            for n, (tt, half) in enumerate(pieces):
                sp.wait_ge(out_ready, n + 1)
                sp.dma_start(out[0, tt * P:(tt + 1) * P, half], xr[:, tt, half]).then_inc(stored, 16)
            sp.wait_ge(stored, 16 * len(pieces))

        @block.gpsimd
        def _(pool):
            pool.memset(kT[:, :, 0:CHUNK], 0.0).then_inc(kt_zero, 1)
            cyc = par[:, 5, :]

            def turns_of(t):
                if t:
                    pool.wait_ge(rot_done, t)
                pool.tensor_scalar(turn, tpos, cyc[:, t:t + 1], MAGIC, ALU.mult, ALU.add).then_inc(turns, 1)

            pool.wait_ge(cst_in, 16)
            pool.wait_ge(blk_done, 1)
            turns_of(0)
            turns_of(1)
            for t in range(ST):
                pr = prs[t % 2]
                pool.wait_ge(prod_done, t + 1)
                pool.tensor_tensor(pr[0], pr[0], pr[1], ALU.add).then_inc(in_done, 1)
                read_out(pool, ("bu", t, 1))
                pool.tensor_tensor(pr[2], pr[2], pr[3], ALU.subtract).then_inc(in_done, 1)
                if t + 2 < ST:
                    turns_of(t + 2)
                pool.wait_ge(out_prod, 2 * t + 1)
                if t:
                    states_read(pool, t - 1)
                pool.tensor_tensor(st_re, pr[0], pr[2], ALU.subtract).then_inc(st_done, 1)
                pool.wait_ge(out_prod, 2 * t + 2)
                pool.tensor_tensor(st_im, pr[1], pr[3], ALU.add).then_inc(st_done, 1)

            pool.wait_ge(list_set, 1)
            for n in range(2):
                pool.wait_ge(row_out[n], 32)

            last_token, last_result = pool.to_reg(T - 1), pool.to_reg(2 * T - 1)

            def gather(n, u):
                i = n * 4 + u
                wait(pool, xe_in[u], n * 16)
                wait(pool, hid_done, i - 3)
                pool.tensor_copy(rc[:, u, :], lst[:, i, :] if isinstance(i, int) else
                                 lst[:, bass.ds(i, 1), :].rearrange("p a f -> p (a f)")).then_inc(rc_ready, 1)
                pool.wait_ge(rc_ready, i + 1)
                wait(pool, xt_full, i - 1)
                pool.sem_inc(dma_begun, 1)
                pool.indirect_dma_start(xe[:, u % 2, :], None, hrow, bass.IndirectOffsetOnAxis(rc[:, u, 0:1], 0),
                                        bounds_check=last_token, oob_is_err=False).then_inc(xe_in[u], 16)

            def scatter(n, u):
                i = n * 4 + u
                wait(pool, sc_done[u], n * 16)
                pool.tensor_copy(to[:, u:u + 1], lst[:, i, 1:2] if isinstance(i, int) else
                                 lst[:, bass.ds(i, 1), 1:2].rearrange("p a f -> p (a f)")).then_inc(to_ready, 1)
                pool.wait_ge(to_ready, i + 1)
                pool.wait_ge(oe_act, i + 1)
                pool.wait_ge(oe_dve, i + 1)
                pool.sem_inc(dma_begun, 1)
                pool.indirect_dma_start(yrow, bass.IndirectOffsetOnAxis(to[:, u:u + 1], 0), oe[:, u % 2, :], None,
                                        bounds_check=last_result, oob_is_err=False).then_inc(sc_done[u], 16)

            def step(n, u):
                if not (isinstance(n, int) and n * 4 + u + 3 >= TILES):
                    gather(n + (u + 3) // 4, (u + 3) % 4)
                scatter(n if u else n - 1, (u - 1) % 4)

            gather(0, 0)
            gather(0, 1)
            gather(0, 2)
            gather(0, 3)
            expert_steps(pool, step)
            scatter(TILES // 4 - 1, 3)
            for u in range(SLOTS):
                pool.wait_ge(sc_done[u], 16 * TILES // 4)

            def more(n, u, j):
                gather(n, u)
                scatter(n, u)
                pool.wait_ge(sc_done[u], (n + 1) * 16)

            def lists(q):
                pool.wait_ge(list_set, q + 1)

            overflow(pool, more, lists)
            pool.sem_inc(moe_done, 1)

        @block.scalar
        def _(act):
            order = Order(act, act_order)

            def evac(key, dst, src, func=ACT.Copy, **kw):
                b, n = of[key]
                act.wait_ge(full[b], n + 1)
                act.activation(dst, src, func, **kw).then_inc(free[b], 1)

            act.dma_start(cst[:, :], consts).then_inc(cst_in, 16)

            for tt in range(TT):
                act.wait_ge(x_in[tt], 16)
                act.activation(hT[:, 2 * tt:2 * tt + 2, :].rearrange("p a b -> p (a b)"), xr[:, tt, :],
                               ACT.Square, accum_out=small[:, tt:tt + 1]).then_inc(ssq_done, 1)
            for tt in range(0, TT, 2):
                act.wait_ge(rstd_done, tt // 2 + 1)
                if tt >= 2:
                    for half in range(2):
                        filled(act, ("xT", tt - 2, half))
                act.activation(xs[:, tt % 2, :], xr[:, tt, :], ACT.Copy,
                               scale=small[:, 8 + tt:9 + tt]).then_inc(xs_done[0], 1)
            act.wait_ge(cst_in, 16)
            act.wait_ge(par_turn, 1)
            act.activation(par[:, 9, :], par[:, 7, :], ACT.Sin, scale=TWO_PI)
            order.link(act.activation(par[:, 7, :], par[:, 7, :], ACT.Abs))
            act.activation(par[:, 10, :], par[:, 7, :], ACT.Sin, scale=-TWO_PI, bias=quarter).then_inc(par_trig, 1)
            for c in range(4):
                evac(("u", c), uT[:, c, :], pb[of[("u", c)][0]][:, :])
            for c in range(4):
                read_out(act, ("u", c))
            act.dma_start(uT2[32:P], uT[0:P - 32]).then_inc(u2_in, 16)
            act.dma_start(uT2[0:32], uT[P - 32:P]).then_inc(u2_in, 16)
            for ri in range(2):
                evac(("bT", ri), bw[:, :, ri, :], pb[of[("bT", ri)][0]][:, :].rearrange("p (q s) -> p q s", s=P))
            for tt in (2, 3):
                for half in range(2):
                    filled(act, ("xT", tt, half))
            for ri in range(2):
                evac(("cT", ri), cw[:, :, ri, :], pb[of[("cT", ri)][0]][:, :].rearrange("p (q s) -> p q s", s=P))

            def whole_turns(t):
                act.wait_ge(turns, t + 1)
                act.activation(turn, turn, ACT.Copy, bias=-MAGIC).then_inc(whole, 1)

            def table(t):
                act.wait_ge(rot_done, t + 1)
                if t >= 2:
                    act.wait_ge(out_prod, 2 * (t - 2) + 2)
                act.activation(sin_t[t % 2], rot, ACT.Sin, scale=TWO_PI)
                order.link(act.activation(rot, rot, ACT.Abs))
                act.activation(cos_t[t % 2], rot, ACT.Sin, scale=-TWO_PI, bias=quarter).then_inc(cs_done, 1)

            def dense(key):
                b = pb[of[key][0]]
                if key[0] == "qkv":
                    blk, tt = divmod(key[1], TT)
                    evac(key, qkv[:, tt, blk * COLS:(blk + 1) * COLS], b[:, 0:COLS])
                else:
                    evac(key, gates[:, key[1], :], b[:, :])

            whole_turns(0)
            table(0)
            whole_turns(1)
            for t in range(ST):
                if t + 1 < ST:
                    table(t + 1)
                if t + 2 < ST:
                    whole_turns(t + 2)
                for w in slot_work(t):
                    if w[2:] != (0,):
                        dense(w[:2])
                if t == 4:
                    for n in range(4):
                        read_out(act, ("qkv", 8 + n))
                    for h in range(2):
                        act.dma_start(v_mid[h * CHUNK:(h + 1) * CHUNK, :, :],
                                      qkv[(1 - h) * CHUNK:(2 - h) * CHUNK, h:h + 3, 640:768]).then_inc(v_moved, 16)
                if 4 <= t < 8:
                    if t > 4:
                        act.wait_ge(sum_done, t - 4)
                    act.activation(sqk, qkv[:, t - 4, 0:640], ACT.Square).then_inc(sq_done, 1)
                if 11 <= t < 15:
                    if t == 11:
                        act.wait_ge(qk_rstd, 1)
                    for h in range(NH + NKV):
                        head = qkv[:, t - 11, h * HD:(h + 1) * HD]
                        ins = act.activation(head, head, ACT.Copy, scale=nrm[:, 2, t - 11, h:h + 1])
                    ins.then_inc(qk_scaled, 1)

            def qk_out(tt):
                evac(("qT", tt), qT[:, :, tt * P:(tt + 1) * P],
                     pb[of[("qT", tt)][0]][:, :].rearrange("p (h t) -> p h t", t=P))
                evac(("kT", tt), kT[:, :, CHUNK + tt * P:CHUNK + (tt + 1) * P],
                     pb[of[("kT", tt)][0]][:, 0:NKV * P].rearrange("p (h t) -> p h t", t=P))

            qk_out(0)
            qk_out(1)

            def exps(c):
                lo = CHUNK if c == 0 else 0
                b, n = of[("score", c)]
                z = soft[:, c % 2]
                act.wait_ge(m_done, c + 1)
                if c >= 2:
                    filled(act, ("pT", c - 2))
                s = pb[b][:, :].rearrange("p (h k) -> p h k", k=P)
                for h in range(PAIRS):
                    ins = act.activation(prob[c % 2][:, h, lo:P], s[:, h, lo:P], ACT.Exp, scale=HD ** -0.5,
                                         bias=z[:, 2, h:h + 1], accum_out=z[:, 3, h:h + 1])
                ins.then_inc(free[b], 1)
                act.activation(z[:, 4, :], z[:, 5, :], ACT.Exp).then_inc(p_exp, 1)

            def gelu():
                for q in range(4):
                    read_out(act, ("y", q))
                    order.link(act.activation(yT[:, q, :], yT[:, q, :], ACT.Gelu_apprx_tanh))
                    act.activation(y2[:, q, :], yT[:, q, :], ACT.Copy, scale=0.5).then_inc(y_act, 1)

            exps(0)
            for c in range(NC):
                lo = CHUNK if c == 0 else 0
                if c in (2, 4):
                    qk_out(1 + c // 2)
                if c + 1 < NC:
                    exps(c + 1)
                if c == 2:
                    gelu()
                if c % 2:
                    dense(("gate", 12 + c // 2))
                if c >= 2:
                    filled(act, ("pv", c - 2))
                evac(("pT", c), prT[c % 2][0:P - lo, :, :],
                     pb[of[("pT", c)][0]][0:P - lo, :].rearrange("p (h k) -> p h k", k=P))
            def gate_tanh(n):
                for m in (4 * n, 4 * n + 2):
                    act.activation(gates[:, m:m + 2, :], gates[:, m:m + 2, :], ACT.Tanh, scale=0.5).then_inc(gates_done, 1)

            for n in range(8, 16):
                read_out(act, ("gate", n))
            gate_tanh(0)
            for j in range(4):
                if j >= 2:
                    act.wait_ge(y2_done, j - 1)
                evac(("glu", j), sgl[:, j % 2, :], pb[of[("glu", j)][0]][:, :], ACT.Tanh, scale=0.5,
                     bias=bgh[:, j:j + 1])
                if j < 3:
                    gate_tanh(j + 1)
            act.wait_ge(mg_done, KD)
            for tt in range(TT):
                read_out(act, ("o", tt, 1))
                act.activation(junk, xr[:, tt, :], ACT.Square, accum_out=small[:, 24 + tt:25 + tt]).then_inc(ssq2_done, 1)
                act.wait_ge(rstd2_done, tt + 1)
                if tt >= 2:
                    act.wait_ge(row_out[tt % 2], 16)
                act.activation(xs[:, tt % 2, :], xr[:, tt, :], ACT.Copy,
                               scale=small[:, 32 + tt:33 + tt]).then_inc(xs2_done, 1)
                act.wait_ge(xs2_done, tt + 1)
                act.dma_start(hrow[tt * P:(tt + 1) * P, :], xs[:, tt % 2, :]).then_inc(row_out[tt % 2], 16)
            act.wait_ge(dexp_in, 1)
            act.activation(gtm, gtm, ACT.Exp)
            act.activation(st4[6], st4[6], ACT.Exp).then_inc(dexp_out, 1)

            def silu(n, u):
                i = n * 4 + u
                act.wait_ge(gu_done, i + 1)
                wait(act, hid_done, i)
                act.activation(sg, gu[u % 2][:, 0:DE], ACT.Silu).then_inc(silu_done, 1)

            def hidT_out(n, u):
                i = n * 4 + u
                act.wait_ge(ht_full, i + 1)
                wait(act, dn_done, i)
                act.activation(hidT, hb[:, 0:DE].rearrange("p (j c) -> p j c", c=P),
                               ACT.Copy).then_inc(ht_out, 1)

            def half_out(n, u):
                i = n * 4 + u
                act.wait_ge(dn_done, i + 1)
                scattered(act, n, u)
                act.activation(oe[:, u % 2, 512:D], ob[1][:, :], ACT.Copy).then_inc(oe_act, 1)

            def step(n, u):
                p, v = (n, u - 1) if u else (n - 1, 3)
                hidT_out(p, v)
                half_out(p, v)
                silu(n, u)

            silu(0, 0)
            expert_steps(act, step)
            hidT_out(TILES // 4 - 1, 3)
            half_out(TILES // 4 - 1, 3)

            def more(n, u, j):
                silu(n, u)
                hidT_out(n, u)
                half_out(n, u)

            overflow(act, more)

        @block.vector
        def _(dve):
            order = Order(dve, dve_order)
            link, mark = order.link, order.mark

            def rsqrt(y, v, t, done=None):
                link(dve.tensor_scalar(y.bitcast(I32), v.bitcast(I32), -0.5, 1597463007.0, ALU.mult, ALU.add))
                for n in range(3):
                    link(dve.tensor_tensor(t, y, y, ALU.mult))
                    link(dve.scalar_tensor_tensor(t, t, -0.5, v, ALU.mult, ALU.mult))
                    ins = dve.scalar_tensor_tensor(y, t, 1.5, y, ALU.add, ALU.mult)
                    if n == 2 and done is not None:
                        ins.then_inc(done, 1)
                    else:
                        link(ins)

            def exp(y, v, n, r, w):
                link(dve.tensor_scalar(v, v, -87.0, 88.0, ALU.max, ALU.min))
                link(dve.tensor_scalar(n, v, 1.4426950408889634, MAGIC, ALU.mult, ALU.add))
                link(dve.tensor_scalar(n, n, -MAGIC, None, ALU.add))
                link(dve.scalar_tensor_tensor(r, n, -LN2_HI, v, ALU.mult, ALU.add))
                link(dve.scalar_tensor_tensor(r, n, -LN2_LO, r, ALU.mult, ALU.add))
                link(dve.tensor_scalar(y, r, 1 / 5040, None, ALU.mult))
                for k in (720, 120, 24, 6, 2, 1):
                    link(dve.scalar_tensor_tensor(y, y, 1 / k, r, ALU.add, ALU.mult))
                link(dve.tensor_scalar(w.bitcast(I32), n, 127.0, 8388608.0, ALU.add, ALU.mult))
                link(dve.scalar_tensor_tensor(y, y, 1.0, w, ALU.add, ALU.mult))

            for n in (0, 2):
                dve.wait_ge(ssq_done, n + 2)
                link(dve.tensor_scalar(small[:, 16 + n:18 + n], small[:, n:n + 2], 1.0 / D, EPS, ALU.mult, ALU.add))
                rsqrt(small[:, 8 + n:10 + n], small[:, 16 + n:18 + n], small[:, 20 + n:22 + n], rstd_done)
                dve.wait_ge(rstd_done, n // 2 + 1)
                tt = n + 1
                if tt >= 2:
                    for half in range(2):
                        filled(dve, ("xT", tt - 2, half))
                dve.tensor_scalar(xs[:, tt % 2, :], xr[:, tt, :], small[:, 8 + tt:9 + tt], None, ALU.mult
                                  ).then_inc(xs_done[1], 1)

            def rows_out(kind, tt, half, g):
                src = filled(dve, (kind, tt, half))[:, :].rearrange("p (k t) -> p k t", t=P)
                ks = slice(4 * half, 4 * half + 4)
                dve.tensor_tensor(hT[:, ks, tt * P:(tt + 1) * P], src,
                                  g[:, ks].unsqueeze(2).broadcast_to([P, 4, P]), ALU.mult
                                  ).then_inc(free[of[(kind, tt, half)][0]], 1)

            dve.wait_ge(gain_in, 16)
            for tt in range(TT):
                for half in range(2):
                    rows_out("xT", tt, half, g1)

            lr, li, step_, mag, cyc, t1, t2, t3, cs, sn = (par[:, n, :] for n in (0, 1, 3, 4, 5, 6, 7, 8, 10, 9))
            ar, ai, den, fr, fi = (par[:, n, :] for n in range(11, 16))
            dve.wait_ge(par_in, 64)
            exp(step_, par[:, 2, :], t1, t2, t3)
            link(dve.tensor_tensor(sn, lr, step_, ALU.mult))
            exp(mag, sn, t1, t2, t3)
            link(dve.tensor_tensor(cyc, li, step_, ALU.mult))
            link(dve.tensor_scalar(cyc, cyc, 0.15915494309189535, None, ALU.mult))
            link(dve.tensor_scalar(t1, cyc, MAGIC, None, ALU.add))
            link(dve.tensor_scalar(t1, t1, -MAGIC, None, ALU.add))
            dve.tensor_tensor(t2, cyc, t1, ALU.subtract).then_inc(par_turn, 1)

            dve.wait_ge(par_trig, 1)
            mark(dve.tensor_tensor(ar, mag, cs, ALU.mult))
            link(dve.tensor_tensor(ai, mag, sn, ALU.mult))
            mark(dve.tensor_tensor(t1, lr, lr, ALU.mult))
            mark(dve.tensor_tensor(t2, li, li, ALU.mult))
            link(dve.tensor_scalar(ar, ar, -1.0, None, ALU.add))
            link(dve.tensor_tensor(den, t1, t2, ALU.add))
            mark(dve.reciprocal(den, den))
            mark(dve.tensor_tensor(t1, ar, lr, ALU.mult))
            mark(dve.tensor_tensor(t2, ai, li, ALU.mult))
            mark(dve.tensor_tensor(t3, ai, lr, ALU.mult))
            link(dve.tensor_tensor(sn, ar, li, ALU.mult))
            mark(dve.tensor_tensor(fr, t1, t2, ALU.add))
            link(dve.tensor_tensor(fi, t3, sn, ALU.subtract))
            mark(dve.tensor_tensor(fr, fr, den, ALU.mult))
            mark(dve.tensor_tensor(fi, fi, den, ALU.mult))
            dve.memset(blk_b[0], 0.0)
            link(dve.memset(blk_b[1], 0.0))
            dve.wait_ge(bc_in, 64)
            fr3, fi3 = (f.unsqueeze(2).broadcast_to([P, ST, SG]) for f in (fr, fi))
            mark(dve.tensor_tensor(tmp_b[0], raw_b[0], fr3, ALU.mult))
            mark(dve.tensor_tensor(tmp_b[1], raw_b[1], fi3, ALU.mult))
            mark(dve.tensor_tensor(tmp_b[2], raw_b[1], fr3, ALU.mult))
            link(dve.tensor_tensor(tmp_b[3], raw_b[0], fi3, ALU.mult))
            for g in range(2):
                h = slice(g * NS, (g + 1) * NS)
                dve.tensor_tensor(blk_b[0][h, :, g, :], tmp_b[0][h], tmp_b[1][h], ALU.subtract)
                dst, re, im = (a.rearrange("p (q j) h -> p q j h", j=4) for a in
                               (blk_b[1][h, :, g, :], tmp_b[2][h], tmp_b[3][h]))
                dve.tensor_tensor(dst[:, :, 1:4], re[:, :, 0:3], im[:, :, 0:3], ALU.add)
                dve.tensor_tensor(dst[:, :, 0:1], re[:, :, 3:4], im[:, :, 3:4], ALU.add)
            dve.wait_ge(cst_in, 16)
            for g in range(2):
                for n in range(2):
                    ins = dve.tensor_scalar(blk_c[n][:, :, g, :], raw_c[n],
                                            cst[:, C_GL + 2 * n + g:C_GL + 2 * n + g + 1], None, ALU.mult)
            ins.then_inc(blk_done, 1)

            def rot_of(t):
                dve.wait_ge(whole, t + 1)
                wait(dve, cs_done, t)
                dve.scalar_tensor_tensor(rot, tpos, cyc[:, t:t + 1], turn, ALU.mult, ALU.subtract).then_inc(rot_done, 1)

            def y_of(q):
                src = filled(dve, ("y", q))
                dve.scalar_tensor_tensor(yT[:, q, :], uT[:, q, :], dsk[:, q:q + 1], src[:, :], ALU.mult, ALU.add
                                         ).then_inc(free[4], 1)

            def qk_sums(tt):
                dve.wait_ge(sq_done, tt + 1)
                dve.tensor_reduce(nrm[:, 0, tt, :], sqk.rearrange("p (h d) -> p h d", d=HD), AX.X, ALU.add
                                  ).then_inc(sum_done, 1)

            def qk_rms():
                dve.wait_ge(sum_done, TT)
                link(dve.tensor_scalar(nrm[:, 1], nrm[:, 0], 1.0 / HD, EPS, ALU.mult, ALU.add))
                rsqrt(nrm[:, 2], nrm[:, 1], nrm[:, 3], qk_rstd)

            def qk_norm(tt):
                dve.wait_ge(qk_scaled, tt + 1)
                qk = qkv[:, tt, 0:640].rearrange("p (h d) -> p h d", d=HD)
                q = qk[:, 0:NH, :]
                mark(dve.tensor_tensor(q, q, qkn[:, 0:1, :].broadcast_to([P, NH, HD]), ALU.mult))
                kd = kdup[:, tt]
                for r in range(2):
                    ins = dve.tensor_tensor(kd[:, :, r, :], qk[:, NH:, :], qkn[:, 1:2, :].broadcast_to([P, NKV, HD]),
                                            ALU.mult)
                link(ins)
                cos, sin = (cst[:, C_ROPE + 32 * tt + 16 * n:C_ROPE + 32 * tt + 16 * n + 16] for n in range(2))
                kf = kd.rearrange("p v r d -> p (v r) d")
                for a, h, n in ((q, NH, 0), (kf, 2 * NKV, 1)):
                    ta = ropet[n].rearrange("p (h c) -> p h c", c=16)
                    tb = ropes[n].rearrange("p (h c) -> p h c", c=16)
                    dve.tensor_tensor(ta, a[:, :, 0:16], cos.unsqueeze(1).broadcast_to([P, h, 16]), ALU.mult)
                    dve.tensor_tensor(tb[:, :, 0:8], a[:, :, 8:16], sin[:, 0:8].unsqueeze(1).broadcast_to([P, h, 8]), ALU.mult)
                    link(dve.tensor_tensor(tb[:, :, 8:16], a[:, :, 0:8], sin[:, 8:16].unsqueeze(1).broadcast_to([P, h, 8]), ALU.mult))
                    ins = dve.tensor_tensor(a[:, :, 0:16], ta, tb, ALU.add)
                ins.then_inc(qk_done, 1)

            dve.wait_ge(late_in, 16 * len(late))
            dve.tensor_scalar(bgh[:, :], bgl[:, :], 0.5, None, ALU.mult)
            rot_of(0)
            for t in range(ST):
                si, co = sin_t[t % 2], cos_t[t % 2]
                pr = prs[t % 2]
                br = filled(dve, ("bu", t, 0))
                bi = filled(dve, ("bu", t, 1))
                dve.wait_ge(cs_done, t + 1)
                if t >= 2:
                    dve.wait_ge(st_done, 2 * t - 2)
                dve.tensor_tensor(pr[0], br[:, :], co, ALU.mult)
                dve.tensor_tensor(pr[1], bi[:, :], si, ALU.mult).then_inc(prod_done, 1)
                dve.tensor_tensor(pr[3], br[:, :], si, ALU.mult).then_inc(free[of[("bu", t, 0)][0]], 1)
                dve.tensor_tensor(pr[2], bi[:, :], co, ALU.mult).then_inc(free[of[("bu", t, 1)][0]], 1)
                if t + 1 < ST:
                    rot_of(t + 1)
                if 5 <= t < 9:
                    qk_sums(t - 5)
                decay = mag[:, t:t + 1].broadcast_to([P, T])
                dve.wait_ge(in_done, 2 * t + 1)
                z_re = mark(dve.tensor_tensor_scan(pr[1], decay, pr[0], 0.0, ALU.mult, ALU.add))
                dve.wait_ge(in_done, 2 * t + 2)
                z_im = mark(dve.tensor_tensor_scan(pr[3], decay, pr[2], 0.0, ALU.mult, ALU.add))
                order.wait(z_re)
                dve.tensor_tensor(pr[0], pr[1], co, ALU.mult)
                order.wait(z_im)
                dve.tensor_tensor(pr[2], pr[3], si, ALU.mult).then_inc(out_prod, 1)
                dve.wait_ge(out_prod, 2 * t + 1)
                dve.tensor_tensor(pr[1], pr[1], si, ALU.mult)
                dve.tensor_tensor(pr[3], pr[3], co, ALU.mult).then_inc(out_prod, 1)
                if t == 10:
                    qk_rms()
                if t in (12, 14):
                    qk_norm((t - 12) // 2)
                if t % 4 == 1 and t > 4:
                    y_of((t - 5) // 4)
            y_of(3)

            def maxima(c):
                lo = CHUNK if c == 0 else 0
                z = soft[:, c % 2]
                s = filled(dve, ("score", c))[:, :].rearrange("p (h k) -> p h k", k=P)
                link(dve.tensor_reduce(z[:, 0, :], s[:, :, lo:P], AX.X, ALU.max))
                link(dve.scalar_tensor_tensor(z[:, 1, :], z[:, 0, :], HD ** -0.5, snk[:, :], ALU.mult, ALU.max))
                dve.tensor_scalar(z[:, 2, :], z[:, 1, :], -1.0, None, ALU.mult)
                dve.tensor_tensor(z[:, 5, :], snk[:, :], z[:, 1, :], ALU.subtract).then_inc(m_done, 1)

            def normalise(c):
                lo = CHUNK if c == 0 else 0
                z = soft[:, c % 2]
                dve.wait_ge(p_exp, c + 1)
                link(dve.tensor_tensor(z[:, 6, :], z[:, 3, :], z[:, 4, :], ALU.add))
                link(dve.reciprocal(z[:, 7, :], z[:, 6, :]))
                pc = prob[c % 2][:, :, lo:P]
                dve.tensor_tensor(pc, pc, z[:, 7, :].unsqueeze(2).broadcast_to([P, PAIRS, P - lo]), ALU.mult
                                  ).then_inc(p_done, 1)

            def attended(c):
                src = filled(dve, ("pv", c))
                dve.tensor_copy(qT[:, :, c * CHUNK:(c + 1) * CHUNK],
                                src[:, 0:PAIRS * CHUNK].rearrange("p (h t) -> p h t", t=CHUNK)).then_inc(free[4], 1)

            maxima(0)
            for c in range(NC):
                if c in (0, 2):
                    qk_norm(2 + c // 2)
                if c + 1 < NC:
                    maxima(c + 1)
                normalise(c)
                if c:
                    attended(c - 1)
            attended(NC - 1)

            for j in range(4):
                read_out(dve, ("glu", j))
                dve.scalar_tensor_tensor(y2[:, j, :], sgl[:, j % 2, :], 1.0, y2[:, j, :], ALU.add, ALU.mult
                                         ).then_inc(y2_done, 1)
            dve.wait_ge(gates_done, 8)
            for j in range(KD):
                src = filled(dve, ("att", j))
                dve.scalar_tensor_tensor(mtmp[:, j % 2, :], gates[:, KD + j, :], 1.0, src[:, :], ALU.add, ALU.mult
                                         ).then_inc(free[of[("att", j)][0]], 1)
                src = filled(dve, ("ssm", j))
                dve.scalar_tensor_tensor(mg[:, j, :], gates[:, j, :], 1.0, src[:, :], ALU.add, ALU.mult
                                         ).then_inc(free[of[("ssm", j)][0]], 1)
                read_out(dve, ("att", j))
                read_out(dve, ("ssm", j))
                dve.tensor_tensor(mg[:, j, :], mg[:, j, :], mtmp[:, j % 2, :], ALU.add).then_inc(mg_done, 1)

            def residual(tt):
                for half in range(2):
                    src = filled(dve, ("o", tt, half))
                    xh = xr[:, tt, half * 512:(half + 1) * 512]
                    dve.scalar_tensor_tensor(xh, src[:, :], 0.5, xh, ALU.mult, ALU.add
                                             ).then_inc(free[of[("o", tt, half)][0]], 1)

            def rms(tt):
                dve.wait_ge(ssq2_done, tt + 1)
                v = small[:, 40 + tt:41 + tt]
                link(dve.tensor_scalar(v, small[:, 24 + tt:25 + tt], 1.0 / D, EPS, ALU.mult, ALU.add))
                rsqrt(small[:, 32 + tt:33 + tt], v, small[:, 44 + tt:45 + tt], rstd2_done)

            def logits(tt):
                src = filled(dve, ("logit", tt))
                dve.wait_ge(rstd2_done, tt + 1)
                dve.scalar_tensor_tensor(lg[:, tt, :], src[:, 0:NR], small[:, 32 + tt:33 + tt], brt[:, :],
                                         ALU.mult, ALU.add).then_inc(free[4], 1)

            residual(0)
            residual(1)
            rms(0)
            for tt in range(TT):
                for half in range(2):
                    rows_out("hT", tt, half, g2)
                if tt + 1 < TT:
                    rms(tt + 1)
                if tt + 2 < TT:
                    residual(tt + 2)
                logits(tt)
            read_out(dve, ("logit", TT - 1))

            def over(a, n):
                return a.unsqueeze(2).broadcast_to([P, TT, n])

            def first_best(v, one, tmp, iota, n, best, at):
                link(dve.tensor_reduce(best, v, AX.X, ALU.max))
                link(dve.tensor_tensor(one, v, over(best, n), ALU.is_equal))
                link(dve.scalar_tensor_tensor(tmp, one, -64.0, iota.unsqueeze(1).broadcast_to([P, TT, n]),
                                              ALU.mult, ALU.add))
                link(dve.tensor_reduce(at, tmp, AX.X, ALU.min))
                link(dve.tensor_tensor(one, tmp, over(at, n), ALU.is_equal))

            i4, i8 = cst[:, C_I4:C_I4 + NGRP], cst[:, C_I8:C_I8 + EPG]
            gl, el = lg[:, :, 0:NGRP], lg[:, :, NGRP:NR].rearrange("p t (g e) -> p t g e", e=EPG)
            first_best(gl, goh, gtm, i4, NGRP, st4[0], st4[1])
            link(dve.tensor_tensor(gtm, gl, over(st4[0], NGRP), ALU.subtract))
            link(dve.tensor_tensor(gsel, el, goh.unsqueeze(3).broadcast_to([P, TT, NGRP, EPG]), ALU.mult))
            link(dve.tensor_reduce(esel, gsel.rearrange("p t g e -> p t e g"), AX.X, ALU.add))
            first_best(esel, oh[0], etm, i8, EPG, st4[2], st4[3])
            link(dve.scalar_tensor_tensor(esel, oh[0], -3e38, esel, ALU.mult, ALU.add))
            first_best(esel, oh[1], etm, i8, EPG, st4[4], st4[5])
            dve.tensor_tensor(st4[6], st4[4], st4[2], ALU.subtract).then_inc(dexp_in, 1)
            for c in range(2):
                mark(dve.tensor_tensor(ohe[c].rearrange("p t (g e) -> p t g e", e=EPG),
                                       goh.unsqueeze(3).broadcast_to([P, TT, NGRP, EPG]),
                                       oh[c].unsqueeze(2).broadcast_to([P, TT, NGRP, EPG]), ALU.mult))
            order.wait()
            dve.tensor_tensor(both, ohe[0], ohe[1], ALU.add).then_inc(both_done, 1)
            mark(dve.tensor_copy(rec, cst[:, C_REC:C_Q].rearrange("p (t c f) -> p t c f", c=2, f=3)))
            dve.wait_ge(dexp_out, 1)
            mark(dve.tensor_reduce(st4[7], gtm, AX.X, ALU.add))
            link(dve.tensor_scalar(st4[8], st4[6], 1.0, None, ALU.add))
            link(dve.tensor_tensor(st4[7], st4[7], st4[8], ALU.mult))
            link(dve.reciprocal(st4[7], st4[7]))
            mark(dve.tensor_copy(rec[:, :, 0, 2], st4[7]))
            mark(dve.tensor_tensor(rec[:, :, 1, 2], st4[7], st4[6], ALU.mult))
            order.wait()
            for c in range(2):
                mark(dve.tensor_tensor(note[c], ohe[c].unsqueeze(2).broadcast_to([P, TT, 3, NE]),
                                       rec[:, :, c, :].unsqueeze(3).broadcast_to([P, TT, 3, NE]), ALU.mult))
            src = filled(dve, ("rank",))
            ranks = src[:, 0:TT * NE].rearrange("p (t e) -> p t e", e=NE)
            flat = gsel.rearrange("p t g e -> p t (g e)")
            mark(dve.tensor_tensor(place, ohe[0], ranks, ALU.mult))
            dve.tensor_tensor(flat, ohe[1], ranks, ALU.mult).then_inc(free[of[("rank",)][0]], 1)
            read_out(dve, ("rank",))
            order.wait()
            for c, tmp in enumerate((place, flat)):
                mark(dve.tensor_reduce(st4[8 + c], tmp, AX.X, ALU.add))
            order.wait()

            def spots(q):
                wait(dve, list_full, q)
                for c in range(2):
                    ins = dve.tensor_tensor(spot[c],
                                            tpos[:, q * ROWS:(q + 1) * ROWS].unsqueeze(1).broadcast_to([P, TT, ROWS]),
                                            over(st4[8 + c], ROWS), ALU.is_equal)
                ins.then_inc(spot_done, 1)

            def entries(q):
                dve.wait_ge(list_full, q + 1)
                dst = lst[:, q * TILES:(q + 1) * TILES, :].rearrange("p j f -> p f j")
                src = pb[LIST][:, 0:3 * TILES].rearrange("p (f j) -> p f j", f=3)
                dve.tensor_scalar(dst[:, 0:2, :], src[:, 0:2, :], float(NONE), None, ALU.add)
                dve.tensor_copy(dst[:, 2, :].bitcast(F32), src[:, 2, :]).then_inc(list_set, 1)

            def lists(q):
                spots(q)
                entries(q)

            spots(0)
            src = filled(dve, ("count",))
            link(dve.tensor_reduce(small[0:1, 48:49], src[0:1, 0:NE], AX.X, ALU.max))
            dve.tensor_copy(most[0:1, 0:1], small[0:1, 48:49]).then_inc(most_done, 1)
            entries(0)

            def rows_turned(n, u):
                i = n * 4 + u
                dve.wait_ge(xt_full, i + 1)
                wait(dve, gu_done, i - 1)
                for half in range(2):
                    ks = slice(4 * half, 4 * half + 4)
                    ins = dve.tensor_tensor(xeT[:, u % 2, ks, :], tb[half][:, :].rearrange("p (k c) -> p k c", c=P),
                                            g2[:, ks].unsqueeze(2).broadcast_to([P, 4, P]), ALU.mult)
                ins.then_inc(xt_out, 1)

            def hidden(n, u):
                i = n * 4 + u
                dve.wait_ge(silu_done, i + 1)
                dve.wait_ge(rc_ready, i + 1)
                wait(dve, ht_full, i)
                dve.scalar_tensor_tensor(hid, gu[u % 2][:, DE:2 * DE], rc[:, u, 2:3].bitcast(F32),
                                         sg, ALU.mult, ALU.mult).then_inc(hid_done, 1)

            def half_out(n, u):
                i = n * 4 + u
                dve.wait_ge(dn_done, i + 1)
                scattered(dve, n, u)
                dve.tensor_copy(oe[:, u % 2, 0:512], ob[0][:, :]).then_inc(oe_dve, 1)

            def step(n, u):
                if not (isinstance(n, int) and n * 4 + u + 1 >= TILES):
                    rows_turned(n + (u + 1) // 4, (u + 1) % 4)
                half_out(n if u else n - 1, (u - 1) % 4)
                hidden(n, u)

            rows_turned(0, 0)
            rows_turned(0, 1)
            hidden(0, 0)
            expert_steps(dve, step)
            half_out(TILES // 4 - 1, 3)

            def more(n, u, j):
                rows_turned(n, u)
                hidden(n, u)
                half_out(n, u)

            overflow(dve, more, lists)
            for n, (tt, half) in enumerate(pieces):
                dve.wait_ge(y_in[n], 16)
                link(dve.tensor_tensor(xr[:, tt, half], xr[:, tt, half], y[n][:, 0, :], ALU.add))
                dve.tensor_tensor(xr[:, tt, half], xr[:, tt, half], y[n][:, 1, :], ALU.add).then_inc(out_ready, 1)

        @block.tensor
        def _(pe):
            def begin(key):
                b, n = of[key]
                if n:
                    pe.wait_ge(free[b], n)
                return pb[b]

            def end(key, ins):
                ins.then_inc(full[of[key][0]], 1)

            def weight(kind, c):
                n = block_at[(kind, c)]
                pe.wait_ge(ring_in[n % RING], 16 * (n // RING + 1))
                return ring[:, n % RING, :].rearrange("p (k n) -> p k n", k=KD if kind in ("in", "out") else 4)

            def product(dst, pairs):
                for n, (lhsT, rhs) in enumerate(pairs):
                    ins = pe.matmul(dst, lhsT, rhs, start=(n == 0), stop=(n == len(pairs) - 1))
                return ins

            def turn_rows(kind, tt, rows):
                for half in range(2):
                    b = begin((kind, tt, half))
                    for k in range(4):
                        ins = pe.transpose(b[:, k * P:(k + 1) * P], rows[:, 4 * half + k::KD], ident)
                    end((kind, tt, half), ins)

            pe.wait_ge(cst_in, 16)
            for tt in range(TT):
                pe.wait_ge(xs_done[tt % 2], tt // 2 + 1)
                turn_rows("xT", tt, xs[:, tt % 2, :])
            for tt in range(TT):
                for half in range(2):
                    read_out(pe, ("xT", tt, half))
            for c in range(4):
                w = weight("in", c // 2)
                b = begin(("u", c))
                cols = slice((c % 2) * P, (c % 2 + 1) * P)
                ins = product(b[:, :], [(w[:, k, cols], hT[:, k, :]) for k in range(KD)])
                end(("u", c), ins)
            pe.wait_ge(blk_done, 1)
            for ri in range(2):
                b = begin(("bT", ri))
                src = blk_b[ri].rearrange("p t g h -> p (t g h)")
                for q in range(4):
                    ins = pe.transpose(b[:, q * P:(q + 1) * P], src[:, q * P:(q + 1) * P], ident)
                end(("bT", ri), ins)
            for ri in range(2):
                b = begin(("cT", ri))
                src = blk_c[ri].rearrange("p q g s -> p (q g s)")
                for q in range(4):
                    ins = pe.transpose(b[:, q * P:(q + 1) * P], src[:, q * P:(q + 1) * P], ident)
                end(("cT", ri), ins)

            def inputs_of(t):
                for ri, u in enumerate((uT, uT2)):
                    j = (t + ri) % 4
                    rows = slice(32 * j, 32 * j + 32)
                    key = ("bu", t, ri)
                    b = begin(key)
                    end(key, pe.matmul(b[:, :], bw[rows, t // 4, ri, :], u[rows, t // 4, :], start=True, stop=True))

            def outputs_of(t):
                j = 32 * (t % 4)
                key = ("y", t // 4)
                b = begin(key) if t % 4 == 0 else pb[4]
                pe.wait_ge(st_done, 2 * t + 1)
                pe.matmul(b[j:j + 32, :], cw[:, t // 4, 0, j:j + 32], st_re, start=True, stop=False)
                pe.wait_ge(st_done, 2 * t + 2)
                ins = pe.matmul(b[j:j + 32, :], cw[:, t // 4, 1, j:j + 32], st_im, start=False, stop=True)
                if t % 4 == 3:
                    end(key, ins)
                else:
                    ins.then_inc(st_used, 1)

            def gate_half(key, half):
                b = begin(key) if half == 0 else pb[of[key][0]]
                w = weight("in", 5 + key[1] // 2)
                cols = slice((key[1] % 2) * P, (key[1] % 2 + 1) * P)
                for k in range(4 * half, 4 * half + 4):
                    ins = pe.matmul(b[:, :], w[:, k, cols], hT[:, k, :], start=(k == 0), stop=(k == KD - 1))
                if half:
                    end(key, ins)

            def dense(key):
                if key[0] == "gate":
                    return gate_half(key[:2], key[2])
                b = begin(key)
                blk, tt = divmod(key[1], TT)
                w = weight("in", 2 + blk)
                end(key, product(b[:, 0:COLS], [(hT[:, k, tt * P:(tt + 1) * P], w[:, k, :]) for k in range(KD)]))

            early_units = slot_work(0)[0:2]
            for key in early_units:
                dense(key)
            for ri in range(2):
                read_out(pe, ("bT", ri))
                read_out(pe, ("cT", ri))
            for c in range(4):
                read_out(pe, ("u", c))
            pe.wait_ge(u2_in, 32)
            for t in range(2):
                inputs_of(t)
            for t in range(ST):
                for key in slot_work(t):
                    if key not in early_units:
                        dense(key)
                if t:
                    outputs_of(t - 1)
                if t + 2 < ST:
                    inputs_of(t + 2)

            def turn_qk(tt):
                pe.wait_ge(qk_done, tt + 1)
                b = begin(("qT", tt))
                for h in range(PAIRS):
                    ins = pe.transpose(b[:, h * P:(h + 1) * P], qkv[:, tt, h * P:(h + 1) * P], ident)
                end(("qT", tt), ins)
                b = begin(("kT", tt))
                for v in range(NKV):
                    ins = pe.transpose(b[:, v * P:(v + 1) * P], kdup[:, tt, v].rearrange("p r d -> p (r d)"), ident)
                end(("kT", tt), ins)

            turn_qk(0)
            turn_qk(1)
            outputs_of(ST - 1)
            pe.wait_ge(kt_zero, 1)

            def scores(c):
                lo = CHUNK if c == 0 else 0
                if c % 2 == 0:
                    read_out(pe, ("qT", c // 2))
                    read_out(pe, ("kT", c // 2))
                b = begin(("score", c))
                for h in range(NH):
                    r = slice((h % 2) * HD, (h % 2 + 1) * HD)
                    ins = pe.matmul(b[r, (h // 2) * P + lo:(h // 2 + 1) * P], qT[r, h // 2, c * CHUNK:(c + 1) * CHUNK],
                                    kT[r, h // (NH // NKV), c * CHUNK + lo:c * CHUNK + P], start=True, stop=True)
                end(("score", c), ins)

            def turn_probs(c):
                lo = CHUNK if c == 0 else 0
                pe.wait_ge(p_done, c + 1)
                b = begin(("pT", c))
                for h in range(PAIRS):
                    ins = pe.transpose(b[0:P - lo, h * P:(h + 1) * P], prob[c % 2][:, h, lo:P], ident)
                end(("pT", c), ins)

            def attend(c):
                k = CHUNK if c == 0 else P
                read_out(pe, ("pT", c))
                b = begin(("pv", c))
                if c == 2:
                    pe.wait_ge(v_moved, 32)
                for v in range(NKV):
                    if c % 2 or c == 0:
                        val = qkv[0:k, c // 2, 640 + v * HD:640 + (v + 1) * HD]
                    else:
                        val = v_mid[:, c // 2 - 1, v * HD:(v + 1) * HD]
                    for r in range(2):
                        ins = pe.matmul(b[r * HD:(r + 1) * HD, v * 2 * CHUNK:(v + 1) * 2 * CHUNK], val,
                                        prT[c % 2][0:k, 2 * v:2 * v + 2, r * CHUNK:(r + 1) * CHUNK],
                                        start=True, stop=True)
                end(("pv", c), ins)

            scores(0)
            for c in range(NC):
                if c in (2, 4):
                    turn_qk(1 + c // 2)
                if c + 1 < NC:
                    scores(c + 1)
                gate_half(("gate", 12 + c // 2), c % 2)
                turn_probs(c)
                if c:
                    attend(c - 1)
            attend(NC - 1)

            w = weight("glu", 0)
            pe.wait_ge(y_act, 4)
            for j in range(4):
                b = begin(("glu", j))
                end(("glu", j), product(b[:, :], [(w[:, k, j * P:(j + 1) * P], yT[:, k, :]) for k in range(4)]))
            read_out(pe, ("pv", NC - 1))
            for j in range(KD):
                cols = slice((j % 4) * P, (j % 4 + 1) * P)
                for kind, src in (("att", qT), ("ssm", y2)):
                    if (kind, j) == ("ssm", 0):
                        pe.wait_ge(y2_done, 4)
                    w = weight(kind, j // 4)
                    b = begin((kind, j))
                    end((kind, j), product(b[:, :], [(w[:, k, cols], src[:, k, :]) for k in range(4)]))

            def project(tt):
                for half in range(2):
                    for c in range(2):
                        weight("out", 2 * half + c)
                    s = block_at[("out", 2 * half)] % RING
                    w = ring[:, s:s + 2, :].rearrange("p c (k n) -> p c k n", k=KD)
                    b = begin(("o", tt, half))
                    for k in range(KD):
                        if (tt, half) == (0, 0):
                            pe.wait_ge(mg_done, k + 1)
                        ins = pe.matmul(b[:, :], mg[:, k, tt * P:(tt + 1) * P], w[:, :, k, :],
                                        start=(k == 0), stop=(k == KD - 1))
                    end(("o", tt, half), ins)

            def turn_stream(tt):
                for half in range(2):
                    read_out(pe, ("o", tt, half))
                turn_rows("hT", tt, xr[:, tt, :])

            def route(tt):
                for half in range(2):
                    read_out(pe, ("hT", tt, half))
                b = begin(("logit", tt))
                end(("logit", tt), product(b[:, 0:NR], [(hT[:, k, tt * P:(tt + 1) * P], wr[:, k, :]) for k in range(KD)]))

            pe.wait_ge(late_in, 16 * len(late))
            project(0)
            project(1)
            for tt in range(TT):
                turn_stream(tt)
                if tt + 2 < TT:
                    project(tt + 2)
                route(tt)
            pe.wait_ge(both_done, 1)
            b = begin(("rank",))
            ins = pe.matmul(b[:, 0:TT * NE], tri, both.rearrange("p t e -> p (t e)"), start=True, stop=False)
            for t in range(TT - 1):
                ins = pe.matmul(b[:, (t + 1) * NE:TT * NE].rearrange("p (s e) -> p s e", e=NE), ones,
                                both[:, t:t + 1, :].broadcast_to([P, TT - 1 - t, NE]), start=False, stop=(t == TT - 2))
            end(("rank",), ins)
            b = begin(("count",))
            end(("count",), product(b[0:1, 0:NE], [(ones[:, 0:1], both[:, s, :]) for s in range(TT)]))

            def lists(q):
                pe.wait_ge(spot_done, q + 1)
                wait(pe, list_set, q)
                pairs = [(spot[c][:, t, :], note[c][:, t, :, :]) for c in range(2) for t in range(TT)]
                for n, (lhsT, rhs) in enumerate(pairs):
                    for h in range(2):
                        ins = pe.matmul(pb[LIST][h * ROWS:(h + 1) * ROWS, 0:3 * TILES], lhsT, rhs[:, :, h::2],
                                        start=(n == 0), stop=(n == len(pairs) - 1))
                ins.then_inc(list_full, 1)

            lists(0)
            for n in range(8):
                if n != LIST + 1:
                    pe.wait_ge(free[n], banks.used[n])
            pe.wait_ge(most_done, 1)

            def turn_tile(n, u):
                i = n * 4 + u
                pe.wait_ge(xe_in[u], (n + 1) * 16)
                wait(pe, xt_out, i)
                for k in range(KD):
                    ins = pe.transpose(tb[k // 4][:, (k % 4) * P:(k % 4 + 1) * P], xe[:, u % 2, k::KD], ident)
                ins.then_inc(xt_full, 1)

            def gate_up(n, u):
                i = n * 4 + u
                pe.wait_ge(xt_out, i + 1)
                wait(pe, hid_done, i - 1)
                w = []
                slots, m = slots_of(n, u)
                for s in slots:
                    pe.wait_ge(gu_in[s], m * 32)
                    w.append(gu_w[s].rearrange("p (m k f) -> p m k f", m=2, k=KD))
                for k in range(KD):
                    for h in range(2):
                        r = slice(h * ROWS, (h + 1) * ROWS)
                        ins = pe.matmul(gu[u % 2][r, :], xeT[:, u % 2, k, r], w[h][:, :, k, :],
                                        start=(k == 0), stop=(k == KD - 1))
                ins.then_inc(gu_done, 1)

            def turn_hidden(n, u):
                i = n * 4 + u
                pe.wait_ge(hid_done, i + 1)
                wait(pe, ht_out, i)
                for j in range(2):
                    ins = pe.transpose(hb[:, j * P:(j + 1) * P], hid[:, j::2], ident)
                ins.then_inc(ht_full, 1)

            def down(n, u):
                i = n * 4 + u
                pe.wait_ge(ht_out, i + 1)
                wait(pe, oe_act, i)
                wait(pe, oe_dve, i)
                w = []
                slots, m = slots_of(n, u)
                for s in slots:
                    pe.wait_ge(dn_in[s], m * 16)
                    w.append(dn_w[s].rearrange("p (j d) -> p j d", j=2))
                for half in range(2):
                    for j in range(2):
                        for h in range(2):
                            r = slice(h * ROWS, (h + 1) * ROWS)
                            ins = pe.matmul(ob[half][r, :], hidT[:, j, r], w[h][:, j, half * 512:(half + 1) * 512],
                                            start=(j == 0), stop=(j == 1))
                ins.then_inc(dn_done, 1)

            def step(n, u):
                p, v = (n, u - 1) if u else (n - 1, 3)
                turn_hidden(p, v)
                if not (isinstance(n, int) and n * 4 + u + 1 >= TILES):
                    turn_tile(n + (u + 1) // 4, (u + 1) % 4)
                down(p, v)
                gate_up(n, u)

            turn_tile(0, 0)
            turn_tile(0, 1)
            gate_up(0, 0)
            expert_steps(pe, step)
            turn_hidden(TILES // 4 - 1, 3)
            down(TILES // 4 - 1, 3)

            def more(n, u, j):
                turn_tile(n, u)
                gate_up(n, u)
                turn_hidden(n, u)
                down(n, u)

            overflow(pe, more, lists)


_INS = ["x", "g_mix", "w_in", "q_norm", "k_norm", "ssm_lambda_re", "ssm_lambda_im", "ssm_log_step",
        "ssm_b_re", "ssm_b_im", "ssm_c_re", "ssm_c_im", "ssm_d", "ssm_w_glu", "ssm_b_glu", "attn_sinks",
        "w_ssm_proj", "w_attn_proj", "w_out", "g_ffn", "w_group_router", "b_group_router",
        "w_expert_router", "b_expert_router", "w_expert_gate", "w_expert_up", "w_expert_down"]


def kernel(**inputs):
    import concourse.bacc as bacc
    from concourse.bass_utils import run_bass_kernel_spmd

    nc = bacc.Bacc("TRN2", target_bir_lowering=False, num_devices=1)
    arrays, args = {}, []
    for name in _INS:
        a = np.ascontiguousarray(inputs[name])
        if name != "x":
            a = a[0]
        arrays[f"in_{name}"] = a
    arrays["in_constants"] = constants()
    for name, a in arrays.items():
        args.append(nc.dram_tensor(name, a.shape, mybir.dt.from_np(a.dtype), kind="ExternalInput").ap())
    out = nc.dram_tensor("out_x", (1, T, D), F32, kind="ExternalOutput").ap()
    build(nc, *args, out)
    r = run_bass_kernel_spmd(nc, [arrays], core_ids=[0])
    return r.results[0]["out_x"]
```
